# Optimizing a Trainium2 kernel written in Bass

```python
import jax, jax.numpy as jnp
from jax import lax
import numpy as np

D_MODEL = 1024
BATCH = 1
SEQ = 256
DEPTH = 2

GRID_W = 64
CTX_LEN = 256
EPS = 1e-6
N_Q_HEADS = 8
N_KV_HEADS = 2
HEAD_DIM = 64
Q_PER_KV = N_Q_HEADS // N_KV_HEADS
ATTN_WIDTH = N_Q_HEADS * HEAD_DIM
KV_WIDTH = N_KV_HEADS * HEAD_DIM
Q_BLOCK = 128
ROPE_THETA = 10000.0
POOL_WINDOWS = (2, 4, 8, 16)
POOL_GROUP = 128
POOL_WIDTH = POOL_GROUP * len(POOL_WINDOWS)
SG_GROUPS = 4
SG_GROUP_WIDTH = 128
SG_CHUNK = 128
SG_WIDTH = SG_GROUPS * SG_GROUP_WIDTH
CONV_WIDTH = 512
CONV_K = 3
EVEN_IN = ATTN_WIDTH + 2 * KV_WIDTH + POOL_WIDTH
ODD_IN = 2 * SG_WIDTH + 3 * CONV_WIDTH
MIX_WIDTH = ATTN_WIDTH + POOL_WIDTH
N_GROUPS = 4
EXPERTS_PER_GROUP = 4
N_EXPERTS = N_GROUPS * EXPERTS_PER_GROUP
TOP_K = 2
D_EXPERT = 256


def rms_norm(x, gain):
    x32 = x.astype(jnp.float32)
    y = x32 * lax.rsqrt(jnp.mean(x32 * x32, axis=-1, keepdims=True) + EPS)
    return (y * gain.astype(jnp.float32)).astype(x.dtype)

def modulate(x, gain, shift, scale):
    return rms_norm(x, gain) * (1 + scale) + shift

def adaln(cond, mod_w, mod_b):
    m = jax.nn.silu(cond) @ mod_w + mod_b
    return jnp.split(m, 6, axis=-1)

def axial_angles(n_rows):
    row = jnp.repeat(jnp.arange(n_rows, dtype=jnp.float32), GRID_W)
    col = jnp.tile(jnp.arange(GRID_W, dtype=jnp.float32), n_rows)
    half = HEAD_DIM // 2
    inv = ROPE_THETA ** (-jnp.arange(0, half, 2, dtype=jnp.float32) / half)
    return row[:, None] * inv, col[:, None] * inv

def rope_1d(x, ang):
    cos = jnp.cos(ang)[None, :, None, :]
    sin = jnp.sin(ang)[None, :, None, :]
    x1, x2 = jnp.split(x, 2, axis=-1)
    return jnp.concatenate([x1 * cos - x2 * sin, x2 * cos + x1 * sin], axis=-1)

def rope_2d(x, row_ang, col_ang):
    x32 = x.astype(jnp.float32)
    xr, xc = jnp.split(x32, 2, axis=-1)
    return jnp.concatenate([rope_1d(xr, row_ang), rope_1d(xc, col_ang)], axis=-1).astype(x.dtype)

def gqa_attend(q, k, v):
    s = jnp.einsum('bqkgd,bskd->bkgqs', q, k, preferred_element_type=jnp.float32) * (HEAD_DIM ** -0.5)
    p = jax.nn.softmax(s, axis=-1).astype(v.dtype)
    return jnp.einsum('bkgqs,bskd->bqkgd', p, v)

def multiscale_pool(p, pool_w, pool_scale):
    bsz, length, _ = p.shape
    p32 = p.astype(jnp.float32)
    cs = jnp.concatenate([jnp.zeros_like(p32[:, :1]), jnp.cumsum(p32, axis=1)], axis=1)
    t = jnp.arange(length)
    diffs = []
    for g, w in enumerate(POOL_WINDOWS):
        lo = jnp.clip(t - w // 2, 0, length)
        hi = jnp.clip(t + w - w // 2, 0, length)
        sl = slice(g * POOL_GROUP, (g + 1) * POOL_GROUP)
        csg = cs[..., sl]
        mean = (csg[:, hi] - csg[:, lo]) / (hi - lo).astype(jnp.float32)[None, :, None]
        diffs.append(mean - p32[..., sl])
    d = jnp.stack(diffs, axis=2).astype(p.dtype)
    y = jnp.einsum('blgc,gcd->blgd', d, pool_w).reshape(bsz, length, POOL_WIDTH)
    return y * pool_scale

def even_mixer(h, hc, w_in, q_gain, k_gain, pool_w, pool_scale, w_out, row_ang, col_ang, need_ctx_out):
    bsz, seq, _ = h.shape
    n_ctx = hc.shape[1]
    q, k, v, p = jnp.split(h @ w_in, [ATTN_WIDTH, ATTN_WIDTH + KV_WIDTH, ATTN_WIDTH + 2 * KV_WIDTH], axis=-1)
    q = rope_2d(rms_norm(q.reshape(bsz, seq, N_Q_HEADS, HEAD_DIM), q_gain), row_ang, col_ang)
    k = rope_2d(rms_norm(k.reshape(bsz, seq, N_KV_HEADS, HEAD_DIM), k_gain), row_ang, col_ang)
    v = v.reshape(bsz, seq, N_KV_HEADS, HEAD_DIM)
    if need_ctx_out:
        qc, kc, vc, pc = jnp.split(hc @ w_in, [ATTN_WIDTH, ATTN_WIDTH + KV_WIDTH, ATTN_WIDTH + 2 * KV_WIDTH], axis=-1)
    else:
        kc, vc = jnp.split(hc @ w_in[:, ATTN_WIDTH:ATTN_WIDTH + 2 * KV_WIDTH], [KV_WIDTH], axis=-1)
    kc = rms_norm(kc.reshape(bsz, n_ctx, N_KV_HEADS, HEAD_DIM), k_gain)
    vc = vc.reshape(bsz, n_ctx, N_KV_HEADS, HEAD_DIM)
    k_all = jnp.concatenate([kc, k], axis=1)
    v_all = jnp.concatenate([vc, v], axis=1)
    n_blk = seq // Q_BLOCK
    qb = q.reshape(bsz, n_blk, Q_BLOCK, N_KV_HEADS, Q_PER_KV, HEAD_DIM).transpose(1, 0, 2, 3, 4, 5)
    o = lax.map(lambda qq: gqa_attend(qq, k_all, v_all), qb)
    o = o.transpose(1, 0, 2, 3, 4, 5).reshape(bsz, seq, ATTN_WIDTH)
    y = jnp.concatenate([o, multiscale_pool(p, pool_w, pool_scale)], axis=-1) @ w_out
    if need_ctx_out:
        qc = rms_norm(qc.reshape(bsz, n_ctx, N_Q_HEADS, HEAD_DIM), q_gain).reshape(bsz, n_ctx, N_KV_HEADS, Q_PER_KV, HEAD_DIM)
        oc = gqa_attend(qc, kc, vc).reshape(bsz, n_ctx, ATTN_WIDTH)
        yc = jnp.concatenate([oc, multiscale_pool(pc, pool_w, pool_scale)], axis=-1) @ w_out
    else:
        yc = None
    return y, yc

def odd_mixer(h, w_in, sg_gain, sg_w, sg_b, conv_w, w_out):
    bsz, length, _ = h.shape
    u, v, hx, bg, cg = jnp.split(h @ w_in, [SG_WIDTH, 2 * SG_WIDTH, 2 * SG_WIDTH + CONV_WIDTH, 2 * SG_WIDTH + 2 * CONV_WIDTH], axis=-1)
    v = rms_norm(v.reshape(bsz, length // SG_CHUNK, SG_CHUNK, SG_GROUPS, SG_GROUP_WIDTH), sg_gain)
    s = jnp.einsum('gpq,bnqgc->bnpgc', sg_w, v) + sg_b.T[:, :, None]
    y_c = u * s.reshape(bsz, length, SG_WIDTH)
    z = cg * hx
    zc = lax.conv_general_dilated(z, conv_w, window_strides=(1,), padding=((CONV_K // 2, CONV_K // 2),),
                                  dimension_numbers=('NWC', 'WIO', 'NWC'), feature_group_count=CONV_WIDTH)
    y_d = bg * zc
    return jnp.concatenate([y_c, y_d], axis=-1) @ w_out

def hier_moe(h, rg_w, rg_b, re_w, re_b, w_gate, w_up, w_down):
    shape = h.shape
    t = h.reshape(-1, shape[-1])
    t32 = t.astype(jnp.float32)
    n_tok = t.shape[0]
    g_prob = jax.nn.softmax(t32 @ rg_w.astype(jnp.float32) + rg_b.astype(jnp.float32), axis=-1)
    g_p, g_idx = lax.top_k(g_prob, 1)
    e_logits = (t32 @ re_w.astype(jnp.float32) + re_b.astype(jnp.float32)).reshape(n_tok, N_GROUPS, EXPERTS_PER_GROUP)
    e_sel = jnp.take_along_axis(e_logits, g_idx[:, :, None], axis=1)[:, 0]
    top_p, top_i = lax.top_k(jax.nn.softmax(e_sel, axis=-1), TOP_K)
    top_p = top_p / jnp.sum(top_p, axis=-1, keepdims=True)
    weights = g_p * top_p
    expert_id = g_idx * EXPERTS_PER_GROUP + top_i
    comb = jnp.sum(jax.nn.one_hot(expert_id, N_EXPERTS, dtype=jnp.float32) * weights[..., None], axis=1)

    def step(acc, xs):
        wg, wu, wd, cw = xs
        y = (jax.nn.silu(t @ wg) * (t @ wu)) @ wd
        return acc + y.astype(jnp.float32) * cw[:, None], None

    acc, _ = lax.scan(step, jnp.zeros(t.shape, jnp.float32), (w_gate, w_up, w_down, comb.T))
    return acc.astype(h.dtype).reshape(shape)

def first_inputs(seed: int = 0) -> dict:
    key = jax.random.key(seed)
    ks = jax.random.split(key, 32)
    n_even = (DEPTH + 1) // 2
    n_odd = DEPTH // 2
    f32 = jnp.float32

    def nrm(k, shape, scale):
        return jax.random.normal(k, shape, f32) * scale

    def gain(k, shape, noise=0.05):
        return 1.0 + nrm(k, shape, noise)

    return {
        'x': nrm(ks[0], (BATCH, SEQ, D_MODEL), 1.0),
        'c': nrm(ks[1], (BATCH, D_MODEL), 1.0),
        'ctx': nrm(ks[2], (BATCH, CTX_LEN, D_MODEL), 1.0),
        'c_ctx': nrm(ks[3], (D_MODEL,), 1.0),
        'mod_w': nrm(ks[4], (DEPTH, D_MODEL, 6 * D_MODEL), 0.5 * D_MODEL ** -0.5),
        'mod_b': nrm(ks[5], (DEPTH, 6 * D_MODEL), 0.02),
        'norm1_g': gain(ks[6], (DEPTH, D_MODEL)),
        'norm2_g': gain(ks[7], (DEPTH, D_MODEL)),
        'even_w_in': nrm(ks[8], (n_even, D_MODEL, EVEN_IN), D_MODEL ** -0.5),
        'q_gain': gain(ks[9], (n_even, HEAD_DIM)),
        'k_gain': gain(ks[10], (n_even, HEAD_DIM)),
        'pool_w': nrm(ks[11], (n_even, len(POOL_WINDOWS), POOL_GROUP, POOL_GROUP), POOL_GROUP ** -0.5),
        'pool_scale': gain(ks[12], (n_even, POOL_WIDTH), 0.1),
        'even_w_out': nrm(ks[13], (n_even, MIX_WIDTH, D_MODEL), MIX_WIDTH ** -0.5),
        'odd_w_in': nrm(ks[14], (n_odd, D_MODEL, ODD_IN), D_MODEL ** -0.5),
        'sg_gain': gain(ks[15], (n_odd, SG_GROUPS, SG_GROUP_WIDTH)),
        'sg_w': nrm(ks[16], (n_odd, SG_GROUPS, SG_CHUNK, SG_CHUNK), SG_CHUNK ** -0.5),
        'sg_b': gain(ks[17], (n_odd, SG_GROUPS, SG_CHUNK), 0.1),
        'conv_w': nrm(ks[18], (n_odd, CONV_K, 1, CONV_WIDTH), CONV_K ** -0.5),
        'odd_w_out': nrm(ks[19], (n_odd, MIX_WIDTH, D_MODEL), MIX_WIDTH ** -0.5),
        'router_g_w': nrm(ks[20], (DEPTH, D_MODEL, N_GROUPS), D_MODEL ** -0.5),
        'router_g_b': nrm(ks[21], (DEPTH, N_GROUPS), 0.01),
        'router_e_w': nrm(ks[22], (DEPTH, D_MODEL, N_EXPERTS), D_MODEL ** -0.5),
        'router_e_b': nrm(ks[23], (DEPTH, N_EXPERTS), 0.01),
        'w_gate': nrm(ks[24], (DEPTH, N_EXPERTS, D_MODEL, D_EXPERT), D_MODEL ** -0.5),
        'w_up': nrm(ks[25], (DEPTH, N_EXPERTS, D_MODEL, D_EXPERT), D_MODEL ** -0.5),
        'w_down': nrm(ks[26], (DEPTH, N_EXPERTS, D_EXPERT, D_MODEL), D_EXPERT ** -0.5),
    }

def first_block(x, c, ctx, c_ctx, mod_w, mod_b, norm1_g, norm2_g, even_w_in, q_gain, k_gain, pool_w, pool_scale,
              even_w_out, odd_w_in, sg_gain, sg_w, sg_b, conv_w, odd_w_out, router_g_w, router_g_b,
              router_e_w, router_e_b, w_gate, w_up, w_down):
    seq = x.shape[1]
    ROWS = seq // GRID_W
    row_ang, col_ang = axial_angles(ROWS)
    last_even = 2 * ((DEPTH - 1) // 2)
    h_lat, h_ctx = x, ctx
    for i in range(DEPTH):
        j = i // 2
        need_ctx_in = i <= last_even
        need_ctx_out = i < last_even
        sh1, sc1, g1, sh2, sc2, g2 = [m[:, None, :] for m in adaln(c, mod_w[i], mod_b[i])]
        a = modulate(h_lat, norm1_g[i], sh1, sc1)
        if need_ctx_in:
            csh1, csc1, cg1, csh2, csc2, cg2 = adaln(c_ctx, mod_w[i], mod_b[i])
            ac = modulate(h_ctx, norm1_g[i], csh1, csc1)
        if i % 2 == 0:
            y, yc = even_mixer(a, ac, even_w_in[j], q_gain[j], k_gain[j], pool_w[j], pool_scale[j],
                               even_w_out[j], row_ang, col_ang, need_ctx_out)
        else:
            y = odd_mixer(a, odd_w_in[j], sg_gain[j], sg_w[j], sg_b[j], conv_w[j], odd_w_out[j])
            yc = odd_mixer(ac, odd_w_in[j], sg_gain[j], sg_w[j], sg_b[j], conv_w[j], odd_w_out[j]) if need_ctx_out else None
        moe_args = (router_g_w[i], router_g_b[i], router_e_w[i], router_e_b[i], w_gate[i], w_up[i], w_down[i])
        h_lat = h_lat + g1 * y
        h_lat = h_lat + g2 * hier_moe(modulate(h_lat, norm2_g[i], sh2, sc2), *moe_args)
        if need_ctx_out:
            h_ctx = h_ctx + cg1 * yc
            h_ctx = h_ctx + cg2 * hier_moe(modulate(h_ctx, norm2_g[i], csh2, csc2), *moe_args)
    return h_lat


ROPE_THETA_2 = 500000.0
NEG_INF = -1e30
NORM_EPS = 1e-6
POS_OFFSET_MAX = 512
PARTIAL_ROT = HEAD_DIM // 4
N_BRANCH = 4
BRANCH_W = 4 * HEAD_DIM
D_FF = 4 * D_MODEL

MLA_HEADS = 4
MLA_NOPE = 64
MLA_ROPE = 32
MLA_V = 64
MLA_Q_LORA = 256
MLA_KV_LORA = 128

NSA_HEADS = 4
NSA_CMP_LEN = 32
NSA_CMP_STRIDE = 16
NSA_SEL_LEN = 64
NSA_TOP_N = 8
NSA_WINDOW = 512
NSA_N_PATHS = 3
NSA_FORCED_SCORE = 1e4

FOX_HEADS = 4

DSA_HEADS = 4
IDX_HEADS = 8
IDX_DIM = 32
IDX_ROT = IDX_DIM // 4
DSA_TOP_K = 256
DSA_KEEP_DIV = 4

MLA_COLS = MLA_Q_LORA + MLA_KV_LORA + MLA_ROPE
NSA_COLS = NSA_HEADS * HEAD_DIM + 6 * HEAD_DIM + NSA_N_PATHS * NSA_HEADS
FOX_COLS = 3 * FOX_HEADS * HEAD_DIM + FOX_HEADS
DSA_COLS = DSA_HEADS * HEAD_DIM + 2 * HEAD_DIM + IDX_HEADS * IDX_DIM + IDX_DIM + IDX_HEADS
GATE_COLS = N_BRANCH * D_MODEL
IN_COLS = MLA_COLS + NSA_COLS + FOX_COLS + DSA_COLS + GATE_COLS


def split_cols(z, sizes):
    cuts = [int(c) for c in np.cumsum(sizes)[:-1]]
    return jnp.split(z, cuts, axis=-1)

def rmsnorm(x, g):
    xf = x.astype(jnp.float32)
    y = xf * lax.rsqrt(jnp.mean(xf * xf, axis=-1, keepdims=True) + NORM_EPS)
    return (y * g.astype(jnp.float32)).astype(x.dtype)

def rope_tables(positions, rot_dim):
    inv = ROPE_THETA_2 ** (-jnp.arange(0, rot_dim, 2, dtype=jnp.float32) / rot_dim)
    ang = positions.astype(jnp.float32)[..., None] * inv
    return (jnp.cos(ang), jnp.sin(ang))

def apply_rope(x, rope):
    cos, sin = rope
    half = cos.shape[-1]
    if x.ndim == 4:
        cos, sin = cos[:, :, None, :], sin[:, :, None, :]
    cos, sin = cos.astype(x.dtype), sin.astype(x.dtype)
    x1, x2 = x[..., :half], x[..., half:2 * half]
    return jnp.concatenate([x1 * cos - x2 * sin, x2 * cos + x1 * sin, x[..., 2 * half:]], axis=-1)

def masked_softmax(s, mask):
    s = jnp.where(mask, s, NEG_INF)
    m = jnp.max(s, axis=-1, keepdims=True)
    p = jnp.exp(s - m) * mask
    return p / jnp.maximum(jnp.sum(p, axis=-1, keepdims=True), 1e-30)

def sweep_query_blocks(fn, seq):
    out = lax.map(fn, jnp.arange(seq // Q_BLOCK))
    out = jnp.moveaxis(out, 0, 1)
    return out.reshape((out.shape[0], seq) + out.shape[3:])

def blocked_causal_attention(q, k, v, scale, decay=None):
    S = q.shape[1]
    key_pos = jnp.arange(S)
    decay_t = None if decay is None else jnp.swapaxes(decay, 1, 2)

    def one_block(i):
        start = i * Q_BLOCK
        qb = lax.dynamic_slice_in_dim(q, start, Q_BLOCK, axis=1)
        s = jnp.einsum('bqhd,bkhd->bhqk', qb, k).astype(jnp.float32) * scale
        if decay_t is not None:
            cq = lax.dynamic_slice_in_dim(decay_t, start, Q_BLOCK, axis=2)
            s = s + (cq[..., :, None] - decay_t[..., None, :])
        q_pos = start + jnp.arange(Q_BLOCK)
        mask = key_pos[None, :] <= q_pos[:, None]
        p = jax.nn.softmax(jnp.where(mask, s, NEG_INF), axis=-1)
        return jnp.einsum('bhqk,bkhd->bqhd', p.astype(v.dtype), v)

    return sweep_query_blocks(one_block, S)

def mla_mixer(z, q_norm_g, w_uq, kv_norm_g, w_ukv, rope):
    B, S, _ = z.shape
    H = MLA_HEADS
    c_q, c_kv, k_rope = split_cols(z, [MLA_Q_LORA, MLA_KV_LORA, MLA_ROPE])
    q = (rmsnorm(c_q, q_norm_g) @ w_uq).reshape(B, S, H, MLA_NOPE + MLA_ROPE)
    q = jnp.concatenate([q[..., :MLA_NOPE], apply_rope(q[..., MLA_NOPE:], rope)], axis=-1)
    kv = (rmsnorm(c_kv, kv_norm_g) @ w_ukv).reshape(B, S, H, MLA_NOPE + MLA_V)
    k_rope = apply_rope(k_rope, rope)
    k = jnp.concatenate([kv[..., :MLA_NOPE],
                         jnp.broadcast_to(k_rope[:, :, None, :], (B, S, H, MLA_ROPE))], axis=-1)
    v = kv[..., MLA_NOPE:]
    o = blocked_causal_attention(q, k, v, (MLA_NOPE + MLA_ROPE) ** -0.5)
    return o.reshape(B, S, H * MLA_V)

def nsa_mixer(z, cmp_w, cmp_pe, rope):
    B, S, _ = z.shape
    H, D = NSA_HEADS, HEAD_DIM
    q, kc, vc, ks, vs, kw, vw, g = split_cols(z, [H * D] + [D] * 6 + [NSA_N_PATHS * H])
    q = apply_rope(q.reshape(B, S, H, D), rope)
    kc, ks, kw = apply_rope(kc, rope), apply_rope(ks, rope), apply_rope(kw, rope)
    g = jax.nn.sigmoid(g.reshape(B, S, NSA_N_PATHS, H))
    scale = D ** -0.5
    t_pos = jnp.arange(S)
    bidx = jnp.arange(B)[:, None, None]

    n_cmp = (S - NSA_CMP_LEN) // NSA_CMP_STRIDE + 1
    cmp_start = jnp.arange(n_cmp) * NSA_CMP_STRIDE
    win_idx = cmp_start[:, None] + jnp.arange(NSA_CMP_LEN)[None, :]

    def compress(t, w, pe):
        blocks = t[:, win_idx] + pe
        return blocks.reshape(B, n_cmp, NSA_CMP_LEN * D) @ w

    k_cmp = compress(kc, cmp_w[0], cmp_pe[0])
    v_cmp = compress(vc, cmp_w[1], cmp_pe[1])
    cmp_mask = (cmp_start + NSA_CMP_LEN - 1)[None, :] <= t_pos[:, None]
    s_cmp = jnp.einsum('bthd,bcd->bhtc', q, k_cmp).astype(jnp.float32) * scale
    p_cmp = masked_softmax(s_cmp, cmp_mask)
    o_cmp = jnp.einsum('bhtc,bcd->bthd', p_cmp.astype(v_cmp.dtype), v_cmp)

    n_sb = S // NSA_SEL_LEN
    sb = jnp.arange(n_sb)
    sb_start = sb * NSA_SEL_LEN
    overlap = jnp.maximum(
        jnp.minimum(cmp_start[:, None] + NSA_CMP_LEN, sb_start[None, :] + NSA_SEL_LEN)
        - jnp.maximum(cmp_start[:, None], sb_start[None, :]), 0).astype(jnp.float32) / NSA_CMP_LEN
    imp = jnp.einsum('bhtc,cj->btj', p_cmp, overlap)
    t_blk = t_pos[:, None] // NSA_SEL_LEN
    forced = (sb[None, :] == 0) | (sb[None, :] == t_blk) | (sb[None, :] == t_blk - 1)
    imp = jnp.where(forced, NSA_FORCED_SCORE, imp)
    imp = jnp.where(sb_start[None, :] <= t_pos[:, None], imp, NEG_INF)
    n_top = min(NSA_TOP_N, n_sb)
    _, sel_idx = lax.top_k(imp, n_top)
    k_blk = ks.reshape(B, n_sb, NSA_SEL_LEN, D)
    v_blk = vs.reshape(B, n_sb, NSA_SEL_LEN, D)

    def sel_block(i):
        start = i * Q_BLOCK
        qb = lax.dynamic_slice_in_dim(q, start, Q_BLOCK, axis=1)
        ib = lax.dynamic_slice_in_dim(sel_idx, start, Q_BLOCK, axis=1)
        kg = k_blk[bidx, ib].reshape(B, Q_BLOCK, n_top * NSA_SEL_LEN, D)
        vg = v_blk[bidx, ib].reshape(B, Q_BLOCK, n_top * NSA_SEL_LEN, D)
        qp = start + jnp.arange(Q_BLOCK)
        kpos = (ib[..., None] * NSA_SEL_LEN + jnp.arange(NSA_SEL_LEN)).reshape(B, Q_BLOCK, -1)
        mask = kpos <= qp[None, :, None]
        s = jnp.einsum('bqhd,bqmd->bhqm', qb, kg).astype(jnp.float32) * scale
        p = masked_softmax(s, mask[:, None])
        return jnp.einsum('bhqm,bqmd->bqhd', p.astype(vg.dtype), vg)

    o_sel = sweep_query_blocks(sel_block, S)

    kpad = jnp.pad(kw, ((0, 0), (NSA_WINDOW, 0), (0, 0)))
    vpad = jnp.pad(vw, ((0, 0), (NSA_WINDOW, 0), (0, 0)))

    def win_block(i):
        start = i * Q_BLOCK
        qb = lax.dynamic_slice_in_dim(q, start, Q_BLOCK, axis=1)
        kb = lax.dynamic_slice_in_dim(kpad, start, NSA_WINDOW + Q_BLOCK, axis=1)
        vb = lax.dynamic_slice_in_dim(vpad, start, NSA_WINDOW + Q_BLOCK, axis=1)
        kpos = start - NSA_WINDOW + jnp.arange(NSA_WINDOW + Q_BLOCK)
        qp = start + jnp.arange(Q_BLOCK)
        mask = ((kpos[None, :] <= qp[:, None]) & (kpos[None, :] > qp[:, None] - NSA_WINDOW)
                & (kpos[None, :] >= 0))
        s = jnp.einsum('bqhd,bkd->bhqk', qb, kb).astype(jnp.float32) * scale
        p = masked_softmax(s, mask)
        return jnp.einsum('bhqk,bkd->bqhd', p.astype(vb.dtype), vb)

    o_win = sweep_query_blocks(win_block, S)

    o = (g[:, :, 0, :, None] * o_cmp + g[:, :, 1, :, None] * o_sel
         + g[:, :, 2, :, None] * o_win)
    return o.reshape(B, S, H * D)

def fox_mixer(z, f_bias):
    B, S, _ = z.shape
    H, D = FOX_HEADS, HEAD_DIM
    q, k, v, f = split_cols(z, [H * D, H * D, H * D, H])
    log_f = jax.nn.log_sigmoid((f + f_bias).astype(jnp.float32))
    c = jnp.cumsum(log_f, axis=1)
    o = blocked_causal_attention(q.reshape(B, S, H, D), k.reshape(B, S, H, D),
                                 v.reshape(B, S, H, D), D ** -0.5, decay=c)
    return o.reshape(B, S, H * D)

def dsa_mixer(z, rope_head, rope_idx):
    B, S, _ = z.shape
    H, D = DSA_HEADS, HEAD_DIM
    q, k, v, qi, ki, w = split_cols(z, [H * D, D, D, IDX_HEADS * IDX_DIM, IDX_DIM, IDX_HEADS])
    q = apply_rope(q.reshape(B, S, H, D), rope_head)
    k = apply_rope(k, rope_head)
    qi = apply_rope(qi.reshape(B, S, IDX_HEADS, IDX_DIM), rope_idx)
    ki = apply_rope(ki, rope_idx)
    n_keep = min(DSA_TOP_K, S // DSA_KEEP_DIV)
    scale = D ** -0.5
    key_pos = jnp.arange(S)
    bidx = jnp.arange(B)[:, None, None]

    def one_block(i):
        start = i * Q_BLOCK
        qb = lax.dynamic_slice_in_dim(q, start, Q_BLOCK, axis=1)
        qib = lax.dynamic_slice_in_dim(qi, start, Q_BLOCK, axis=1)
        wb = lax.dynamic_slice_in_dim(w, start, Q_BLOCK, axis=1).astype(jnp.float32)
        logits = jnp.einsum('bqhd,bkd->bqhk', qib, ki).astype(jnp.float32) * IDX_DIM ** -0.5
        score = jnp.einsum('bqhk,bqh->bqk', jax.nn.relu(logits), wb) * IDX_HEADS ** -0.5
        qp = start + jnp.arange(Q_BLOCK)
        score = jnp.where(key_pos[None, None, :] <= qp[None, :, None], score, NEG_INF)
        _, idx = lax.top_k(score, n_keep)
        kg = k[bidx, idx]
        vg = v[bidx, idx]
        s = jnp.einsum('bqhd,bqkd->bhqk', qb, kg).astype(jnp.float32) * scale
        valid = idx <= qp[None, :, None]
        p = masked_softmax(s, valid[:, None])
        return jnp.einsum('bhqk,bqkd->bqhd', p.astype(vg.dtype), vg)

    o = sweep_query_blocks(one_block, S)
    return o.reshape(B, S, H * D)

def second_inputs(seed: int = 0) -> dict:
    key = jax.random.key(seed)
    ks = jax.random.split(key, 18)

    def nrm(k, shape, fan_in):
        return jax.random.normal(k, shape, jnp.float32) * fan_in ** -0.5

    def gain(k, shape):
        return 1.0 + 0.02 * jax.random.normal(k, shape, jnp.float32)

    x = jax.random.normal(ks[0], (BATCH, SEQ, D_MODEL), jnp.float32)
    offset = jax.random.randint(ks[1], (BATCH, 1), 0, POS_OFFSET_MAX, dtype=jnp.int32)
    positions = offset + jnp.arange(SEQ, dtype=jnp.int32)[None, :]
    return {
        "x": x,
        "positions": positions,
        "norm1_g": gain(ks[2], (DEPTH, D_MODEL)),
        "w_in": nrm(ks[3], (DEPTH, D_MODEL, IN_COLS), D_MODEL),
        "mla_q_norm_g": gain(ks[4], (DEPTH, MLA_Q_LORA)),
        "mla_w_uq": nrm(ks[5], (DEPTH, MLA_Q_LORA, MLA_HEADS * (MLA_NOPE + MLA_ROPE)), MLA_Q_LORA),
        "mla_kv_norm_g": gain(ks[6], (DEPTH, MLA_KV_LORA)),
        "mla_w_ukv": nrm(ks[7], (DEPTH, MLA_KV_LORA, MLA_HEADS * (MLA_NOPE + MLA_V)), MLA_KV_LORA),
        "nsa_cmp_pe": 0.1 * jax.random.normal(ks[8], (DEPTH, 2, NSA_CMP_LEN, HEAD_DIM), jnp.float32),
        "nsa_cmp_w": nrm(ks[9], (DEPTH, 2, NSA_CMP_LEN * HEAD_DIM, HEAD_DIM), NSA_CMP_LEN * HEAD_DIM),
        "fox_f_bias": 1.0 + 0.1 * jax.random.normal(ks[10], (DEPTH, FOX_HEADS), jnp.float32),
        "w_branch": nrm(ks[11], (DEPTH, N_BRANCH, BRANCH_W, D_MODEL), BRANCH_W),
        "w_out": nrm(ks[12], (DEPTH, D_MODEL, D_MODEL), D_MODEL),
        "norm2_g": gain(ks[13], (DEPTH, D_MODEL)),
        "w_up": nrm(ks[14], (DEPTH, D_MODEL, D_FF), D_MODEL),
        "w_down": nrm(ks[15], (DEPTH, D_FF, D_MODEL), D_FF),
        "final_g": gain(ks[16], (D_MODEL,)),
    }

def second_block(x, positions, norm1_g, w_in, mla_q_norm_g, mla_w_uq, mla_kv_norm_g, mla_w_ukv,
              nsa_cmp_pe, nsa_cmp_w, fox_f_bias, w_branch, w_out, norm2_g, w_up, w_down, final_g):
    B, S, _ = x.shape
    rope_mla = rope_tables(positions, MLA_ROPE)
    rope_head = rope_tables(positions, PARTIAL_ROT)
    rope_idx = rope_tables(positions, IDX_ROT)
    for l in range(DEPTH):
        h = rmsnorm(x, norm1_g[l])
        z = h @ w_in[l]
        z_mla, z_nsa, z_fox, z_dsa, z_gate = split_cols(
            z, [MLA_COLS, NSA_COLS, FOX_COLS, DSA_COLS, GATE_COLS])
        o_mla = mla_mixer(z_mla, mla_q_norm_g[l], mla_w_uq[l], mla_kv_norm_g[l], mla_w_ukv[l], rope_mla)
        o_nsa = nsa_mixer(z_nsa, nsa_cmp_w[l], nsa_cmp_pe[l], rope_head)
        o_fox = fox_mixer(z_fox, fox_f_bias[l])
        o_dsa = dsa_mixer(z_dsa, rope_head, rope_idx)
        branches = jnp.stack([o_mla, o_nsa, o_fox, o_dsa], axis=2)
        lifted = jnp.einsum('bsnc,ncd->bsnd', branches, w_branch[l])
        gates = jax.nn.sigmoid(z_gate.reshape(B, S, N_BRANCH, D_MODEL))
        mixed = jnp.sum(gates * lifted, axis=2)
        x = x + mixed @ w_out[l]
        h2 = rmsnorm(x, norm2_g[l])
        x = x + jnp.square(jax.nn.relu(h2 @ w_up[l])) @ w_down[l]
    return rmsnorm(x, final_g)


def setup_inputs(seed=0):
    out = dict(first_inputs(seed))
    for name, value in second_inputs(seed + 1).items():
        if name != "x":
            out[name + "_2"] = value
    return out


def reference(
    x, c, ctx, c_ctx, mod_w, mod_b, norm1_g, norm2_g, even_w_in, q_gain, k_gain, pool_w,
    pool_scale, even_w_out, odd_w_in, sg_gain, sg_w, sg_b, conv_w, odd_w_out, router_g_w,
    router_g_b, router_e_w, router_e_b, w_gate, w_up, w_down, positions_2, norm1_g_2, w_in_2,
    mla_q_norm_g_2, mla_w_uq_2, mla_kv_norm_g_2, mla_w_ukv_2, nsa_cmp_pe_2, nsa_cmp_w_2,
    fox_f_bias_2, w_branch_2, w_out_2, norm2_g_2, w_up_2, w_down_2, final_g_2,
):
    x = first_block(
        x, c, ctx, c_ctx, mod_w, mod_b, norm1_g, norm2_g, even_w_in, q_gain, k_gain, pool_w,
        pool_scale, even_w_out, odd_w_in, sg_gain, sg_w, sg_b, conv_w, odd_w_out, router_g_w,
        router_g_b, router_e_w, router_e_b, w_gate, w_up, w_down,
    )
    return second_block(
        x, positions_2, norm1_g_2, w_in_2, mla_q_norm_g_2, mla_w_uq_2, mla_kv_norm_g_2,
        mla_w_ukv_2, nsa_cmp_pe_2, nsa_cmp_w_2, fox_f_bias_2, w_branch_2, w_out_2, norm2_g_2,
        w_up_2, w_down_2, final_g_2,
    )


_drawn_inputs = setup_inputs


def setup_inputs(seed=0):
    import zlib

    import numpy as np

    out = dict(_drawn_inputs(seed))
    spreads = {}
    factors = {'q_gain': 6.211,
     'k_gain': 5.76,
     'sg_gain': 2.795,
     'router_g_b': 8.0,
     'router_e_b': 8.0,
     'norm1_g_2': 2.725,
     'mla_q_norm_g_2': 8.0,
     'mla_kv_norm_g_2': 8.0,
     'fox_f_bias_2': 3.177,
     'final_g_2': 2.725}
    for name, (base, spread) in spreads.items():
        noise = np.random.default_rng([zlib.crc32(name.encode()), seed]).standard_normal(out[name].shape)
        drawn = base * np.exp(spread * noise) if base else spread * noise
        out[name] = __import__('jax').numpy.asarray(drawn.astype(out[name].dtype))
    for name, factor in factors.items():
        out[name] = (out[name] * factor).astype(out[name].dtype)
    return out
```

```python
from contextlib import ExitStack

import concourse.bass as bass
from concourse import mybir
from concourse.alu_op_type import AluOpType as ALU

F32 = mybir.dt.float32
I32 = mybir.dt.int32
ACT = mybir.ActivationFunctionType
AX = mybir.AxisListType.X
P = 128
EPS = 1e-6
NEG = -1e30
TWO_PI = 6.283185307179586
SLOT = 4096
ZW = (312, 512, 512, 416, 512, 256)

CST = dict(ident=(0, 128), ones=(128, 128), tri=(256, 128), mask=(384, 256), cadd=(640, 30),
           cmul=(670, 30), ropc=(700, 128), rops=(828, 128), inv=(956, 28))
NCST = 984
COL = dict(n1a=(0, 16), n2a=(16, 16), n1b=(32, 16), n2b=(48, 16), modb=(64, 96), c=(160, 8),
           cc=(168, 8), ps=(176, 4), cw=(180, 12), sgw=(192, 512), plw=(704, 512),
           rw=(1216, 320), gq=(1536, 4), gkv=(1540, 2), pe=(1542, 128))
NCOL = 1670
ROW = dict(qkg=(0, 640), sgg=(640, 512), sgb=(1152, 512), rb=(1664, 40), fb=(1704, 8),
           fg=(1712, 1024), gb=(2736, 4096))
NROW = 6832
RKEEP = 1712


class Engine:

    def __init__(self, key, chained):
        self.key, self.chained, self.n, self.queue = key, chained, 0, []

    def do(self, fns, *after):
        fns = fns if isinstance(fns, list) else [fns]
        if self.chained and self.n:
            after = (*after, (self.key, self.n))
        self.n += 1
        self.queue.append((after, fns, self.key, 1))
        return (self.key, self.n)

    def dma(self, fn, key, count, *after):
        self.queue.append((after, [fn], key, 16))
        return (key, count)


def tokens(after):
    for t in after:
        if t is None:
            continue
        if callable(t):
            yield from tokens([t()])
        elif isinstance(t, list):
            yield from tokens(t)
        else:
            yield t


def replay(engine, unit, sems):
    seen = {}
    for after, fns, key, inc in engine.queue:
        need = {}
        for k, v in tokens(after):
            need[k] = max(need.get(k, 0), v)
        for k, v in need.items():
            if seen.get(k, 0) < v:
                unit.wait_ge(sems[k], v)
                seen[k] = v
        for fn in fns:
            ins = fn(unit)
        ins.then_inc(sems[key], inc)


def build(nc, t_in, out, dbg=None):
    with ExitStack() as ctx:
        def sb(name, *shape, dt=F32):
            return ctx.enter_context(nc.sbuf_tensor(name, [P, *shape], dt))

        pe, ac, ve, po, sp = (Engine("pe", False), Engine("ac", True), Engine("ve", True),
                              Engine("po", True), Engine("sp", False))

        NRING = 3
        ring = [sb(f"ring{i}", SLOT) for i in range(NRING)]
        cst = sb("cst", NCST)
        col = sb("col", NCOL)
        row = sb("row", RKEEP)
        x = sb("x", 2, 1024)
        xn = sb("xn", 2, 1024)
        hT = sb("hT", 8, 256)
        yT = sb("yT", 8, 256)
        big = sb("big", 8192)
        z = sb("z", 2, 2520)
        s1 = sb("s1", 1024)
        s2 = sb("s2", 1024)
        st = sb("st", 96)
        mcol = sb("mcol", 64)
        sil = sb("sil", 16)
        grow = sb("grow", 2, 1024)
        acc = sb("acc", 2, 512)
        cadj = sb("cadj", 4, 8)
        rt = sb("rt", 400)
        tab = sb("tab", 56 * 6)
        posi = sb("posi", 2, dt=I32)
        ps = ctx.enter_context(nc.psum_tensor("ps", [P, 8, 512], F32))

        def C(name):
            a, n = CST[name]
            return cst[:, a:a + n]

        def K(name, a=0, n=None):
            b, m = COL[name]
            return col[:, b + a:b + (m if n is None else a + n)]

        def R(name, a=0, n=None):
            b, m = ROW[name]
            return row[:, b + a:b + (m if n is None else a + n)]

        bank_free = [[] for _ in range(8)]
        turn = dict(A=0, B=0)

        def take(pool):
            b = (0 if pool == "A" else 4) + turn[pool]
            turn[pool] = (turn[pool] + 1) % 4
            return b

        def take2():
            b = 0 if turn["A"] in (0, 3) else 2
            turn["A"] = (b + 2) % 4
            return b

        chunks = []

        class Chunk:
            pass

        def load(src, parts=P):
            c = Chunk()
            n = len(chunks)
            c.free = None
            w = src.shape[1]
            c.buf = ring[n % NRING]
            c.ap = c.buf[0:parts, 0:w]
            c.ready = (f"w{n % NRING}", 16 * (n // NRING + 1))
            sp.dma(lambda e: e.dma_start(c.buf[0:parts, 0:w], src), *c.ready,
                   (lambda: chunks[n - NRING].free) if n >= NRING else None)
            chunks.append(c)
            return c

        def mm(o, l, r, first, last):
            return lambda e: e.matmul(o, l, r, start=first, stop=last)

        def tr(o, i, n=P):
            return lambda e: e.transpose(o, i, C("ident")[0:n, 0:n])

        def bc(ap, n, at=1):
            a = ap.unsqueeze(at)
            return a.broadcast_to([*a.shape[:at], n, *a.shape[at + 1:]])

        def TT(o, a, b, op):
            return lambda e: e.tensor_tensor(o, a, b, op)

        def TS(o, a, x1, x2, op0, op1=None):
            if op1 is None:
                return lambda e: e.tensor_scalar(o, a, x1, None, op0)
            return lambda e: e.tensor_scalar(o, a, x1, x2, op0, op1)

        def STT(o, a, s, b, op0, op1):
            return lambda e: e.scalar_tensor_tensor(out=o, in0=a, scalar=s, in1=b, op0=op0, op1=op1)

        def CP(o, a):
            return lambda e: e.tensor_copy(o, a)

        def AC(o, a, f=ACT.Copy, **kw):
            return lambda e: e.activation(o, a, f, **kw)

        def dump(name, ap, tok):
            if dbg is not None:
                dbg(name, ap, tok, sp)

        ndma = 0

        def small(dst, src):
            nonlocal ndma
            ndma += 1
            return sp.dma(lambda e: e.dma_start(dst, src), f"d{ndma}", 16)

        t_cst = small(cst[:, :], t_in["cst"])
        t_col = small(col[:, :], t_in["colp"])
        t_x = small(x[:, :, :], t_in["x"])
        t_cx = small(z[:, :, 0:1024], t_in["ctx"])
        t_row = small(row[:, :], t_in["rowp"][0:1, 0:RKEEP].broadcast_to([P, RKEEP]))
        t_pos = small(posi[:, :], t_in["pos"])

        t = ac.do(AC(sil[:, :], col[:, 160:176], ACT.Exp, scale=-1.0), t_col)
        t = ve.do(TS(sil[:, :], sil[:, :], 1.0, None, ALU.add), t)
        t = ve.do(lambda e: e.reciprocal(sil[:, :], sil[:, :]))
        t_sil = ve.do(TT(sil[:, :], sil[:, :], col[:, 160:176], ALU.mult), t_col)

        acc_free = [None, None]
        n_acc = 0
        t_mcol = {}
        t_grow = {}
        grow_free = [None, None]

        def adaln_acc(w, which):
            nonlocal n_acc
            a = n_acc % 2
            n_acc += 1
            wv = w.ap.rearrange("p (k n) -> p k n", k=8)
            for k in range(8):
                s = sil[:, 8 * which + k:8 * which + k + 1]
                if k == 0:
                    t = ve.do(TS(acc[:, a, :], wv[:, k, :], s, None, ALU.mult), w.ready, acc_free[a], t_sil)
                else:
                    t = ve.do(STT(acc[:, a, :], wv[:, k, :], s, acc[:, a, :], ALU.mult, ALU.add))
            return a, t

        def adaln_cols(a, t, dst, bias):
            b = take("B")
            tp = pe.do([mm(ps[:, b, j:j + 1], acc[:, a, 128 * j:128 * j + 128], C("ones")[:, 0:1], True, True)
                        for j in range(4)], t, t_cst, bank_free[b])
            acc_free[a] = tp
            t = ve.do(TT(dst, ps[:, b, 0:4], bias, ALU.add), tp, t_col)
            bank_free[b] = [t]
            return t

        def adaln(l, piece):
            part, half = piece // 2, piece % 2
            w = load(t_in["wmod"][l, piece])
            a, t = adaln_acc(w, 0)
            w.free = t
            if part in (2, 5):
                g = 0 if part == 2 else 1
                b = take("B")
                tp = pe.do([mm(ps[:, b, :], C("ones"), acc[:, a, :], True, True)], t, t_cst, bank_free[b])
                acc_free[a] = tp
                n0 = (2 * l + g) * 1024 + half * 512
                t_b = t_gb.pop((l, g)) if (l, g) in t_gb else t_gbs[(l, g)]
                t_gbs[(l, g)] = t_b
                dst = grow[:, g, 512 * half:512 * half + 512]
                t = ve.do(TT(dst, dst, ps[:, b, :], ALU.add), tp, t_b)
                bank_free[b] = [t]
                t_grow[(l, g, half)] = t
            else:
                j = {0: 0, 1: 1, 3: 2, 4: 3}[part]
                m0 = (32 * (l % 2)) + 8 * j + 4 * half
                t = adaln_cols(a, t, mcol[:, m0:m0 + 4], K("modb", 48 * l + 8 * part + 4 * half, 4))
                t_mcol[(l, j)] = t
            return w, (a, t)

        t_gb, t_gbs = {}, {}

        def gate_bias(l, g, free):
            nonlocal ndma
            n0 = 2736 + (2 * l + g) * 1024
            ndma += 1
            t_gb[(l, g)] = sp.dma(
                lambda e: e.dma_start(grow[:, g, :], t_in["rowp"][0:1, n0:n0 + 1024].broadcast_to([P, 1024])),
                f"d{ndma}", 16, lambda: free[0] if free else None)

        def rstd(dst, ss, inv_n, tmp, after):
            ve.do(TS(ss, ss, inv_n, EPS, ALU.mult, ALU.add), after)
            t = ve.do(CP(tmp, ss))
            t = ac.do(AC(dst, ss, ACT.Ln), t)
            t = ac.do(AC(dst, dst, ACT.Exp, scale=-0.5))
            ve.do(TT(tmp, tmp, dst, ALU.mult), t)
            ve.do(TT(tmp, tmp, dst, ALU.mult))
            ve.do(TS(tmp, tmp, -0.5, 1.5, ALU.mult, ALU.add))
            return ve.do(TT(dst, dst, tmp, ALU.mult))

        hT_free = []
        xn_free = []

        def norm_rows(src, after, scales):
            for t in range(2):
                ta = ac.do(AC(s1[:, 0:1024], src[:, t, :], ACT.Square, accum_out=st[:, t:t + 1]),
                           after, s1_free[:])
            tr_ = rstd(st[:, 2:4], st[:, 0:2], 1.0 / 1024, st[:, 4:6], ta)
            s1_free[:] = [ta]
            ts = []
            for t in range(2):
                ts.append(ac.do(AC(xn[:, t, :], src[:, t, :], scale=st[:, 2 + t:3 + t]), tr_, xn_free[:]))
            return ts[-1]

        s1_free = []

        def norm_T(src, after, scale, shift, t_sc, dst=None, dst_free=None):
            dst = hT if dst is None else dst
            free = hT_free[:] if dst_free is None else dst_free
            tn = norm_rows(src, after, None)
            out_t = []
            for k in range(0, 8, 2):
                b = take("B")
                tp = pe.do([tr(ps[:, b, 256 * j + 128 * t:256 * j + 128 * t + 128],
                               xn[:, t, 128 * (k + j):128 * (k + j) + 128])
                            for j in range(2) for t in range(2)], tn, t_cst, bank_free[b])
                for j in range(2):
                    i, o = ps[:, b, 256 * j:256 * j + 256], dst[:, k + j, :]
                    sc = scale[:, k + j:k + j + 1]
                    sh = 0.0 if shift is None else shift[:, k + j:k + j + 1]
                    if k % 4 == 0:
                        f = TS(o, i, sc, None, ALU.mult) if shift is None else TS(o, i, sc, sh, ALU.mult, ALU.add)
                        tt = ve.do(f, tp, t_sc, free)
                    else:
                        f = AC(o, i, scale=sc) if shift is None else AC(o, i, ACT.Identity, scale=sc, bias=sh)
                        tt = ac.do(f, tp, t_sc, free)
                bank_free[b] = [tt]
                out_t.append(tt)
            xn_free[:] = [tp]
            return out_t

        def cond_scale(l, which, norm, dst):
            sc = mcol[:, 32 * l + 16 * which + 8:32 * l + 16 * which + 16]
            return ve.do(STT(dst, sc, 1.0, norm, ALU.add, ALU.mult), t_mcol[(l, 2 * which + 1)], t_col)

        def proj_rows(w, c0, n, hs, t_h, tile, pool="B"):
            b = take(pool)
            wv = w.ap.rearrange("p (k n) -> p k n", k=8)
            tp = pe.do([mm(ps[:, b, 0:n], hs[:, k, 128 * tile:128 * tile + 128], wv[:, k, c0:c0 + n],
                           k == 0, k == 7) for k in range(8)], w.ready, t_h, bank_free[b])
            return b, tp

        def out_proj(wname, l, ysrc, t_y, gate):
            res = []
            for h in range(2):
                w = load(t_in[wname][h] if l is None else t_in[wname][l, h])
                for t in range(2):
                    b, tp = proj_rows(w, 0, 512, ysrc, t_y, t)
                    w.free = tp
                    xs = x[:, t, 512 * h:512 * h + 512]
                    if gate is None:
                        tt = ve.do(TT(xs, xs, ps[:, b, :], ALU.add), tp)
                    else:
                        gl, g = gate
                        ve.do(TT(s2[:, 0:512], ps[:, b, :], grow[:, g, 512 * h:512 * h + 512], ALU.mult), tp,
                              t_grow[(gl, g, h)], s2_free[:])
                        tt = ve.do(TT(xs, xs, s2[:, 0:512], ALU.add))
                    bank_free[b] = [tt]
                    res.append(tt)
            return res, tp

        s2_free = []

        gate_bias(0, 0, None)
        gate_bias(0, 1, None)
        ctx_pieces = []
        for piece in range(4):
            w, (a, _) = adaln(0, piece)
            a2, t2 = adaln_acc(w, 1)
            w.free = t2
            part, half = piece // 2, piece % 2
            ctx_pieces.append(adaln_cols(a2, t2, cadj[:, part, 4 * half:4 * half + 4],
                                         K("modb", 8 * part + 4 * half, 4)))
        t_cc = ve.do(STT(cadj[:, 2, :], cadj[:, 1, :], 1.0, K("n1a", 0, 8), ALU.add, ALU.mult), *ctx_pieces)
        t_sc = cond_scale(0, 0, K("n1a", 0, 8), cadj[:, 3, :])
        th = norm_T(x, t_x, cadj[:, 3, :], mcol[:, 0:8], t_sc)
        thc = norm_T(z[:, :, 0:1024], t_cx, cadj[:, 2, :], cadj[:, 0, :], t_cc, dst=yT, dst_free=[])
        dump("hT0", hT, th)
        dump("cT0", yT, thc)
        cs = z
        wq = load(t_in["we_q"])
        wkv = load(t_in["we_kv"])
        wp = load(t_in["we_p"])
        tz = []
        for t in range(2):
            b, tp = proj_rows(wkv, 0, 256, yT, thc, t)
            t_ = ve.do(CP(z[:, t, 1280:1536], ps[:, b, 0:256]), tp, xn_free[:])
            bank_free[b] = [t_]
            tz.append(t_)
        for t in range(2):
            b, tp = proj_rows(wq, 0, 512, hT, th, t)
            wq.free = tp
            t_ = ve.do(CP(z[:, t, 0:512], ps[:, b, :]), tp)
            bank_free[b] = [t_]
            b, tp = proj_rows(wkv, 0, 256, hT, th, t)
            wkv.free = tp
            t_ = ve.do(CP(z[:, t, 512:768], ps[:, b, 0:256]), tp)
            bank_free[b] = [t_]
            b, tp = proj_rows(wp, 0, 512, hT, th, t)
            wp.free = tp
            t_ = ac.do(AC(z[:, t, 768:1280], ps[:, b, :]), tp)
            bank_free[b] = [t_]
            tz.append(t_)
        hT_free[:] = [tp]
        yT_free = [tp]
        for t in range(2):
            ve.do(TT(s1[:, 0:640], z[:, t, 0:640], z[:, t, 0:640], ALU.mult), s1_free[:], tz)
            ve.do(lambda e, t=t: e.tensor_reduce(st[:, 8 + 12 * t:18 + 12 * t],
                                                 s1[:, 0:640].rearrange("p (h d) -> p h d", d=64), AX, ALU.add))
            ve.do(TT(s1[:, 640:768], z[:, t, 1280:1408], z[:, t, 1280:1408], ALU.mult))
            tr_ = ve.do(lambda e, t=t: e.tensor_reduce(st[:, 18 + 12 * t:20 + 12 * t],
                                                       s1[:, 640:768].rearrange("p (h d) -> p h d", d=64),
                                                       AX, ALU.add))
        tr_ = rstd(st[:, 32:56], st[:, 8:32], 1.0 / 64, st[:, 56:80], tr_)
        for t in range(2):
            zq = z[:, t, 0:640].rearrange("p (h d) -> p h d", d=64)
            zc = z[:, t, 1280:1408].rearrange("p (h d) -> p h d", d=64)
            r = st[:, 32 + 12 * t:42 + 12 * t].unsqueeze(2).broadcast_to([P, 10, 64])
            rc = st[:, 42 + 12 * t:44 + 12 * t].unsqueeze(2).broadcast_to([P, 2, 64])
            ve.do(TT(zq, zq, r, ALU.mult), t_row)
            ve.do(TT(z[:, t, 0:640], z[:, t, 0:640], R("qkg"), ALU.mult))
            ve.do(TT(zc, zc, rc, ALU.mult))
            t_kc = ve.do(TT(z[:, t, 1280:1408], z[:, t, 1280:1408], R("qkg", 512, 128), ALU.mult))
            cosv, sinv = C("ropc")[:, 64 * t:64 * t + 64], C("rops")[:, 64 * t:64 * t + 64]
            ve.do(TT(s1[:, 0:640].rearrange("p (h d) -> p h d", d=64), zq, bc(cosv, 10), ALU.mult))
            z5 = z[:, t, 0:640].rearrange("p (h a b j) -> p h a b j", a=2, b=2, j=16)
            s5 = s2[:, 0:640].rearrange("p (h a b j) -> p h a b j", a=2, b=2, j=16)
            v4 = sinv.rearrange("p (a b j) -> p a b j", a=2, b=2)
            for a in range(2):
                for q in range(2):
                    ve.do(TT(s5[:, :, a, q, :], z5[:, :, a, 1 - q, :], bc(v4[:, a, q, :], 10), ALU.mult))
            t_q = ve.do(TT(z[:, t, 0:640], s1[:, 0:640], s2[:, 0:640], ALU.add))
        s1_free[:] = s2_free[:] = []
        qT = big[:, 0:1024].rearrange("p (i n) -> p i n", i=4)
        kT = big[:, 1024:1536]
        tq = []
        for i in range(6):
            b = take("B")
            c0 = 128 * i if i < 5 else 1280
            tp = pe.do([tr(ps[:, b, 128 * t:128 * t + 128], z[:, t, c0:c0 + 128]) for t in range(2)],
                       t_q, t_kc, bank_free[b])
            dst = qT[:, i, :] if i < 4 else (kT[:, 256:512] if i == 4 else kT[:, 0:256])
            t_ = ac.do(AC(dst, ps[:, b, 0:256]), tp)
            bank_free[b] = [t_]
            tq.append(t_)
        dump("qT0", big[:, 0:1536], tq)
        for piece in range(4, 6):
            adaln(0, piece)
        pT = big[:, 2048:6144].rearrange("p (u k n) -> p u k n", u=4, k=4)
        pT_free = [None] * 4
        pb_free = [None] * 4
        pbuf = big[:, 6144:8192].rearrange("p (u n) -> p u n", u=4)
        oT_tok = []
        nh = 0
        for i in range(4):
            ob = None
            for s in range(2):
                lo = 64 * s
                u = nh % 4
                nh += 1
                for t in range(2):
                    v = (2 * nh + t) % 4
                    b = take("A")
                    tp = pe.do([mm(ps[:, b, :], qT[lo:lo + 64, i, 128 * t:128 * t + 128], kT[lo:lo + 64, :],
                                   True, True)], tq, bank_free[b])
                    m = st[:, 80 + v:81 + v]
                    ve.do(lambda e, b=b, m=m: e.tensor_reduce(m, ps[:, b, :], AX, ALU.max), tp, pb_free[v])
                    t_ = ve.do(TS(m, m, -0.125, None, ALU.mult))
                    sm = st[:, 84 + v:85 + v]
                    t_ = ac.do(AC(pbuf[:, v, :], ps[:, b, :], ACT.Exp, bias=m, scale=0.125, accum_out=sm), t_)
                    bank_free[b] = [t_]
                    ve.do(lambda e, sm=sm: e.reciprocal(sm, sm), t_)
                    t_ = ve.do(TS(pbuf[:, v, :], pbuf[:, v, :], sm, None, ALU.mult))
                    b = take("B")
                    tp = pe.do([tr(ps[:, b, 128 * k:128 * k + 128], pbuf[:, v, 128 * k:128 * k + 128])
                                for k in range(4)], t_, bank_free[b])
                    pb_free[v] = tp
                    t_p = ac.do(AC(pT[:, u, :, 128 * t:128 * t + 128],
                                   ps[:, b, :].rearrange("p (k n) -> p k n", k=4)), tp, pT_free[u])
                    bank_free[b] = [t_p]
                if ob is None:
                    ob = take("B")
                fns = []
                for k in range(4):
                    vv = z[:, k % 2, 1408 + lo:1472 + lo] if k < 2 else z[:, k % 2, 640 + lo:704 + lo]
                    fns.append(mm(ps[lo:lo + 64, ob, 0:256], vv, pT[:, u, k, :], k == 0, k == 3))
                tp = pe.do(fns, t_p, bank_free[ob])
                pT_free[u] = tp
            t_ = ve.do(CP(yT[:, i, :], ps[:, ob, 0:256]), tp, yT_free)
            bank_free[ob] = [t_]
            oT_tok.append(t_)
        wpm = load(t_in["pm"])
        pm = wpm.ap.rearrange("p (k g n) -> p k g n", k=2, g=4)
        for g in range(4):
            b = take("B")
            tp = pe.do([mm(ps[:, b, 0:256], z[:, k, 768 + 128 * g:896 + 128 * g], pm[:, k, g, :], k == 0, k == 1)
                        for k in range(2)], wpm.ready, tz, bank_free[b])
            wpm.free = tp
            t_ = ac.do(AC(s1[:, 256 * g:256 * g + 256], ps[:, b, 0:256]), tp, t_q)
            bank_free[b] = [t_]
            b = take("B")
            tp = pe.do([mm(ps[:, b, 0:256], K("plw", 128 * g, 128), s1[:, 256 * g:256 * g + 256], True, True)],
                       t_, t_col, bank_free[b])
            t_ = ve.do(TS(yT[:, 4 + g, :], ps[:, b, 0:256], K("ps", g, 1), None, ALU.mult), tp)
            bank_free[b] = [t_]
            oT_tok.append(t_)
        s1_free[:] = [tp]
        dump("yT0", yT, oT_tok)
        tx, tp = out_proj("we_out", None, yT, oT_tok, (0, 0))
        yT_free = [tp]
        dump("x0", x, tx)
        gfree = tx[-1:]

        for piece in range(6, 12):
            adaln(0, piece)

        def router(l, t_h):
            L = rt[:, 0:40].rearrange("p (t n) -> p t n", t=2)
            b = take("B")
            rw = K("rw", 160 * l, 160).rearrange("p (k n) -> p k n", k=8)
            fns = []
            for t in range(2):
                fns += [mm(ps[:, b, 20 * t:20 * t + 20], hT[:, k, 128 * t:128 * t + 128], rw[:, k, :],
                           k == 0, k == 7) for k in range(8)]
            tp = pe.do(fns, t_h, t_col, bank_free[b])
            tv = ve.do(TT(L, ps[:, b, 0:40].rearrange("p (t n) -> p t n", t=2), bc(R("rb", 20 * l, 20), 2),
                          ALU.add), tp, t_row)
            bank_free[b] = [tv]
            G, E_ = L[:, :, 0:4], L[:, :, 4:20]
            gm, gs = rt[:, 40:42], rt[:, 42:44]
            m1, m2, d = rt[:, 44:46], rt[:, 46:48], rt[:, 48:50]
            w1, w2 = rt[:, 50:52], rt[:, 52:54]
            ge = rt[:, 56:64].rearrange("p (t n) -> p t n", t=2)
            gk = rt[:, 64:72].rearrange("p (t n) -> p t n", t=2)
            gc = rt[:, 72:80].rearrange("p (t n) -> p t n", t=2)
            em = rt[:, 80:112].rearrange("p (t n) -> p t n", t=2)
            k1 = rt[:, 112:144].rearrange("p (t n) -> p t n", t=2)
            k2 = rt[:, 144:176].rearrange("p (t n) -> p t n", t=2)
            cu = rt[:, 176:208].rearrange("p (t n) -> p t n", t=2)
            comb = rt[:, 208:240].rearrange("p (t n) -> p t n", t=2)

            def b3(a, n):
                return a.unsqueeze(2).broadcast_to([P, 2, n])

            def red(o, i, op):
                return ve.do(lambda e: e.tensor_reduce(o, i, AX, op))

            def first_only(k, c):
                for t in range(2):
                    ve.do(lambda e, t=t: e.tensor_tensor_scan(c[:, t, :], k[:, t, :], k[:, t, :], 0.0,
                                                              ALU.add, ALU.bypass))
                ve.do(STT(k, c, 1.0, k, ALU.is_equal, ALU.mult))

            red(gm, G, ALU.max)
            tv = ve.do(TT(ge, G, b3(gm, 4), ALU.subtract))
            ta = ac.do(AC(ge, ge, ACT.Exp), tv)
            ve.do(TT(gk, G, b3(gm, 4), ALU.is_equal))
            first_only(gk, gc)
            pen = rt[:, 240:248].rearrange("p (t n) -> p t n", t=2)
            ve.do(TS(pen, gk, 1.0, 1e30, ALU.subtract, ALU.mult))
            for t in range(2):
                ve.do(TT(em[:, t, :].rearrange("p (g n) -> p g n", n=4),
                         E_[:, t, :].rearrange("p (g n) -> p g n", n=4),
                         pen[:, t, :].unsqueeze(2).broadcast_to([P, 4, 4]), ALU.add))
            red(m1, em, ALU.max)
            ve.do(TT(k1, em, b3(m1, 16), ALU.is_equal))
            first_only(k1, cu)
            ve.do(STT(em, k1, -3e30, em, ALU.mult, ALU.add))
            red(m2, em, ALU.max)
            ve.do(TT(k2, em, b3(m2, 16), ALU.is_equal))
            first_only(k2, cu)
            tv = ve.do(TT(d, m2, m1, ALU.subtract))
            ta = ac.do(AC(d, d, ACT.Exp), tv)
            ve.do(lambda e: e.tensor_reduce(gs, ge, AX, ALU.add), ta)
            ve.do(STT(w1, d, 1.0, gs, ALU.add, ALU.mult))
            ve.do(lambda e: e.reciprocal(w1, w1))
            ve.do(TT(w2, w1, d, ALU.mult))
            ve.do(TT(comb, k1, b3(w1, 16), ALU.mult))
            ve.do(TT(k2, k2, b3(w2, 16), ALU.mult))
            tv = ve.do(TT(comb, comb, k2, ALU.add))
            b = take("B")
            tp = pe.do([tr(ps[0:16, b, 128 * t:128 * t + 128], comb[:, t, :]) for t in range(2)], tv, bank_free[b])
            cT = tab16[:, :]
            t_ = ve.do(CP(cT, ps[0:16, b, 0:256]), tp, cT_free[:])
            bank_free[b] = [t_]
            return t_

        tab16 = ctx.enter_context(nc.sbuf_tensor("tab16", [16, 256], F32))
        cT_free = []
        hid_free = [None, None]
        hid = big[:, 0:1024].rearrange("p (u f n) -> p u f n", u=2, f=2)
        ex = big[:, 2048:4096].rearrange("p (u n) -> p u n", u=4)

        def experts(l, t_h, extra):
            acc_b = [0, 1, 2, 3]
            acc_first = [bank_free[b] for b in acc_b]
            t_c = router(l, t_h)
            dump(f"comb{l}", tab16, t_c)
            done = {}
            dw = None
            for e_ in range(17):
                if e_ < 16:
                    w = load(t_in["wgu"][l, e_])
                    wv = w.ap.rearrange("p (s k n) -> p s k n", s=2, k=8)
                    u = e_ % 2
                    b = take("B")
                    cb = b
                    tcw = pe.do([mm(ps[:, b, 0:256], C("ident")[0:16, e_:e_ + 1].broadcast_to([16, P]),
                                    tab16[:, :], True, True)], t_c, bank_free[b])
                    cw = s2[:, 256 * (e_ % 4):256 * (e_ % 4) + 256]
                    t_cw = ac.do(AC(cw, ps[:, b, 0:256]), tcw, cw_free[e_ % 4])
                    bank_free[b] = [t_cw]
                    toks = []
                    for f in range(2):
                        b = take("B")
                        tp = pe.do([mm(ps[:, b, 256 * s:256 * s + 256], wv[:, s, k, 128 * f:128 * f + 128],
                                       hT[:, k, :], k == 0, k == 7) for s in range(2) for k in range(8)],
                                   w.ready, t_h, bank_free[b])
                        w.free = tp
                        v = ex[:, 2 * u + f, 0:256]
                        v2 = ex[:, 2 * u + f, 256:512]
                        ta = ac.do(AC(v, ps[:, b, 0:256], ACT.Exp, scale=-1.0), tp, hid_free[u])
                        ve.do(TS(v, v, 1.0, None, ALU.add), ta)
                        ve.do(lambda e, v=v: e.reciprocal(v, v))
                        ve.do(TT(v, v, ps[:, b, 0:256], ALU.mult))
                        tv = ve.do(TT(v, v, ps[:, b, 256:512], ALU.mult))
                        bank_free[b] = [tv]
                        tv = ve.do(TT(hid[:, u, f, :], v, cw, ALU.mult), t_cw)
                        cw_free[e_ % 4] = tv
                    done[e_] = tv
                if e_ >= 1:
                    q = e_ - 1
                    if q % 2 == 0:
                        dw = load(t_in["wdn"][l, q // 2])
                    dv = dw.ap.rearrange("p (j f n) -> p j f n", j=2, f=2)
                    fns = []
                    for t in range(2):
                        for h in range(2):
                            for f in range(2):
                                fns.append(mm(ps[:, 2 * t + h, :], hid[:, q % 2, f, 128 * t:128 * t + 128],
                                              dv[:, q % 2, f, 512 * h:512 * h + 512],
                                              q == 0 and f == 0, q == 15 and f == 1))
                    tp = pe.do(fns, dw.ready, done[q], acc_first if q == 0 else None)
                    dw.free = tp
                    hid_free[q % 2] = tp
                if e_ in extra:
                    extra[e_]()
            hT_free[:] = [tp]
            cT_free[:] = [tp]
            res = []
            for t in range(2):
                for h in range(2):
                    b = 2 * t + h
                    ve.do(TT(s1[:, 0:512], ps[:, b, :], grow[:, 1, 512 * h:512 * h + 512], ALU.mult), tp,
                          t_grow[(l, 1, h)], s1_free[:])
                    xs = x[:, t, 512 * h:512 * h + 512]
                    tt = ve.do(TT(xs, xs, s1[:, 0:512], ALU.add))
                    bank_free[b] = [tt]
                    res.append(tt)
            s1_free[:] = s2_free[:] = []
            return res

        cw_free = [None] * 4

        t_sc = cond_scale(0, 1, K("n2a", 0, 8), cadj[:, 3, :])
        th = norm_T(x, tx, cadj[:, 3, :], mcol[:, 16:24], t_sc)
        gate_bias(1, 0, gfree)
        extra = {e_: (lambda e_=e_: adaln(1, e_ - 2)) for e_ in range(2, 12)}
        tx = experts(0, th, extra)
        gate_bias(1, 1, tx[-1:])
        dump("x1", x, tx)
        for piece in (10, 11):
            adaln(1, piece)

        t_sc = cond_scale(1, 0, K("n1a", 8, 8), cadj[:, 3, :])
        th = norm_T(x, tx, cadj[:, 3, :], mcol[:, 32:40], t_sc)
        wv_ = load(t_in["wo_in"][1])
        for t in range(2):
            b, tp = proj_rows(wv_, 0, 512, hT, th, t)
            wv_.free = tp
            tv = ve.do(CP(z[:, t, 0:512], ps[:, b, :]), tp)
            bank_free[b] = [tv]
            ve.do(TT(s1[:, 512 * t:512 * t + 512], z[:, t, 0:512], z[:, t, 0:512], ALU.mult))
            tv = ve.do(lambda e, t=t: e.tensor_reduce(
                st[:, 8 + 4 * t:12 + 4 * t], s1[:, 512 * t:512 * t + 512].rearrange("p (g c) -> p g c", g=4),
                AX, ALU.add))
        tv = rstd(st[:, 16:24], st[:, 8:16], 1.0 / 128, st[:, 24:32], tv)
        for t in range(2):
            zg = z[:, t, 0:512].rearrange("p (g c) -> p g c", g=4)
            ve.do(TT(zg, zg, st[:, 16 + 4 * t:20 + 4 * t].unsqueeze(2).broadcast_to([P, 4, 128]), ALU.mult))
            tv = ve.do(TT(z[:, t, 0:512], z[:, t, 0:512], R("sgg"), ALU.mult), t_row)
        t_v = tv

        def cols_T(w, tiles, hs, t_h, evac):
            wv = w.ap.rearrange("p (k n) -> p k n", k=8)
            for j in range(0, tiles, 2):
                b = take("B")
                tp = pe.do([mm(ps[:, b, 256 * i:256 * i + 256], wv[:, k, 128 * (j + i):128 * (j + i) + 128],
                               hs[:, k, :], k == 0, k == 7) for i in range(2) for k in range(8)],
                           w.ready, t_h, bank_free[b])
                w.free = tp
                bank_free[b] = [evac(j, b, tp)]
            return tp

        uT = big[:, 0:1024].rearrange("p (g n) -> p g n", g=4)
        hxT = big[:, 1024:2048].rearrange("p (g n) -> p g n", g=4)
        bgT = big[:, 2048:3072].rearrange("p (g n) -> p g n", g=4)
        zT = big[:, 3072:3072 + 4 * 258].rearrange("p (g n) -> p g n", g=4)
        two = lambda a: a.rearrange("p (g n) -> p g n", g=2)
        t_pad = ve.do(lambda e: e.memset(big[:, 3072:3072 + 4 * 258], 0.0))
        for name, idx, dst in (("u", 0, uT), ("hx", 2, hxT), ("bg", 3, bgT)):
            w = load(t_in["wo_in"][idx])
            cols_T(w, 4, hT, th, lambda j, b, tp, dst=dst: ac.do(AC(dst[:, j:j + 2, :], two(ps[:, b, :])), tp, t_pad))
        w = load(t_in["wo_in"][4])
        tp = cols_T(w, 4, hT, th, lambda j, b, tp: ve.do(
            TT(zT[:, j:j + 2, 1:257], two(ps[:, b, :]), hxT[:, j:j + 2, :], ALU.mult), tp, ("ac", ac.n)))
        hT_free[:] = [tp]
        yt = []
        for g in range(4):
            b = take("B")
            tp = pe.do([mm(ps[:, b, 128 * t:128 * t + 128], z[:, t, 128 * g:128 * g + 128], K("sgw", 128 * g, 128),
                           True, True) for t in range(2)], t_v, t_col, bank_free[b])
            tv = ve.do(TT(yT[:, g, :].rearrange("p (t n) -> p t n", t=2),
                          ps[:, b, 0:256].rearrange("p (t n) -> p t n", t=2), bc(R("sgb", 128 * g, 128), 2),
                          ALU.add), tp, yT_free)
            bank_free[b] = [tv]
            yt.append(ve.do(TT(yT[:, g, :], yT[:, g, :], uT[:, g, :], ALU.mult), ("ac", ac.n)))
        for g in range(4):
            y = yT[:, 4 + g, :]
            ve.do(TS(y, zT[:, g, 0:256], K("cw", g, 1), None, ALU.mult))
            ve.do(STT(y, zT[:, g, 1:257], K("cw", 4 + g, 1), y, ALU.mult, ALU.add))
            ve.do(STT(y, zT[:, g, 2:258], K("cw", 8 + g, 1), y, ALU.mult, ALU.add))
            yt.append(ve.do(TT(y, y, bgT[:, g, :], ALU.mult)))
        dump("yT1", yT, yt)
        tx, tp = out_proj("wo_out", None, yT, yt, (1, 0))
        yT_free = [tp]
        dump("x2", x, tx)
        t_sc = cond_scale(1, 1, K("n2a", 8, 8), cadj[:, 3, :])
        th = norm_T(x, tx, cadj[:, 3, :], mcol[:, 48:56], t_sc)
        tx = experts(1, th, {})
        dump("x3", x, tx)

        T = [tab[:, 56 * i:56 * i + 56] for i in range(6)]
        t3 = lambda a: a.rearrange("p (t n) -> p t n", t=2)
        posf = st[:, 90:92]
        ve.do(CP(posf, posi[:, :]), t_pos)
        ve.do(TT(t3(T[0]), posf.unsqueeze(2).broadcast_to([P, 2, 28]), bc(C("inv"), 2), ALU.mult), t_cst)
        ve.do(TS(T[1], T[0], 1.0 / TWO_PI, None, ALU.mult))
        ve.do(TS(T[1], T[1], 12582912.0, None, ALU.add))
        ve.do(TS(T[1], T[1], 12582912.0, None, ALU.subtract))
        for part in (6.28125, 1.9350051879882812e-03, 3.0199159819567e-07):
            ve.do(STT(T[0], T[1], -part, T[0], ALU.mult, ALU.add))
        PI = 3.1415925
        ve.do(TS(T[2], T[0], 1.5707963267948966, None, ALU.add))
        ve.do(TS(T[3], T[2], PI, -TWO_PI, ALU.is_gt, ALU.mult))
        ve.do(TT(T[2], T[2], T[3], ALU.add))
        ve.do(TS(T[0], T[0], PI, -PI, ALU.min, ALU.max))
        tv = ve.do(TS(T[2], T[2], PI, -PI, ALU.min, ALU.max))
        ac.do(AC(T[4], T[2], ACT.Sin), tv)
        t_tab = ac.do(AC(T[5], T[0], ACT.Sin))
        cos, sin = t3(T[4]), t3(T[5])
        dump("tab", tab, t_tab)

        sgT = big[:, 0:8192].rearrange("p (g n) -> p g n", g=32)
        ar = sb("ar", 7400)
        off = [0]

        def area(n):
            a = off[0]
            off[0] += n
            return ar[:, a:a + n]

        nq = area(512).rearrange("p (i n) -> p i n", i=2)
        dq = area(512).rearrange("p (i n) -> p i n", i=2)
        kk = area(768).rearrange("p (i n) -> p i n", i=3)
        mq = area(1024).rearrange("p (h n) -> p h n", h=4)
        mk = area(1024).rearrange("p (h n) -> p h n", h=4)
        oTs = yT[:, :, :].rearrange("p k n -> p (k n)").rearrange("p (n i m) -> p n i m", n=4, i=2)
        pT2 = [area(1024).rearrange("p (h n) -> p h n", h=4), area(512).rearrange("p (h n) -> p h n", h=4)]
        cmpb = area(400)
        pbA = area(1536)
        lf = area(64)
        rp = sb("rp", 384)
        mixT = hT

        state = dict(ar=None)

        def rope(view, half, c0, tmp, toks):
            n = view.shape[2]
            c = cos[:, :, c0:c0 + half].unsqueeze(2).broadcast_to([P, 2, n, half])
            s = sin[:, :, c0:c0 + half].unsqueeze(2).broadcast_to([P, 2, n, half])
            m = 2 * n * half
            a, b = [tmp[:, m * i:m * i + m].rearrange("p (t h j) -> p t h j", t=2, h=n) for i in range(2)]
            x1, x2 = view[:, :, :, 0:half], view[:, :, :, half:2 * half]
            for t in range(2):
                ve.do(TT(a[:, t], x1[:, t], s[:, t], ALU.mult), toks, t_tab)
                ve.do(TT(b[:, t], x2[:, t], s[:, t], ALU.mult))
            for t in range(2):
                ve.do(TT(x1[:, t], x1[:, t], c[:, t], ALU.mult))
                ve.do(TT(x2[:, t], x2[:, t], c[:, t], ALU.mult))
            for t in range(2):
                ve.do(TT(x1[:, t], x1[:, t], b[:, t], ALU.subtract))
                tv = ve.do(TT(x2[:, t], x2[:, t], a[:, t], ALU.add))
            return tv

        def layer2(l, tx):
            th = norm_T(x, tx, K("n1b", 8 * l, 8), None, t_col)
            dump(f"h2_{l}", hT, th)
            zo = [0]
            for wd in ZW:
                zo.append(zo[-1] + wd)
            tz = []
            for i, wd in enumerate(ZW):
                w = load(t_in["wz"][l, :, 8 * zo[i]:8 * zo[i] + 8 * wd])
                for t in range(2):
                    b, tp = proj_rows(w, 0, wd, hT, th, t)
                    w.free = tp
                    o, i_ = z[:, t, zo[i]:zo[i] + wd], ps[:, b, 0:wd]
                    tt = ac.do(AC(o, i_), tp, z_free[:]) if i % 2 else ve.do(CP(o, i_), tp, z_free[:])
                    bank_free[b] = [tt]
                tz.append(tt)
            gates = []

            def gate_tiles():
                for d in range(8):
                    w = load(t_in["wgt"][l, d])
                    wv = w.ap.rearrange("p (k n) -> p k n", k=8)
                    for n in range(4):
                        b = take("B")
                        tp = pe.do([mm(ps[:, b, 0:256], wv[:, k, 128 * n:128 * n + 128], hT[:, k, :],
                                       k == 0, k == 7) for k in range(8)], w.ready, th, bank_free[b])
                        w.free = tp
                        g = sgT[:, 4 * d + n, :]
                        ta = ac.do(AC(g, ps[:, b, 0:256], ACT.Exp, scale=-1.0), tp, big_free[:])
                        bank_free[b] = [ta]
                        po.do(TS(g, g, 1.0, None, ALU.add), ta)
                        tv = ve.do(lambda e, g=g: e.reciprocal(g, g), ("po", po.n))
                        gates.append(tv)
                        last_gate[:] = [tp]
                        yield

            last_gate = []
            gen = gate_tiles()

            def fill(n):
                for _ in range(n):
                    next(gen, None)

            zi = z[:, :, 0:288].rearrange("p t (h d) -> p t h d", d=32)
            zr = z[:, :, 312:1080].rearrange("p t (h d) -> p t h d", d=64)
            Z = lambda t, a, n: z[:, t, a:a + n]
            SM = 288
            RQ, VV, ML, FQ, FV = 312, 1080, 1336, 1752, 2264
            tr_i = rope(zi, 4, 24, rp, tz[0])
            big3 = ar
            qiT = mq[:, 0:2, :]
            kiT = mq[:, 2, :]
            b = take("B")
            tp = pe.do([tr(ps[:, b, 256 * i + 128 * t:256 * i + 128 * t + 128], Z(t, 128 * i, 128))
                        for i in range(2) for t in range(2)], tr_i, bank_free[b])
            ta1 = ac.do(AC(mq[:, 0:2, :], ps[:, b, :].rearrange("p (i n) -> p i n", i=2)), tp, ar_free[:])
            bank_free[b] = [ta1]
            b = take("B")
            kd = s2[:, 0:256].rearrange("p (t n) -> p t n", t=2)
            for t in range(2):
                td = ve.do(CP(kd[:, t, :].rearrange("p (r d) -> p r d", r=4), bc(Z(t, 256, 32), 4)), s2_free[:])
            tp = pe.do([tr(ps[:, b, 128 * t:128 * t + 128], kd[:, t, :]) for t in range(2)], td, bank_free[b])
            s2_free[:] = [tp]
            ta2 = ac.do(AC(kiT, ps[:, b, 0:256]), tp)
            bank_free[b] = [ta2]
            wi = lf[:, 0:16].rearrange("p (t h) -> p t h", t=2)
            tw = ve.do(TS(wi, z[:, :, SM + 16:SM + 24], 8 ** -0.5, None, ALU.mult))
            sel = dict()
            dmask = dm[:, :].rearrange("p (t n) -> p t n", t=2)
            for t in range(2):
                nk = 128 * (t + 1)
                sc = s1[:, 256 * t:256 * t + nk]
                toks = []
                for j in range(4):
                    b = j
                    tp = pe.do([mm(ps[:, b, 256 * i:256 * i + nk], qiT[32 * j:32 * j + 32, i, 128 * t:128 * t + 128],
                                   kiT[32 * j:32 * j + 32, 0:nk], True, True) for i in range(2)],
                               ta1, ta2, bank_free[b])
                    toks.append(tp)
                for j in range(4):
                    for i in range(2):
                        h = 4 * i + j
                        r = s2[:, 256 * (h % 4):256 * (h % 4) + nk]
                        ta = ac.do(AC(r, ps[:, j, 256 * i:256 * i + nk], ACT.Relu, scale=32 ** -0.5), toks[j],
                                   s2_free[:], rfree[h % 4])
                        wcol = wi[:, t, h:h + 1]
                        if j == 0 and i == 0:
                            tv = ve.do(TS(sc, r, wcol, None, ALU.mult), ta, s1_free[:])
                        else:
                            tv = ve.do(STT(sc, r, wcol, sc, ALU.mult, ALU.add), ta)
                        rfree[h % 4] = tv
                    bank_free[j] = [ta]
                turn["A"] = 0
                if t == 0:
                    fill(2)
                mk_ = C("mask")[:, 256 - nk:256]
                ve.do(TT(sc, sc, mk_, ALU.add))
                wk = s1[:, 512 + 256 * t:512 + 256 * t + nk]
                m8 = lf[:, 16:24]
                src = sc
                for _ in range(8):
                    ve.do(lambda e, src=src, m8=m8: e.max(m8, src))
                    ve.do(lambda e, src=src, wk=wk, m8=m8: e.match_replace(wk, m8, src, -3e38))
                    src = wk
                ve.do(TS(wk, wk, -2e38, NEG, ALU.is_gt, ALU.mult))
                tv = ve.do(TT(dmask[:, t, 0:nk], wk, mk_, ALU.min), dm_free[:])
                if t == 0:
                    fill(2)
            s1_free[:] = []
            s2_free[:] = []
            t_sel = tv
            dump(f"dm{l}", dm, t_sel)

            tr_h = rope(zr[:, :, :, 0:16], 8, 16, rp, [tz[1], tz[2]])
            tr_m = rope(z[:, :, ML + 384:ML + 416].unsqueeze(2), 16, 0, rp, tz[3])
            toks = []
            for dst, c0 in ((nq[:, 0], 0), (nq[:, 1], 128), (dq[:, 0], 448), (dq[:, 1], 576)):
                b = take("B")
                tp = pe.do([tr(ps[:, b, 128 * t:128 * t + 128], Z(t, RQ + c0, 128)) for t in range(2)], tr_h,
                           bank_free[b])
                t_ = ac.do(AC(dst, ps[:, b, 0:256]), tp, ar_free[:])
                bank_free[b] = [t_]
            for i, c0 in enumerate((320, 384, 704)):
                b = take("B")
                k2 = s2[:, 0:256].rearrange("p (t n) -> p t n", t=2)
                for t in range(2):
                    td = po.do(CP(k2[:, t, :].rearrange("p (r d) -> p r d", r=2), bc(Z(t, RQ + c0, 64), 2)), tr_h,
                               s2_free[:], t_sel)
                tp = pe.do([tr(ps[:, b, 128 * t:128 * t + 128], k2[:, t, :]) for t in range(2)], td, bank_free[b])
                s2_free[:] = [tp]
                t_kk = ac.do(AC(kk[:, i], ps[:, b, 0:256]), tp)
                bank_free[b] = [t_kk]
            fill(2)
            wc = load(t_in["wcmp"][l], parts=64)
            wcv = wc.ap.rearrange("p (s m d) -> p s m d", s=2, m=32)
            b = take("B")
            tp = pe.do([tr(ps[0:64, b, 256 * s + 128 * t:256 * s + 128 * t + 128], Z(t, c0, 64))
                        for s, c0 in ((0, RQ + 256), (1, VV)) for t in range(2)], tr_h, tz[2], bank_free[b])
            kcT = s2[0:64, 512:1024]
            t_ = ac.do(AC(kcT, ps[0:64, b, :]), tp, s2_free[:])
            bank_free[b] = [t_]
            G = pbA[0:64, 0:1024].rearrange("p (s m c) -> p s m c", s=2, m=32)
            for s in range(2):
                src = kcT[:, 256 * s:256 * s + 256]
                for c in range(2):
                    nwin = 8 if c == 0 else 7
                    for hh in range(2):
                        base = 128 * c + 16 * hh
                        ap = src[:, base:base + 16 * nwin] if base + 16 * nwin <= 256 else None
                        tv = ve.do(CP(G[:, s, 16 * hh:16 * hh + 16, 8 * c:8 * c + nwin],
                                      ap.rearrange("p (w m) -> p m w", m=16)), t_, pb2_free[:])
                pe_ = K("pe", 64 * l + 32 * s, 32)[0:64, :]
                tv = ve.do(CP(G[:, s, :, 15], pe_))
            kvc = cmpb[0:64, 0:32].rearrange("p (s c) -> p s c", s=2)
            b = take("B")
            tp = pe.do([mm(ps[0:64, b, 16 * s:16 * s + 16], wcv[:, s, m, :], G[:, s, m, :], m == 0, m == 31)
                        for s in range(2) for m in range(32)], tv, wc.ready, bank_free[b])
            wc.free = tp
            pb2_free[:] = [tp]
            pc = ps[0:64, b, 0:32].rearrange("p (s c) -> p s c", s=2)
            kv_ = cmpb[0:64, 32:34]
            ve.do(CP(kv_, pc[:, :, 15]), tp, ar_free[:])
            for s in range(2):
                tv = ve.do(TS(kvc[:, s, 0:15], pc[:, s, 0:15], kv_[:, s:s + 1], None, ALU.add))
            bank_free[b] = [tv]
            kct = cmpb[:, 40:56]
            vct = cmpb[0:15, 64:128]
            b = take("B")
            dup = s2[0:64, 0:30]
            td = ve.do(CP(dup[:, 0:15], kvc[:, 0, 0:15]), s2_free[:])
            b2 = take("B")
            fns = [tr(ps[0:15, b, 0:64], kvc[:, 0, 0:15], 64), tr(ps[0:15, b, 64:128], kvc[:, 1, 0:15], 64)]
            tp = pe.do(fns, tv, bank_free[b])
            kr = cmpb[0:15, 128:256]
            ve.do(CP(kr[:, 0:64], ps[0:15, b, 0:64]), tp)
            ve.do(CP(kr[:, 64:128], ps[0:15, b, 0:64]))
            t_vc = ve.do(CP(vct, ps[0:15, b, 64:128]))
            bank_free[b] = [t_vc]
            tp = pe.do([tr(ps[:, b2, 0:15], kr, 15)], t_vc, bank_free[b2])
            t_kc = ve.do(CP(kct[:, 0:15], ps[:, b2, 0:15]), tp)
            bank_free[b2] = [t_kc]
            s2_free[:] = [t_kc]
            fill(2)
            sg = lf[:, 24:48].rearrange("p (t n) -> p t n", t=2)
            ta = ac.do(AC(sg, z[:, :, SM:SM + 12], ACT.Exp, scale=-1.0), tz[0])
            ve.do(TS(sg, sg, 1.0, None, ALU.add), ta)
            t_sg = ve.do(lambda e: e.reciprocal(sg, sg))

            def soft(pap, nh, n, scale, t_in_, gate, stc, mul=None):
                m = st[:, stc:stc + nh]
                sm = st[:, stc + 4:stc + 4 + nh]
                ve.do(lambda e: e.tensor_reduce(m, pap, AX, ALU.max), t_in_)
                tv = ve.do(TT(pap, pap, m.unsqueeze(2).broadcast_to([P, nh, n]), ALU.subtract))
                ta = ac.do(AC(pap, pap, ACT.Exp, scale=scale), tv)
                tv = ta
                if mul is not None:
                    tv = ve.do(TT(pap, pap, mul, ALU.mult), ta)
                ve.do(lambda e: e.tensor_reduce(sm, pap, AX, ALU.add), tv)
                if mul is not None:
                    ve.do(TS(sm, sm, 1e-30, None, ALU.max))
                ve.do(lambda e: e.reciprocal(sm, sm))
                if gate is not None:
                    ve.do(TT(sm, sm, gate, ALU.mult), t_sg)
                return ve.do(TT(pap, pap, sm.unsqueeze(2).broadcast_to([P, nh, n]), ALU.mult))

            def attend(q, k, pair, scale, mask, gate, toks, pT):
                for t in range(2):
                    n = 128 * (t + 1)
                    b = take2()
                    fns = []
                    for h in range(4):
                        o = ps[:, b + h % 2, n * (h // 2):n * (h // 2) + n]
                        fns.append(mm(o, q(h, t), k(h, n), True, True))
                    tp = pe.do(fns, toks, bank_free[b], bank_free[b + 1])
                    pap = pbA[:, 0:4 * n].rearrange("p (h n) -> p h n", h=4)
                    tm = None
                    for e2 in range(2):
                        o = pbA[:, 0:4 * n].rearrange("p (i e n) -> p i e n", e=2, n=n)[:, :, e2, :]
                        i_ = ps[:, b + e2, 0:2 * n].rearrange("p (i n) -> p i n", i=2)
                        tm = ve.do(TT(o, i_, bc(mask(t, n), 2), ALU.add), tp, pb2_free[:])
                        bank_free[b + e2] = [tm]
                    g = None if gate is None else gate[:, t, :]
                    tv = soft(pap, 4, n, scale, tm, g, 80)
                    for kt in range(t + 1):
                        bb = take("B")
                        tp = pe.do([tr(ps[:, bb, 128 * h:128 * h + 128], pap[:, h, 128 * kt:128 * kt + 128])
                                    for h in range(4)], tv, bank_free[bb])
                        pb2_free[:] = [tp]
                        dst = pT[0][:, :, 128 * t:128 * t + 128] if kt == 0 else pT[1][:, :, :]
                        t_ = ac.do(AC(dst, ps[:, bb, :].rearrange("p (h n) -> p h n", h=4)), tp, pT_free2[:])
                        bank_free[bb] = [t_]
                    fill(2)
                return t_

            def values(n, paths, toks):
                b = take("B")
                fns = []
                for h in range(4):
                    lo = 64 * (h % 2)
                    c0 = 256 * (h // 2)
                    ops = paths(h)
                    for i, (l_, r_, q0) in enumerate(ops):
                        fns.append(mm(ps[lo:lo + 64, b, c0 + q0:c0 + 256], l_, r_, i == 0, i == len(ops) - 1))
                tp = pe.do(fns, toks, bank_free[b])
                pT_free2[:] = [tp]
                t_ = ve.do(CP(oTs[:, n], ps[:, b, :].rearrange("p (i m) -> p i m", i=2)), tp, oTs_free[:])
                bank_free[b] = [t_]
                return t_

            causal = lambda t, n: C("mask")[:, 256 - n:256]
            HB = lambda ap, h: ap[64 * (h % 2):64 * (h % 2) + 64]

            tdp = attend(lambda h, t: HB(dq, h)[:, h // 2, 128 * t:128 * t + 128], lambda h, n: HB(kk, h)[:, 2, 0:n],
                         True, 0.125, lambda t, n: dmask[:, t, 0:n], None, [t_kk, t_sel], pT2)
            to = [values(3, lambda h: [(Z(0, VV + 192, 64), pT2[0][:, h, :], 0), (Z(1, VV + 192, 64), pT2[1][:, h, :], 128)],
                         tdp)]
            dm_free[:] = [("ve", ve.n)]
            b = take2()
            pcp = cmpb[:, 256:376].rearrange("p (t h c) -> p t h c", t=2, h=4)
            tp = pe.do([mm(ps[:, b + h % 2, 32 * t + 16 * (h // 2):32 * t + 16 * (h // 2) + 15],
                           HB(nq, h)[:, h // 2, 128 * t:128 * t + 128], HB(kct, h)[:, 0:15], True, True)
                        for t in range(2) for h in range(4)], t_kc, t_kk, bank_free[b], bank_free[b + 1])
            ca, cm = C("cadd"), C("cmul")
            for t in range(2):
                for e2 in range(2):
                    i_ = ps[:, b + e2, 32 * t:32 * t + 32].rearrange("p (i c) -> p i c", i=2)[:, :, 0:15]
                    o = pcp[:, t].rearrange("p (i e) c -> p i e c", e=2)[:, :, e2, :]
                    tm = ve.do(TT(o, i_, bc(ca[:, 15 * t:15 * t + 15], 2), ALU.add), tp)
            bank_free[b] = [tm]
            bank_free[b + 1] = [tm]
            for t in range(2):
                tv = soft(pcp[:, t], 4, 15, 0.125, tm, sg[:, t, 0:4], 80, bc(cm[:, 15 * t:15 * t + 15], 4))
            pcT = cmb[0:15, :].rearrange("p (h n) -> p h n", h=4)
            for t in range(2):
                bb = take("B")
                tp = pe.do([tr(ps[0:15, bb, 128 * h:128 * h + 128], pcp[:, t, h, :]) for h in range(4)], tv,
                           bank_free[bb])
                t_c = ac.do(AC(pcT[:, :, 128 * t:128 * t + 128],
                               ps[0:15, bb, :].rearrange("p (h n) -> p h n", h=4)), tp, oTs_free[:])
                bank_free[bb] = [t_c]
            tsel = attend(lambda h, t: HB(nq, h)[:, h // 2, 128 * t:128 * t + 128], lambda h, n: HB(kk, h)[:, 0, 0:n],
                          True, 0.125, causal, sg[:, :, 4:8], t_kk, pT2)
            twin = attend(lambda h, t: HB(nq, h)[:, h // 2, 128 * t:128 * t + 128], lambda h, n: HB(kk, h)[:, 1, 0:n],
                          True, 0.125, causal, sg[:, :, 8:12], t_kk, pT3)
            to.append(values(1, lambda h: [
                (vct, pcT[:, h, :], 0),
                (Z(0, VV + 64, 64), pT2[0][:, h, :], 0), (Z(1, VV + 64, 64), pT2[1][:, h, :], 128),
                (Z(0, VV + 128, 64), pT3[0][:, h, :], 0), (Z(1, VV + 128, 64), pT3[1][:, h, :], 128)],
                [t_vc, t_c, tsel, twin]))
            wm = load(t_in["wmla"][l])
            st_q = 8
            for t in range(2):
                ve.do(TT(s1[:, 0:384], Z(t, ML, 384), Z(t, ML, 384), ALU.mult), tz[3])
                ve.do(lambda e, t=t: e.tensor_reduce(st[:, 8 + 2 * t:9 + 2 * t], s1[:, 0:256], AX, ALU.add))
                tv = ve.do(lambda e, t=t: e.tensor_reduce(st[:, 9 + 2 * t:10 + 2 * t], s1[:, 256:384], AX, ALU.add))
                tv = ve.do(TS(st[:, 9 + 2 * t:10 + 2 * t], st[:, 9 + 2 * t:10 + 2 * t], 2.0, None, ALU.mult))
            tv = rstd(st[:, 12:16], st[:, 8:12], 1.0 / 256, st[:, 16:20], tv)
            for t in range(2):
                ve.do(TS(Z(t, ML, 256), Z(t, ML, 256), st[:, 12 + 2 * t:13 + 2 * t], None, ALU.mult))
                tv = ve.do(TS(Z(t, ML + 256, 128), Z(t, ML + 256, 128), st[:, 13 + 2 * t:14 + 2 * t], None, ALU.mult))
            cT_ = s2[:, 0:768].rearrange("p (i n) -> p i n", i=3)
            for i in range(3):
                b = take("B")
                tp = pe.do([tr(ps[:, b, 128 * t:128 * t + 128], Z(t, ML + 128 * i, 128)) for t in range(2)], tv,
                           bank_free[b])
                g = K("gq", 2 * l + i, 1) if i < 2 else K("gkv", l, 1)
                t_ = ac.do(AC(cT_[:, i, :], ps[:, b, 0:256], scale=g), tp, s2_free[:])
                bank_free[b] = [t_]
            fill(2)
            mz = mzb[:, :].rearrange("p (t n) -> p t n", t=2)
            for t in range(2):
                b = take("B")
                tp = pe.do([mm(ps[:, b, 0:384], cT_[:, k, 128 * t:128 * t + 128], wm.ap[:, 384 * k:384 * k + 384],
                               k == 0, k == 1) for k in range(2)], t_, wm.ready, bank_free[b])
                tq_ = ve.do(CP(mz[:, t, 0:384], ps[:, b, 0:384]), tp, mz_free[:])
                bank_free[b] = [tq_]
                b = take("B")
                tp = pe.do([mm(ps[:, b, :], cT_[:, 2, 128 * t:128 * t + 128], wm.ap[:, 768:1280], True, True)],
                           bank_free[b])
                wm.free = tp
                pv = ps[:, b, :].rearrange("p (h n) -> p h n", h=4)
                k4 = mz[:, t, 384:768].rearrange("p (h n) -> p h n", h=4)
                ve.do(CP(k4[:, :, 0:64], pv[:, :, 0:64]), tp)
                tv = ve.do(CP(mz[:, t, 768:1024].rearrange("p (h n) -> p h n", h=4), pv[:, :, 64:128]))
                bank_free[b] = [tv]
                tv = ve.do(CP(k4[:, :, 64:96], bc(Z(t, ML + 384, 32), 4)))
            s2_free[:] = [tp]
            mqv = mz[:, :, 0:384].rearrange("p t (h n) -> p t h n", h=4)
            tv = rope(mqv[:, :, :, 64:96], 16, 0, rp, None)
            for dst, c0 in ((mq, 0), (mk, 384)):
                for hp in range(2):
                    b = take("B")
                    tp = pe.do([tr(ps[0:96, b, 256 * i + 128 * t:256 * i + 128 * t + 128],
                                   mz[:, t, c0 + 96 * (2 * hp + i):c0 + 96 * (2 * hp + i) + 96])
                                for i in range(2) for t in range(2)], tv, bank_free[b])
                    t_mk = ac.do(AC(dst[0:96, 2 * hp:2 * hp + 2, :],
                                    ps[0:96, b, :].rearrange("p (i n) -> p i n", i=2)), tp)
                    bank_free[b] = [t_mk]
            tmp_ = attend(lambda h, t: mq[0:96, h, 128 * t:128 * t + 128], lambda h, n: mk[0:96, h, 0:n],
                          False, 96 ** -0.5, causal, None, t_mk, pT2)
            to.append(values(0, lambda h: [(mz[:, 0, 768 + 64 * h:832 + 64 * h], pT2[0][:, h, :], 0),
                                           (mz[:, 1, 768 + 64 * h:832 + 64 * h], pT2[1][:, h, :], 128)], tmp_))
            tmla = to[-1]
            f = lf[:, 48:56].rearrange("p (t n) -> p t n", t=2)
            g_ = lf[:, 56:64].rearrange("p (t n) -> p t n", t=2)
            ve.do(TT(f, z[:, :, SM + 12:SM + 16], bc(R("fb", 4 * l, 4), 2), ALU.add), t_row)
            tv = ve.do(STT(g_, f, -1.0, f, ALU.mult, ALU.min))
            ta = ac.do(AC(g_, g_, ACT.Exp), tv)
            ta = ac.do(AC(g_, g_, ACT.Ln, bias=1.0))
            tv = ve.do(STT(f, f, 0.0, g_, ALU.min, ALU.subtract), ta)
            b = take("B")
            tp = pe.do([mm(ps[:, b, 0:4], C("tri"), f[:, 0, :], True, True),
                        mm(ps[:, b, 8:12], C("ones"), f[:, 0, :], True, False),
                        mm(ps[:, b, 8:12], C("tri"), f[:, 1, :], False, True)], tv, bank_free[b])
            fz = mzb[:, 0:1056].rearrange("p (t s h n) -> p t s h n", t=2, s=2, h=4)
            for t in range(2):
                zq = Z(t, FQ, 256).rearrange("p (h n) -> p h n", h=4)
                zk = Z(t, FQ + 256, 256).rearrange("p (h n) -> p h n", h=4)
                cc = ps[:, b, 8 * t:8 * t + 4]
                ve.do(TS(fz[:, t, 0, :, 0:64], zq, 0.125, None, ALU.mult), tp, tmla, tz[4])
                ve.do(CP(fz[:, t, 1, :, 0:64], zk))
                ve.do(CP(fz[:, t, 0, :, 64], cc))
                ve.do(TS(fz[:, t, 1, :, 65], cc, -1.0, None, ALU.mult))
                ve.do(lambda e, t=t: e.memset(fz[:, t, 0, :, 65:66], 1.0))
                tv = ve.do(lambda e, t=t: e.memset(fz[:, t, 1, :, 64:65], 1.0))
            bank_free[b] = [tv]
            for s, dst in ((0, mq), (1, mk)):
                for hp in range(2):
                    b = take("B")
                    tp = pe.do([tr(ps[0:66, b, 256 * i + 128 * t:256 * i + 128 * t + 128], fz[:, t, s, 2 * hp + i, :])
                                for i in range(2) for t in range(2)], tv, bank_free[b])
                    t_fk = ac.do(AC(dst[0:66, 2 * hp:2 * hp + 2, :],
                                    ps[0:66, b, :].rearrange("p (i n) -> p i n", i=2)), tp)
                    bank_free[b] = [t_fk]
            mz_free[:] = [tp]
            tfp = attend(lambda h, t: mq[0:66, h, 128 * t:128 * t + 128], lambda h, n: mk[0:66, h, 0:n],
                         False, 1.0, causal, None, t_fk, pT2)
            to.append(values(2, lambda h: [(Z(0, FV + 64 * h, 64), pT2[0][:, h, :], 0),
                                           (Z(1, FV + 64 * h, 64), pT2[1][:, h, :], 128)], [tfp, tz[5]]))
            dump(f"oT{l}", oTs, to)
            ar_free[:] = [tp]
            z_free[:] = [pT_free2[0]]
            fill(40)
            wb = [load(t_in["wbr"][l, i]) for i in range(2)]
            wbv = [w.ap.rearrange("p (n k d) -> p n k d", n=2, k=2) for w in wb]
            tm = []
            for d in range(8):
                for n2 in range(2):
                    b = take("B")
                    tp = pe.do([mm(ps[:, b, 256 * i:256 * i + 256], wbv[n2][:, i, k, 128 * d:128 * d + 128],
                                   oTs[:, 2 * n2 + i, k, :], k == 0, k == 1) for i in range(2) for k in range(2)],
                               [w.ready for w in wb], to, bank_free[b])
                    wb[0].free = wb[1].free = tp
                    g2 = sgT[:, 4 * d + 2 * n2:4 * d + 2 * n2 + 2, :]
                    tv = ve.do(TT(g2, g2, two(ps[:, b, :]), ALU.mult), tp, gates)
                    bank_free[b] = [tv]
                g4 = sgT[:, 4 * d:4 * d + 4, :]
                tv = po.do(TT(g4[:, 0:2, :], g4[:, 0:2, :], g4[:, 2:4, :], ALU.add), tv)
                tm.append(po.do(TT(mixT[:, d, :], g4[:, 0, :], g4[:, 1, :], ALU.add), last_gate[:]))
            oTs_free[:] = [tp]
            dump(f"mix{l}", mixT, tm)
            tx, tp = out_proj("wout", l, mixT, tm, None)
            hT_free[:] = [tp]
            dump(f"xa{l}", x, tx)
            th = norm_T(x, tx, K("n2b", 8 * l, 8), None, t_col)
            tf = []
            for c in range(8):
                w = load(t_in["wup"][l, c])

                def evac(j, b, tp, c=c):
                    r = s2[:, 512 * (j // 2 % 2):512 * (j // 2 % 2) + 512]
                    ta = ac.do(AC(r, ps[:, b, :], ACT.Relu), tp, s2_free[:], rf2[j // 2 % 2])
                    o = sgT[:, 4 * c + j:4 * c + j + 2, :]
                    tv = ve.do(TT(o, two(r), two(r), ALU.mult), ta, tm)
                    rf2[j // 2 % 2] = tv
                    tf.append(tv)
                    return ta

                tp = cols_T(w, 4, hT, th, evac)
            hT_free[:] = [tp]
            for c in range(8):
                w = load(t_in["wdown"][l, c])
                wv = w.ap.rearrange("p (k n) -> p k n", k=4)
                fns = []
                for k in range(4):
                    for t in range(2):
                        for h in range(2):
                            fns.append(mm(ps[:, 2 * t + h, :], sgT[:, 4 * c + k, 128 * t:128 * t + 128],
                                          wv[:, k, 512 * h:512 * h + 512], c == 0 and k == 0, c == 7 and k == 3))
                tp = pe.do(fns, w.ready, tf[2 * c:2 * c + 2],
                           [bank_free[b] for b in range(4)] if c == 0 else None)
                w.free = tp
            big_free[:] = [tp]
            res = []
            for t in range(2):
                for h in range(2):
                    xs = x[:, t, 512 * h:512 * h + 512]
                    tt = ve.do(TT(xs, xs, ps[:, 2 * t + h, :], ALU.add), tp)
                    bank_free[2 * t + h] = [tt]
                    res.append(tt)
            s2_free[:] = []
            dump(f"xb{l}", x, res)
            return res

        dm = sb("dm", 512)
        cmb = acc[:, :, :].rearrange("p a n -> p (a n)")
        gr = grow[:, :, :].rearrange("p a n -> p (a n)")
        pT3 = [gr[:, 0:1024].rearrange("p (h n) -> p h n", h=4), gr[:, 1024:1536].rearrange("p (h n) -> p h n", h=4)]
        mzb = xn[:, :, :].rearrange("p t n -> p (t n)")
        dm_free, mz_free, ar_free, z_free, pb2_free, pT_free2, oTs_free = [], [], [], [], [], [], []
        big_free = [] if not tx else [tx[-1]]
        yTf = list(yT_free)
        rf2 = [None, None]
        rfree = [None] * 4

        tx = layer2(0, tx)
        tx = layer2(1, tx)

        ndma += 1
        t_fg = sp.dma(lambda e: e.dma_start(grow[:, 0, :], t_in["rowp"][0:1, 1712:2736].broadcast_to([P, 1024])),
                      f"d{ndma}", 16, pT_free2[:])
        norm_rows(x, tx, None)
        outs = []
        for t in range(2):
            tv = ve.do(TT(xn[:, t, :], xn[:, t, :], grow[:, 0, :], ALU.mult), ("ac", ac.n), t_fg)
            outs.append(sp.dma(lambda e, t=t: e.dma_start(out[:, t, :], xn[:, t, :]), "out", 16 * (t + 1), tv))

        sems = {k: ctx.enter_context(nc.semaphore(f"s_{k}")) for k in
                ["pe", "ac", "ve", "po", "out", *[f"w{i}" for i in range(NRING)],
                 *[f"d{i + 1}" for i in range(ndma)], *(["dbg"] if dbg else [])]}
        block = ctx.enter_context(nc.Block())

        @block.sync
        def _(e):
            replay(sp, e, sems)
            e.wait_ge(sems["out"], 32)
            if dbg:
                e.wait_ge(sems["dbg"], 16 * dbg.n)

        @block.tensor
        def _(e):
            replay(pe, e, sems)

        @block.scalar
        def _(e):
            replay(ac, e, sems)

        @block.vector
        def _(e):
            replay(ve, e, sems)

        @block.gpsimd
        def _(e):
            replay(po, e, sems)


def constants(np):
    f = np.float32
    c = np.zeros((P, NCST), f)

    def put(name, v):
        a, n = CST[name]
        c[:, a:a + n] = v

    i = np.arange(P)
    put("ident", np.eye(P))
    put("ones", 1.0)
    put("tri", i[:, None] <= i[None, :])
    put("mask", np.concatenate([np.zeros((P, P)), np.where(i[None, :] <= i[:, None], 0.0, NEG)], 1))
    tok = np.arange(256).reshape(2, P).T
    ok = (16 * np.arange(15) + 31)[None, None, :] <= tok[:, :, None]
    put("cadd", np.where(ok, 0.0, NEG).reshape(P, 30))
    put("cmul", ok.reshape(P, 30))
    inv = (f(10000.0) ** (-np.arange(0, 32, 2, dtype=f) / f(32))).astype(f)
    ra = (tok // 64).astype(f)[:, :, None] * inv
    ca = (tok % 64).astype(f)[:, :, None] * inv
    put("ropc", np.cos(np.concatenate([ra, ra, ca, ca], 2)).reshape(P, 128))
    put("rops", np.concatenate([-np.sin(ra), np.sin(ra), -np.sin(ca), np.sin(ca)], 2).reshape(P, 128))
    put("inv", np.concatenate([(f(500000.0) ** (-np.arange(0, r, 2, dtype=f) / f(r))).astype(f)
                               for r in (32, 16, 8)]))
    pm = np.zeros((256, 4, 256), f)
    for g, w in enumerate((2, 4, 8, 16)):
        for t in range(256):
            lo, hi = max(t - w // 2, 0), min(t + w - w // 2, 256)
            pm[lo:hi, g, t] = f(1.0) / f(hi - lo)
            pm[t, g, t] -= f(1.0)
    return c, pm.reshape(2, P, 4, 256).transpose(1, 0, 2, 3).reshape(P, 2048)


def layout(np, i):
    def rows(w, n):
        k, m = w.shape[-2] // P, w.shape[-1] // n
        lead = w.shape[:-2]
        w = w.reshape(*lead, k, P, m, n)
        r = len(lead)
        return np.ascontiguousarray(np.transpose(w, (*range(r), r + 2, r + 1, r, r + 3)).reshape(*lead, m, P, k * n))

    def cols(v):
        return v.reshape(-1, P).T

    a = {k: np.asarray(v) for k, v in i.items()}
    d = {}
    c, pm = constants(np)
    d["cst"], d["pm"] = c, pm
    colp = np.zeros((P, NCOL), np.float32)

    def put(name, v):
        b, n = COL[name]
        colp[:v.shape[0], b:b + n] = v

    put("n1a", cols(a["norm1_g"]))
    put("n2a", cols(a["norm2_g"]))
    put("n1b", cols(a["norm1_g_2"]))
    put("n2b", cols(a["norm2_g_2"]))
    put("modb", cols(a["mod_b"]))
    put("c", cols(a["c"]))
    put("cc", cols(a["c_ctx"]))
    put("ps", cols(a["pool_scale"]))
    put("cw", cols(a["conv_w"]))
    put("sgw", a["sg_w"][0].transpose(2, 0, 1).reshape(P, 512))
    put("plw", a["pool_w"][0].transpose(1, 0, 2).reshape(P, 512))
    r = np.concatenate([a["router_g_w"], a["router_e_w"]], 2)
    put("rw", r.reshape(2, 8, P, 20).transpose(2, 0, 1, 3).reshape(P, 320))
    put("gq", cols(a["mla_q_norm_g_2"]))
    put("gkv", cols(a["mla_kv_norm_g_2"]))
    put("pe", a["nsa_cmp_pe_2"].transpose(3, 0, 1, 2).reshape(64, 128))
    d["colp"] = colp
    kg = a["k_gain"].reshape(-1)
    qg = a["q_gain"].reshape(-1)
    gb = a["mod_b"].reshape(2, 6, 1024)[:, [2, 5], :].reshape(-1)
    rb = np.concatenate([a["router_g_b"], a["router_e_b"]], 1).reshape(-1)
    d["rowp"] = np.concatenate([np.tile(qg, 8), np.tile(kg, 2), a["sg_gain"].reshape(-1), a["sg_b"].reshape(-1),
                                rb, a["fox_f_bias_2"].reshape(-1), a["final_g_2"], gb]).reshape(1, NROW)
    d["x"] = np.ascontiguousarray(a["x"].reshape(2, P, 1024).transpose(1, 0, 2))
    d["ctx"] = np.ascontiguousarray(a["ctx"].reshape(2, P, 1024).transpose(1, 0, 2))
    d["pos"] = np.ascontiguousarray(a["positions_2"].reshape(2, P).T)
    d["wmod"] = rows(a["mod_w"], 512)
    w = a["even_w_in"][0]
    q = w[:, 0:512].reshape(1024, 2, 4, 64).transpose(0, 2, 1, 3).reshape(1024, 512)
    d["we_q"] = rows(q, 512)[0]
    d["we_kv"] = rows(w[:, 512:768], 256)[0]
    d["we_p"] = rows(w[:, 768:1280], 512)[0]
    w = a["even_w_out"][0]
    w = np.concatenate([w[0:512].reshape(2, 4, 64, 1024).transpose(1, 0, 2, 3).reshape(512, 1024), w[512:]], 0)
    d["we_out"] = rows(w, 512)
    d["wo_in"] = rows(a["odd_w_in"][0], 512)
    d["wo_out"] = rows(a["odd_w_out"][0], 512)
    gu = np.stack([a["w_gate"], a["w_up"]], 2)
    d["wgu"] = np.ascontiguousarray(gu.reshape(2, 16, 2, 8, P, 256).transpose(0, 1, 4, 2, 3, 5)).reshape(2, 16, P, 4096)
    d["wdn"] = np.ascontiguousarray(a["w_down"].reshape(2, 8, 2, 2, P, 1024).transpose(0, 1, 4, 2, 3, 5)
                                    ).reshape(2, 8, P, 4096)
    w = a["w_in_2"]
    m, n, f, s = 0, 416, 1068, 1840
    order = [(s + 384, 288), (n + 640, 12), (f + 768, 4), (s + 672, 8),
             (n, 256), (n + 256, 64), (n + 384, 64), (n + 512, 64), (s, 256), (s + 256, 64),
             (n + 320, 64), (n + 448, 64), (n + 576, 64), (s + 320, 64),
             (m, 416), (f, 512), (f + 512, 256)]
    zw = np.concatenate([w[:, :, b:b + k] for b, k in order], 2)
    parts, b = [], 0
    for k in ZW:
        parts.append(zw[:, :, b:b + k].reshape(2, 8, P, k).transpose(0, 2, 1, 3).reshape(2, P, 8 * k))
        b += k
    d["wz"] = np.concatenate(parts, 2)
    g = w[:, :, 2520:].reshape(2, 8, P, 4, 8, P)
    d["wgt"] = np.ascontiguousarray(g.transpose(0, 4, 2, 1, 3, 5)).reshape(2, 8, P, 4096)
    d["wmla"] = np.concatenate([a["mla_w_uq_2"].reshape(2, 2, P, 384).transpose(0, 2, 1, 3).reshape(2, P, 768),
                                a["mla_w_ukv_2"]], 2)
    d["wcmp"] = np.ascontiguousarray(a["nsa_cmp_w_2"].reshape(2, 2, 32, 64, 64).transpose(0, 3, 1, 2, 4)
                                     ).reshape(2, 64, 4096)
    d["wbr"] = np.ascontiguousarray(a["w_branch_2"].reshape(2, 2, 2, 2, P, 1024).transpose(0, 1, 4, 2, 3, 5)
                                    ).reshape(2, 2, P, 4096)
    d["wout"] = rows(a["w_out_2"], 512)
    d["wup"] = rows(a["w_up_2"], 512)
    d["wdown"] = np.ascontiguousarray(a["w_down_2"].reshape(2, 8, 4, P, 1024).transpose(0, 1, 3, 2, 4)
                                      ).reshape(2, 8, P, 4096)
    return d


def kernel(**inputs):
    import numpy as np
    from concourse import bacc
    from concourse.bass_utils import run_bass_kernel_spmd

    arrays = layout(np, inputs)
    nc = bacc.Bacc("TRN2", target_bir_lowering=False, num_devices=1)
    t_in = {k: nc.dram_tensor(f"in_{k}", v.shape, mybir.dt.from_np(v.dtype), kind="ExternalInput").ap()
            for k, v in arrays.items()}
    out = nc.dram_tensor("out_x", (P, 2, 1024), F32, kind="ExternalOutput").ap()
    build(nc, t_in, out)
    r = run_bass_kernel_spmd(nc, [{f"in_{k}": v for k, v in arrays.items()}], core_ids=[0])
    y = r.results[0]["out_x"]
    return y.transpose(1, 0, 2).reshape(1, 256, 1024)
```

```python
from contextlib import ExitStack

from concourse import mybir
from concourse.alu_op_type import AluOpType as ALU

F32 = mybir.dt.float32
I32 = mybir.dt.int32
ACT = mybir.ActivationFunctionType
AX = mybir.AxisListType.X
P = 128
EPS = 1e-6
NEG = -1e30
TWO_PI = 6.283185307179586
PIECE = 2048
NRAW = 4
NHL = 3
F32R = mybir.dt.float32r
ZW = (312, 512, 512, 416, 512, 256)

CST = dict(ident=(0, 128), ones=(128, 128), tri=(256, 128), mask=(384, 256), cadd=(640, 30),
           cmul=(670, 30), ropc=(700, 128), rops=(828, 128), inv=(956, 28))
NCST = 984
COL = dict(n1a=(0, 16), n2a=(16, 16), n1b=(32, 16), n2b=(48, 16), modb=(64, 96), c=(160, 8),
           cc=(168, 8), ps=(176, 4), cw=(180, 12), sgw=(192, 512), plw=(704, 512),
           rw=(1216, 320), gq=(1536, 4), gkv=(1540, 2), pe=(1542, 128))
NCOL = 1670
ROW = dict(qkg=(0, 640), sgg=(640, 512), sgb=(1152, 512), rb=(1664, 40), fb=(1704, 8),
           fg=(1712, 1024), gb=(2736, 4096))
NROW = 6832
RKEEP = 1712


class Engine:

    def __init__(self, key, chained):
        self.key, self.chained, self.n, self.queue = key, chained, 0, []

    def do(self, fns, *after):
        fns = fns if isinstance(fns, list) else [fns]
        if self.chained and self.n:
            after = (*after, (self.key, self.n))
        self.n += 1
        self.queue.append((after, fns, self.key, 1))
        return (self.key, self.n)

    def dma(self, fn, key, count, *after):
        self.queue.append((after, [fn], key, 16))
        return (key, count)


def tokens(after):
    for t in after:
        if t is None:
            continue
        if callable(t):
            yield from tokens([t()])
        elif isinstance(t, list):
            yield from tokens(t)
        else:
            yield t


def replay(engine, unit, sems):
    seen = {}
    for after, fns, key, inc in engine.queue:
        need = {}
        for k, v in tokens(after):
            need[k] = max(need.get(k, 0), v)
        for k, v in need.items():
            if seen.get(k, 0) < v:
                unit.wait_ge(sems[k], v)
                seen[k] = v
        for fn in fns:
            ins = fn(unit)
        ins.then_inc(sems[key], inc)


class Chunk:
    pass


def build(nc, t_in, out, dbg=None):
    with ExitStack() as ctx:
        base = nc.sbuf_base + (-nc.sbuf_base) % 64
        arena = ctx.enter_context(nc.sbuf_tensor("arena", [P, 52500], F32))
        del arena
        where = [base]

        def at(name, off, *shape, dt=F32, parts=P):
            return nc.alloc_sbuf_tensor_at(name, [parts, *shape], dt, offset=off)

        def sb(name, *shape, dt=F32, parts=P):
            n = 1
            for d in shape:
                n *= d
            off = where[0]
            where[0] += 4 * n + (-4 * n) % 32
            return at(name, off, *shape, dt=dt, parts=parts)

        S = {}
        S["cst"] = sb("cst", NCST)
        S["col"] = sb("col", NCOL)
        S["row"] = sb("row", RKEEP)
        S["mcol"] = sb("mcol", 64)
        S["sil"] = sb("sil", 16)
        S["st"] = sb("st", 160)
        S["cadj"] = sb("cadj", 4, 8)
        S["rt"] = sb("rt", 400)
        S["lf"] = sb("lf", 64)
        S["posi"] = sb("posi", 2, dt=I32)
        S["tab16"] = sb("tab16", 256, parts=16)
        S["x"] = sb("x", 2, 1024)
        S["xn"] = sb("xn", 2, 1024)
        S["s1"] = sb("s1", 1024)
        S["s2"] = sb("s2", 1024)
        S["grow"] = sb("grow", 2, 1024)
        S["acc"] = sb("acc", 2, 512)
        S["hT"] = sb("hT", 8, 256)
        S["raw"] = [sb(f"raw{i}", PIECE) for i in range(NRAW)]
        hl = where[0]
        S["hi"], S["lo"] = [], []
        for i in range(NHL):
            S["hi"].append(sb(f"hi{i}", PIECE, dt=F32R))
            S["lo"].append(sb(f"lo{i}", PIECE, dt=F32R))
        S["hTh"] = sb("hTh", 8, 256, dt=F32R)
        S["hTl"] = sb("hTl", 8, 256, dt=F32R)
        ye = where[0]
        S["yTh"] = sb("yTh", 8, 256, dt=F32R)
        S["yTl"] = sb("yTl", 8, 256, dt=F32R)
        ze = where[0]
        S["z"] = sb("z", 2, 2520)
        S["big"] = at("big", hl, 8192)
        S["ar"] = at("ar", hl + 4 * 8192, 8192)
        S["oTs"] = at("oTs", ye, 2048)
        S["yf"] = at("yf", ze, 2048)
        S["hidh"] = at("hidh", ze, 2, 2, 256, dt=F32R)
        S["hidl"] = at("hidl", ze + 4096, 2, 2, 256, dt=F32R)
        S["ex"] = at("ex", ze + 8192, 2048)
        S["fTh"] = at("fTh", ze, 2, 4, 256, dt=F32R)
        S["fTl"] = at("fTl", ze + 8192, 2, 4, 256, dt=F32R)
        assert where[0] <= base + 4 * 52500
        S["ps"] = ctx.enter_context(nc.psum_tensor("ps", [P, 8, 512], F32))

        plan = emit(S, t_in, out, None, None)[0]
        _, engines, ndma = emit(S, t_in, out, plan, dbg)
        sems = {k: ctx.enter_context(nc.semaphore(f"s_{k}")) for k in
                ["pe", "ac", "ve", "po", "out", *[f"w{i}" for i in range(NRAW)],
                 *[f"d{i + 1}" for i in range(ndma)], *(["dbg"] if dbg else [])]}
        block = ctx.enter_context(nc.Block())

        @block.sync
        def _(e):
            replay(engines["sp"], e, sems)
            e.wait_ge(sems["out"], 32)
            if dbg:
                e.wait_ge(sems["dbg"], 16 * dbg.n)

        @block.tensor
        def _(e):
            replay(engines["pe"], e, sems)

        @block.scalar
        def _(e):
            replay(engines["ac"], e, sems)

        @block.vector
        def _(e):
            replay(engines["ve"], e, sems)

        @block.gpsimd
        def _(e):
            replay(engines["po"], e, sems)


def emit(S, t_in, out, plan, dbg):
    pe, ac, ve, po, sp = (Engine("pe", False), Engine("ac", True), Engine("ve", True),
                          Engine("po", True), Engine("sp", False))
    cst, col, row, mcol, sil, st, cadj, rt, lf, posi, tab16, x, xn, s1, s2, grow, acc, hT, z, big, ar, ps = (
        S[k] for k in ("cst", "col", "row", "mcol", "sil", "st", "cadj", "rt", "lf", "posi", "tab16", "x", "xn",
                       "s1", "s2", "grow", "acc", "hT", "z", "big", "ar", "ps"))
    H3, Y3 = (S["hTh"], S["hTl"]), (S["yTh"], S["yTl"])

    def C(name):
        a, n = CST[name]
        return cst[:, a:a + n]

    def K(name, a=0, n=None):
        b, m = COL[name]
        return col[:, b + a:b + (m if n is None else a + n)]

    def R(name, a=0, n=None):
        b, m = ROW[name]
        return row[:, b + a:b + (m if n is None else a + n)]

    bank_free = [[] for _ in range(8)]
    turn = dict(A=0, B=0)

    def take(pool):
        b = (0 if pool == "A" else 4) + turn[pool]
        turn[pool] = (turn[pool] + 1) % 4
        return b

    def take2():
        b = 0 if turn["A"] in (0, 3) else 2
        turn["A"] = (b + 2) % 4
        return b

    def mm(o, l, r, first, last):
        return lambda e: e.matmul(o, l, r, start=first, stop=last)

    def mm3(o, l, r, first, last):
        return [mm(o, l[0], r[0], first, False), mm(o, l[0], r[1], False, False), mm(o, l[1], r[0], False, last)]

    def tr(o, i, n=P):
        return lambda e: e.transpose(o, i, C("ident")[0:n, 0:n])

    def bc(ap, n, at=1):
        a = ap.unsqueeze(at)
        return a.broadcast_to([*a.shape[:at], n, *a.shape[at + 1:]])

    def TT(o, a, b, op):
        return lambda e: e.tensor_tensor(o, a, b, op)

    def TS(o, a, x1, x2, op0, op1=None):
        if op1 is None:
            return lambda e: e.tensor_scalar(o, a, x1, None, op0)
        return lambda e: e.tensor_scalar(o, a, x1, x2, op0, op1)

    def STT(o, a, s, b, op0, op1):
        return lambda e: e.scalar_tensor_tensor(out=o, in0=a, scalar=s, in1=b, op0=op0, op1=op1)

    def CP(o, a):
        return lambda e: e.tensor_copy(o, a)

    def AC(o, a, f=ACT.Copy, **kw):
        return lambda e: e.activation(o, a, f, **kw)

    def RED(o, i, op):
        return lambda e: e.tensor_reduce(o, i, AX, op)

    def ADDMAX(o, a, b, m):
        return lambda e: e.tensor_tensor_reduce(o, a, b, 1.0, -3e38, ALU.add, ALU.max, m)

    def RCP(o):
        return lambda e: e.reciprocal(o, o)

    def dump(name, ap, tok):
        if dbg is not None:
            dbg(name, ap, tok, sp)

    two = lambda a: a.rearrange("p (g n) -> p g n", g=2)
    kn = lambda a, k: a.rearrange("p (k n) -> p k n", k=k)

    noted = []
    chunks = {}
    at_chunk = [0]
    state = dict(dma=0, split=0, nsplit=0)
    hl_free = []
    slot_user = {}
    split_engine = dict(lo=[ve])

    def chunk(n):
        if n not in chunks:
            c = chunks[n] = Chunk()
            c.free = c.pe = None
            c.ready = None
        return chunks[n]

    raw_no = {}

    def send_loads(upto):
        while state["dma"] < min(upto, len(noted) if plan is None else len(plan)):
            m = state["dma"]
            state["dma"] += 1
            item = (noted if plan is None else plan)[m]
            if item is None:
                continue
            src, parts, _, _ = item
            c = chunk(m)
            r = len(raw_no)
            raw_no[m] = r
            order.append(m)
            buf = S["raw"][r % NRAW]
            w = src.shape[1]
            c.raw = buf[0:parts, 0:w]
            c.landed = (f"w{r % NRAW}", 16 * (r // NRAW + 1))
            before = chunk(order[r - NRAW]) if r >= NRAW else None
            sp.dma(lambda e, c=c, src=src: e.dma_start(c.raw, src), *c.landed,
                   (lambda before=before: before.free) if before is not None else None)

    order = []

    def send_splits(upto):
        items = noted if plan is None else plan
        m = state["split"]
        while m < min(upto, len(items)):
            item = items[m]
            if item is None:
                break
            m += 1
            state["split"] = m
            src, parts, split, lo_on = item
            if not split:
                continue
            c = chunk(m - 1)
            send_loads(m)
            k = state["nsplit"]
            state["nsplit"] += 1
            w = src.shape[1]
            c.hi, c.lo = S["hi"][k % NHL][:, 0:w], S["lo"][k % NHL][:, 0:w]
            before = slot_user.get(k % NHL)
            slot_user[k % NHL] = c
            wait = (lambda before=before: before.pe) if before is not None else None
            th = ac.do(AC(c.hi, c.raw), c.landed, wait, hl_free[:])
            eng = po if lo_on == "po" else ve
            tl = eng.do(TT(c.lo, c.raw, c.hi.bitcast(F32), ALU.subtract), th)
            c.ready = [th, tl]
            c.free = [th, tl]

    def load(src, parts=P, split=True, lo="ve"):
        noted.append((src, parts, split, lo))
        n = at_chunk[0]
        at_chunk[0] += 1
        send_loads(n + 1)
        send_splits(n + 1)
        send_loads(n + 1 + NRAW)
        send_splits(n + NHL)
        c = chunk(n)
        if not split:
            c.ready = [c.landed]
        return c

    def barrier():
        noted.append(None)
        assert state["split"] == at_chunk[0]
        at_chunk[0] += 1
        state["split"] = at_chunk[0]
        send_loads(at_chunk[0])

    def used(c, t):
        c.pe = t
        if c.free is None or c.free_is_pe:
            c.free, c.free_is_pe = [t], True

    Chunk.free_is_pe = False

    ndma = 0

    def small(dst, src, *after):
        nonlocal ndma
        ndma += 1
        return sp.dma(lambda e: e.dma_start(dst, src), f"d{ndma}", 16, *after)

    zf = z[:, :, :].rearrange("p t n -> p (t n)")
    cx = zf[:, 0:2048].rearrange("p (t n) -> p t n", t=2)
    t_col = small(col[:, :], t_in["colp"])
    t_cst = small(cst[:, :], t_in["cst"])
    send_loads(3)
    t_cx = small(cx, t_in["ctx"])
    t_x = small(x[:, :, :], t_in["x"])
    t_row = small(row[:, :], t_in["rowp"][0:1, 0:RKEEP].broadcast_to([P, RKEEP]))
    t_pos = small(posi[:, :], t_in["pos"])

    t = ac.do(AC(sil[:, :], col[:, 160:176], ACT.Exp, scale=-1.0), t_col)
    ve.do(TS(sil[:, :], sil[:, :], 1.0, None, ALU.add), t)
    ve.do(RCP(sil[:, :]))
    t_sil = ve.do(TT(sil[:, :], sil[:, :], col[:, 160:176], ALU.mult), t_col)

    acc_free = [None, None]
    t_mcol, t_grow, t_gb = {}, {}, {}

    def adaln_acc(w2, which, a, eng):
        for i, w in enumerate(w2):
            wv = kn(w.raw, 4)
            for k in range(4):
                s = sil[:, 8 * which + 4 * i + k:8 * which + 4 * i + k + 1]
                if i == k == 0:
                    t = eng.do(TS(acc[:, a, :], wv[:, k, :], s, None, ALU.mult), w.landed, acc_free[a], t_sil)
                else:
                    t = eng.do(STT(acc[:, a, :], wv[:, k, :], s, acc[:, a, :], ALU.mult, ALU.add), w.landed)
            w.free = (w.free or []) + [t]
        return t

    def adaln_cols(a, t, dst, bias):
        b = take("B")
        tp = pe.do([mm(ps[:, b, j:j + 1], acc[:, a, 128 * j:128 * j + 128], C("ones")[:, 0:1], True, True)
                    for j in range(4)], t, t_cst, bank_free[b])
        acc_free[a] = tp
        t = ve.do(TT(dst, ps[:, b, 0:4], bias, ALU.add), tp, t_col)
        bank_free[b] = [t]
        return t

    def part_of(piece):
        part, half = piece // 2, piece % 2
        return part, half, {0: 0, 1: 1, 3: 2, 4: 3}.get(part)

    def adaln_gate(l, piece, b, tp):
        part, half, _ = part_of(piece)
        g = 0 if part == 2 else 1
        dst = grow[:, g, 512 * half:512 * half + 512]
        tv = ve.do(TT(dst, dst, ps[:, b, :], ALU.add), tp, t_gb[(l, g)])
        bank_free[b] = [tv]
        t_grow[(l, g, half)] = tv

    def adaln_ve(l, piece):
        part, half, j = part_of(piece)
        w2 = [load(t_in["wmod"][l, piece, :, 2048 * i:2048 * i + 2048], split=False) for i in range(2)]
        a = piece % 2
        t = adaln_acc(w2, 0, a, ve)

        def rest():
            if j is None:
                b = take("B")
                tp = pe.do([mm(ps[:, b, :], C("ones"), acc[:, a, :], True, True)], t, t_cst, bank_free[b])
                acc_free[a] = tp
                adaln_gate(l, piece, b, tp)
            else:
                m0 = 32 * l + 8 * j + 4 * half
                t_mcol[(l, j)] = adaln_cols(a, t, mcol[:, m0:m0 + 4], K("modb", 48 * l + 8 * part + 4 * half, 4))
        return rest

    def adaln_pe(l, piece, cdst=None):
        part, half, j = part_of(piece)
        sv = sil[:, :].rearrange("p (w k) -> p w k", w=2)
        b = take("B")
        for i in range(2):
            w = load(t_in["wmod"][l, piece, :, 2048 * i:2048 * i + 2048], split=False)
            wv = kn(w.raw, 4)
            fns = []
            for k in range(4):
                o = 4 * i + k
                if j is None:
                    fns.append(mm(ps[:, b, :], sil[:, o:o + 1].broadcast_to([P, P]), wv[:, k, :], o == 0, o == 7))
                else:
                    fns.append(mm(ps[0:2, b, :], sv[:, :, o], wv[:, k, :], o == 0, o == 7))
            tp = pe.do(fns, w.landed, t_sil, bank_free[b] if i == 0 else None)
            used(w, tp)
        if j is None:
            adaln_gate(l, piece, b, tp)
            return None
        a = piece % 2
        r2 = acc[0:2, a, :]
        ta = ac.do(AC(r2, ps[0:2, b, :]), tp, acc_free[a])
        bank_free[b] = [ta]
        b = take("B")
        tp = pe.do([tr(ps[:, b, 2 * q:2 * q + 2], r2[:, 128 * q:128 * q + 128], 2) for q in range(4)], ta, t_cst,
                   bank_free[b])
        acc_free[a] = tp
        m0 = 32 * l + 8 * j + 4 * half
        bias = K("modb", 48 * l + 8 * part + 4 * half, 4)
        pv2 = ps[:, b, 0:8].rearrange("p (q w) -> p q w", w=2)
        fns = [TT(mcol[:, m0:m0 + 4], pv2[:, :, 0], bias, ALU.add)]
        if cdst is not None:
            fns.append(TT(cdst, pv2[:, :, 1], bias, ALU.add))
        t = ve.do(fns, tp, t_col)
        bank_free[b] = [t]
        t_mcol[(l, j)] = t
        return t

    def gate_bias(l, g, *free):
        n0 = 2736 + (2 * l + g) * 1024
        t_gb[(l, g)] = small(grow[:, g, :], t_in["rowp"][0:1, n0:n0 + 1024].broadcast_to([P, 1024]), *free)

    def rstd(dst, ss, inv_n, tmp, *after):
        ve.do(TS(ss, ss, inv_n, EPS, ALU.mult, ALU.add), *after)
        ve.do(TS(tmp.bitcast(I32), ss.bitcast(I32), 1, None, ALU.arith_shift_right))
        ve.do(TS(dst.bitcast(I32), tmp.bitcast(I32), -1.0, 1597463007.0, ALU.mult, ALU.add))
        for _ in range(4):
            ve.do(STT(tmp, dst, -0.5, dst, ALU.mult, ALU.mult))
            ve.do(TT(tmp, tmp, ss, ALU.mult))
            t = ve.do(STT(dst, tmp, 1.5, dst, ALU.add, ALU.mult))
        return t

    hT_free, xn_free, s1_free, s2_free = [], [], [], []

    def norm_rows(src, after):
        ta = [ac.do(AC(s1[:, :], src[:, t, :], ACT.Square, accum_out=st[:, t:t + 1]), after, s1_free[:])
              for t in range(2)]
        t_r = rstd(st[:, 2:4], st[:, 0:2], 1.0 / 1024, st[:, 4:6], ta)
        s1_free[:] = [ta[-1]]
        return [ac.do(AC(xn[:, 0, :], src[:, 0, :], scale=st[:, 2:3]), t_r, xn_free[:]),
                ve.do(TS(xn[:, 1, :], src[:, 1, :], st[:, 3:4], None, ALU.mult), t_r, xn_free[:])]

    def norm_T(src, after, scale, shift, t_sc, f32, parts, *free):
        tn = norm_rows(src, after)
        res = []
        for k in range(0, 8, 2):
            b = take("B")
            tp = pe.do([tr(ps[:, b, 256 * j + 128 * t:256 * j + 128 * t + 128],
                           xn[:, t, 128 * (k + j):128 * (k + j) + 128])
                        for j in range(2) for t in range(2)], tn, t_cst, bank_free[b])
            fns = []
            for j in range(2):
                i, o = ps[:, b, 256 * j:256 * j + 256], f32[:, k + j, :]
                sc = scale[:, k + j:k + j + 1]
                sh = 0.0 if shift is None else shift[:, k + j:k + j + 1]
                if k % 4 == 0:
                    fns.append(TS(o, i, sc, None, ALU.mult) if shift is None else TS(o, i, sc, sh, ALU.mult, ALU.add))
                else:
                    fns.append(AC(o, i, scale=sc) if shift is None else AC(o, i, ACT.Identity, scale=sc, bias=sh))
            tt = (ve if k % 4 == 0 else ac).do(fns, tp, t_sc, *free)
            bank_free[b] = [tt]
            res += split_cols(f32[:, k:k + 2, :], [q[:, k:k + 2, :] for q in parts], tt, *free)
        xn_free[:] = [tp]
        return res

    def split_cols(f, parts, *after):
        th = ac.do(AC(parts[0], f), *after)
        tl = ve.do(TT(parts[1], f, parts[0].bitcast(F32), ALU.subtract), th, *after)
        return [th, tl]

    def cond_scale(l, which, norm, dst):
        sc = mcol[:, 32 * l + 16 * which + 8:32 * l + 16 * which + 16]
        return ve.do(STT(dst, sc, 1.0, norm, ALU.add, ALU.mult), t_mcol[(l, 2 * which + 1)], t_col)

    def rows_of(src, wd, jobs, lo="ve", pool="B"):
        banks = [take(pool) for _ in jobs]
        for i in range(2):
            w = load(src[:, 4 * wd * i:4 * wd * i + 4 * wd], lo=lo)
            wh, wl = kn(w.hi, 4), kn(w.lo, 4)
            toks = []
            for b, (hs, t_h, tile) in zip(banks, jobs):
                fns = []
                for k in range(4):
                    lh = [q[:, 4 * i + k, 128 * tile:128 * tile + 128] for q in hs]
                    fns += mm3(ps[:, b, 0:wd], lh, (wh[:, k, :], wl[:, k, :]), i == k == 0, i == 1 and k == 3)
                toks.append(pe.do(fns, w.ready, t_h, bank_free[b] if i == 0 else None))
            used(w, toks[-1])
        return list(zip(banks, toks))

    def cols_of(src, hs, t_h, lo="ve"):
        w = load(src, lo=lo)
        wh, wl = kn(w.hi, 8), kn(w.lo, 8)
        b = take("B")
        fns = []
        for i in range(2):
            for k in range(8):
                fns += mm3(ps[:, b, 256 * i:256 * i + 256],
                           [q[:, k, 128 * i:128 * i + 128] for q in (wh, wl)], [q[:, k, :] for q in hs], k == 0, k == 7)
        tp = pe.do(fns, w.ready, t_h, bank_free[b])
        used(w, tp)
        return b, tp

    def out_proj(srcs, ys, t_y, gate, lo="ve"):
        res = []
        for h in range(2):
            for t, (b, tp) in enumerate(rows_of(srcs[h], 512, [(ys, t_y, 0), (ys, t_y, 1)], lo=lo)):
                xs = x[:, t, 512 * h:512 * h + 512]
                if gate is None:
                    tt = ve.do(TT(xs, xs, ps[:, b, :], ALU.add), tp)
                else:
                    gl, g = gate
                    ve.do(TT(s2[:, 0:512], ps[:, b, :], grow[:, g, 512 * h:512 * h + 512], ALU.mult), tp,
                          t_grow[(gl, g, h)], s2_free[:])
                    tt = ve.do(TT(xs, xs, s2[:, 0:512], ALU.add))
                bank_free[b] = [tt]
                res.append(tt)
        return res, tp

    def weave(tasks, width, filler):
        live, tasks = [], list(tasks)
        while live or tasks:
            while tasks and len(live) < width:
                live.append(tasks.pop(0))
            for g in list(live):
                if next(g, "end") == "end":
                    live.remove(g)
                else:
                    filler()

    gate_bias(0, 0)
    gate_bias(0, 1)
    ctx_pieces = []
    for piece in range(4):
        part, half = piece // 2, piece % 2
        ctx_pieces.append(adaln_pe(0, piece, cadj[:, part, 4 * half:4 * half + 4]))
    t_cc = ve.do(STT(cadj[:, 2, :], cadj[:, 1, :], 1.0, K("n1a", 0, 8), ALU.add, ALU.mult), *ctx_pieces)
    t_sc = cond_scale(0, 0, K("n1a", 0, 8), cadj[:, 3, :])
    th = norm_T(x, t_x, cadj[:, 3, :], mcol[:, 0:8], t_sc, hT, H3)
    thc = norm_T(cx, t_cx, cadj[:, 2, :], cadj[:, 0, :], t_cc,
                 zf[:, 2048:4096].rearrange("p (k n) -> p k n", k=8), Y3)
    tz = []
    r = rows_of(t_in["we_kv"], 256, [(H3, th, 0), (H3, th, 1), (Y3, thc, 0), (Y3, thc, 1)])
    for i, (b, tp) in enumerate(r):
        c0 = 512 if i < 2 else 1280
        tt = ve.do(CP(z[:, i % 2, c0:c0 + 256], ps[:, b, 0:256]), tp, thc, ("pe", pe.n))
        bank_free[b] = [tt]
    for t, (b, tp) in enumerate(rows_of(t_in["we_q"], 512, [(H3, th, 0), (H3, th, 1)])):
        tt = ve.do(CP(z[:, t, 0:512], ps[:, b, :]), tp)
        bank_free[b] = [tt]
    t_qk = tt
    for t, (b, tp) in enumerate(rows_of(t_in["we_p"], 512, [(H3, th, 0), (H3, th, 1)])):
        tt = ac.do(AC(z[:, t, 768:1280], ps[:, b, :]), tp)
        bank_free[b] = [tt]
        tz.append(tt)
    hT_free[:] = [tp]
    yT_free = [tp]
    barrier()
    t_hl = tp
    for t in range(2):
        ve.do(TT(s1[:, 0:640], z[:, t, 0:640], z[:, t, 0:640], ALU.mult), s1_free[:], t_qk)
        ve.do(RED(st[:, 8 + 12 * t:18 + 12 * t], s1[:, 0:640].rearrange("p (h d) -> p h d", d=64), ALU.add))
        ve.do(TT(s1[:, 640:768], z[:, t, 1280:1408], z[:, t, 1280:1408], ALU.mult))
        t_r = ve.do(RED(st[:, 18 + 12 * t:20 + 12 * t], s1[:, 640:768].rearrange("p (h d) -> p h d", d=64), ALU.add))
    t_r = rstd(st[:, 32:56], st[:, 8:32], 1.0 / 64, st[:, 56:80], t_r)
    qT = big[:, 0:1024].rearrange("p (i n) -> p i n", i=4)
    kT = big[:, 1024:1536]
    for t in range(2):
        zq = z[:, t, 0:640].rearrange("p (h d) -> p h d", d=64)
        zc = z[:, t, 1280:1408].rearrange("p (h d) -> p h d", d=64)
        r = st[:, 32 + 12 * t:42 + 12 * t].unsqueeze(2).broadcast_to([P, 10, 64])
        rc = st[:, 42 + 12 * t:44 + 12 * t].unsqueeze(2).broadcast_to([P, 2, 64])
        ve.do(TT(zq, zq, r, ALU.mult), t_row)
        ve.do(TT(z[:, t, 0:640], z[:, t, 0:640], R("qkg"), ALU.mult))
        po.do(TT(zc, zc, rc, ALU.mult), t_r, t_row)
        t_kc = po.do(TT(z[:, t, 1280:1408], z[:, t, 1280:1408], R("qkg", 512, 128), ALU.mult))
        cosv, sinv = C("ropc")[:, 64 * t:64 * t + 64], C("rops")[:, 64 * t:64 * t + 64]
        z5 = z[:, t, 0:640].rearrange("p (h a b j) -> p h a b j", a=2, b=2, j=16)
        s5 = s2[:, 0:640].rearrange("p (h a b j) -> p h a b j", a=2, b=2, j=16)
        v4 = sinv.rearrange("p (a b j) -> p a b j", a=2, b=2)
        ve.do([TT(s1[:, 0:640].rearrange("p (h d) -> p h d", d=64), zq, bc(cosv, 10), ALU.mult)]
              + [TT(s5[:, :, a, q, :], z5[:, :, a, 1 - q, :], bc(v4[:, a, q, :], 10), ALU.mult)
                 for a in range(2) for q in range(2)])
        t_q = ve.do(TT(z[:, t, 0:640], s1[:, 0:640], s2[:, 0:640], ALU.add))
    s1_free[:], s2_free[:] = [], []
    tq = []
    for i in (5, 4, 0, 1, 2, 3):
        b = take("B")
        c0 = 128 * i if i < 5 else 1280
        tp = pe.do([tr(ps[:, b, 128 * t:128 * t + 128], z[:, t, c0:c0 + 128]) for t in range(2)],
                   t_kc if i == 5 else t_q, bank_free[b])
        dst = qT[:, i, :] if i < 4 else (kT[:, 256:512] if i == 4 else kT[:, 0:256])
        t_ = ac.do(AC(dst, ps[:, b, 0:256]), tp, t_hl)
        bank_free[b] = [t_]
        tq.append(t_)
    pT = big[:, 1536:5632].rearrange("p (u k n) -> p u k n", u=4, k=4)
    pbuf = big[:, 5632:7680].rearrange("p (u n) -> p u n", u=4)
    pT_free, pb_free = [None] * 4, [None] * 4
    o_bank = {}
    yf = ar[:, 0:2048].rearrange("p (k n) -> p k n", k=8)
    oT_tok = []
    vno = [0]

    def head(i, s):
        lo = 64 * s
        u = (2 * i + s) % 4
        for t in range(2):
            v = vno[0] % 4
            vno[0] += 1
            b = take("A")
            tp = pe.do([mm(ps[:, b, :], qT[lo:lo + 64, i, 128 * t:128 * t + 128], kT[lo:lo + 64, :], True, True)],
                       tq, bank_free[b])
            m, sm = st[:, 80 + v:81 + v], st[:, 84 + v:85 + v]
            ve.do(RED(m, ps[:, b, :], ALU.max), tp, pb_free[v])
            tv = ve.do(TS(m, m, -0.125, None, ALU.mult))
            ta = ac.do(AC(pbuf[:, v, :], ps[:, b, :], ACT.Exp, bias=m, scale=0.125, accum_out=sm), tv, pb_free[v])
            bank_free[b] = [ta]
            yield
            ve.do(RCP(sm), ta)
            tv = ve.do(TS(pbuf[:, v, :], pbuf[:, v, :], sm, None, ALU.mult))
            b = take("B")
            tp = pe.do([tr(ps[:, b, 128 * k:128 * k + 128], pbuf[:, v, 128 * k:128 * k + 128]) for k in range(4)],
                       tv, bank_free[b])
            pb_free[v] = tp
            t_p = ac.do(AC(pT[:, u, :, 128 * t:128 * t + 128], ps[:, b, :].rearrange("p (k n) -> p k n", k=4)), tp,
                        pT_free[u])
            bank_free[b] = [t_p]
            yield
        b = take("B")
        fns = []
        for k in range(4):
            vv = z[:, k % 2, 1408 + lo:1472 + lo] if k < 2 else z[:, k % 2, 640 + lo:704 + lo]
            fns.append(mm(ps[lo:lo + 64, b, 0:256], vv, pT[:, u, k, :], k == 0, k == 3))
        tp = pe.do(fns, t_p, bank_free[b])
        pT_free[u] = tp
        t_ = ve.do(CP(yf[lo:lo + 64, i, :], ps[lo:lo + 64, b, 0:256]), tp, t_hl)
        bank_free[b] = [t_]
        oT_tok.append(t_)

    def pooling():
        w = load(t_in["pm"], split=False)
        pm = w.raw.rearrange("p (k g n) -> p k g n", k=2, g=4)
        ta = []
        for g in range(0, 4, 2):
            b = take("B")
            tp = pe.do([mm(ps[:, b, 256 * i:256 * i + 256], z[:, k, 768 + 128 * (g + i):896 + 128 * (g + i)],
                           pm[:, k, g + i, :], k == 0, k == 1) for i in range(2) for k in range(2)],
                       w.landed, tz, bank_free[b])
            used(w, tp)
            ta.append(ac.do(AC(s1[:, 256 * g:256 * g + 512], ps[:, b, :]), tp, t_q))
            bank_free[b] = [ta[-1]]
        yield
        for g in range(4):
            b = take("B")
            tp = pe.do([mm(ps[:, b, 0:256], K("plw", 128 * g, 128), s1[:, 256 * g:256 * g + 256], True, True)],
                       ta[g // 2], t_col, bank_free[b])
            tv = ve.do(TS(yf[:, 4 + g, :], ps[:, b, 0:256], K("ps", g, 1), None, ALU.mult), tp, t_hl)
            bank_free[b] = [tv]
            oT_tok.append(tv)
            yield
        s1_free[:] = [tp]

    def conditions():
        for piece in range(4, 12):
            adaln_pe(0, piece)
            for _ in range(4):
                yield

    cond = conditions()
    weave([pooling(), *[head(i, s) for i in range(4) for s in range(2)]], 4, lambda: next(cond, None))
    for _ in cond:
        pass
    barrier()
    hl_free[:] = [("pe", pe.n), ("ve", ve.n)]
    ty = []
    for k in range(0, 8, 2):
        ty += split_cols(yf[:, k:k + 2, :], [q[:, k:k + 2, :] for q in Y3], oT_tok)
    hl_free += ty
    tx, tp = out_proj(t_in["we_out"], Y3, ty, (0, 0))
    dump("x0", x, tx)
    gfree = tx[-1:]

    cT_free = []

    def router(l, t_h):
        L = rt[:, 0:40].rearrange("p (t n) -> p t n", t=2)
        b = take("B")
        rw = K("rw", 160 * l, 160).rearrange("p (k n) -> p k n", k=8)
        fns = []
        for t in range(2):
            fns += [mm(ps[:, b, 20 * t:20 * t + 20], hT[:, k, 128 * t:128 * t + 128], rw[:, k, :],
                       k == 0, k == 7) for k in range(8)]
        tp = pe.do(fns, t_h, t_col, bank_free[b])
        tv = ve.do(TT(L, ps[:, b, 0:40].rearrange("p (t n) -> p t n", t=2), bc(R("rb", 20 * l, 20), 2),
                      ALU.add), tp, t_row)
        bank_free[b] = [tv]
        G, E_ = L[:, :, 0:4], L[:, :, 4:20]
        gm, gs = rt[:, 40:42], rt[:, 42:44]
        m1, m2, d = rt[:, 44:46], rt[:, 46:48], rt[:, 48:50]
        w1, w2 = rt[:, 50:52], rt[:, 52:54]
        v3 = lambda a, n: rt[:, a:a + n].rearrange("p (t n) -> p t n", t=2)
        ge, gk, gc, em, k1, k2, cu, comb, pen = (v3(56, 8), v3(64, 8), v3(72, 8), v3(80, 32), v3(112, 32),
                                                 v3(144, 32), v3(176, 32), v3(208, 32), v3(240, 8))
        b3 = lambda a, n: a.unsqueeze(2).broadcast_to([P, 2, n])

        def first_only(k, c):
            ve.do([lambda e, t=t: e.tensor_tensor_scan(c[:, t, :], k[:, t, :], k[:, t, :], 0.0,
                                                       ALU.add, ALU.bypass) for t in range(2)])
            ve.do(STT(k, c, 1.0, k, ALU.is_equal, ALU.mult))

        ve.do(RED(gm, G, ALU.max))
        tv = ve.do(TT(ge, G, b3(gm, 4), ALU.subtract))
        ac.do(AC(ge, ge, ACT.Exp), tv)
        ve.do(TT(gk, G, b3(gm, 4), ALU.is_equal))
        first_only(gk, gc)
        ve.do(TS(pen, gk, 1.0, 1e30, ALU.subtract, ALU.mult))
        ve.do([TT(em[:, t, :].rearrange("p (g n) -> p g n", n=4), E_[:, t, :].rearrange("p (g n) -> p g n", n=4),
                  pen[:, t, :].unsqueeze(2).broadcast_to([P, 4, 4]), ALU.add) for t in range(2)])
        ve.do(RED(m1, em, ALU.max))
        ve.do(TT(k1, em, b3(m1, 16), ALU.is_equal))
        first_only(k1, cu)
        ve.do(STT(em, k1, -3e30, em, ALU.mult, ALU.add))
        ve.do(RED(m2, em, ALU.max))
        ve.do(TT(k2, em, b3(m2, 16), ALU.is_equal))
        first_only(k2, cu)
        tv = ve.do(TT(d, m2, m1, ALU.subtract))
        ta = ac.do(AC(d, d, ACT.Exp), tv)
        ve.do(RED(gs, ge, ALU.add), ta)
        ve.do(STT(w1, d, 1.0, gs, ALU.add, ALU.mult))
        ve.do(RCP(w1))
        ve.do(TT(w2, w1, d, ALU.mult))
        ve.do([TT(comb, k1, b3(w1, 16), ALU.mult), TT(k2, k2, b3(w2, 16), ALU.mult)])
        tv = ve.do(TT(comb, comb, k2, ALU.add))

        def to_rows():
            b = take("B")
            tp = pe.do([tr(ps[0:16, b, 128 * t:128 * t + 128], comb[:, t, :]) for t in range(2)], tv, bank_free[b])
            t_ = ve.do(CP(tab16[:, :], ps[0:16, b, 0:256]), tp, cT_free[:])
            bank_free[b] = [t_]
            return t_
        return to_rows

    hidh, hidl, ex = S["hidh"], S["hidl"], S["ex"][:, :].rearrange("p (u n) -> p u n", u=4)

    def experts(l, t_h, extra):
        to_rows = router(l, t_h)
        t_c = None
        cw_free = [None] * 4
        hid_free = [None, None]
        done = {}
        rests = {}
        for e_ in range(17):
            if e_ < 16:
                u = e_ % 2
                banks = [take("B"), take("B")]
                for s in range(2):
                    w = load(t_in["wgu"][l, e_, :, 2048 * s:2048 * s + 2048], lo="ve")
                    wh, wl = kn(w.hi, 8), kn(w.lo, 8)
                    for f in range(2):
                        fns = []
                        for k in range(8):
                            fns += mm3(ps[:, banks[f], 256 * s:256 * s + 256],
                                       [q[:, k, 128 * f:128 * f + 128] for q in (wh, wl)],
                                       [q[:, k, :] for q in H3], k == 0, k == 7)
                        tp = pe.do(fns, w.ready, t_h, bank_free[banks[f]] if s == 0 else None)
                        if s == 1:
                            b = banks[f]
                            v = ex[:, 2 * u + f, 0:256]
                            ta = ac.do(AC(v, ps[:, b, 0:256], ACT.Silu), tp, hid_free[u])
                            tv = ve.do(TT(v, v, ps[:, b, 256:512], ALU.mult), ta)
                            bank_free[b] = [tv]
                    used(w, tp)
                if t_c is None:
                    t_c = to_rows()
                b = take("B")
                tcw = pe.do([mm(ps[:, b, 0:256], C("ident")[0:16, e_:e_ + 1].broadcast_to([16, P]),
                                tab16[:, :], True, True)], t_c, bank_free[b])
                hf = []
                for f in range(2):
                    v = ex[:, 2 * u + f, 0:256]
                    v2 = ex[:, 2 * u + f, 256:512]
                    tv = ve.do(TT(v2, v, ps[:, b, 0:256], ALU.mult), tcw)
                    hf += split_cols(v2, (hidh[:, u, f, :], hidl[:, u, f, :]), tv, hid_free[u])
                bank_free[b] = [tv]
                done[e_] = hf
            if e_ >= 1:
                q = e_ - 1
                w = load(t_in["wdn"][l, q // 2, :, 2048 * (q % 2):2048 * (q % 2) + 2048], lo="po")
                wh, wl = kn(w.hi, 2), kn(w.lo, 2)
                fns = []
                for t in range(2):
                    for h in range(2):
                        for f in range(2):
                            fns += mm3(ps[:, 2 * t + h, :],
                                       [a[:, q % 2, f, 128 * t:128 * t + 128] for a in (hidh, hidl)],
                                       [a[:, f, 512 * h:512 * h + 512] for a in (wh, wl)],
                                       q == 0 and f == 0, q == 15 and f == 1)
                tp = pe.do(fns, w.ready, done[q], [bank_free[b] for b in range(4)] if q == 0 else None)
                used(w, tp)
                hid_free[q % 2] = tp
            if e_ in extra:
                if e_ - 1 in rests:
                    rests.pop(e_ - 1)()
                rests[e_] = extra[e_]()
        for r_ in rests.values():
            r_()
        hT_free[:] = [tp]
        cT_free[:] = [tp]
        res = []
        for t in range(2):
            for h in range(2):
                b = 2 * t + h
                ve.do(TT(s1[:, 0:512], ps[:, b, :], grow[:, 1, 512 * h:512 * h + 512], ALU.mult), tp,
                      t_grow[(l, 1, h)], s1_free[:])
                xs = x[:, t, 512 * h:512 * h + 512]
                tt = ve.do(TT(xs, xs, s1[:, 0:512], ALU.add))
                bank_free[b] = [tt]
                res.append(tt)
        s1_free[:] = []
        return res

    t_sc = cond_scale(0, 1, K("n2a", 0, 8), cadj[:, 3, :])
    th = norm_T(x, tx, cadj[:, 3, :], mcol[:, 16:24], t_sc, hT, H3, hT_free[:])
    gate_bias(1, 0, gfree)
    extra = {e_: (lambda e_=e_: adaln_ve(1, e_ - 2)) for e_ in range(2, 12)}
    tx = experts(0, th, extra)
    gate_bias(1, 1, tx[-1:])
    dump("x1", x, tx)

    t_sc = cond_scale(1, 0, K("n1a", 8, 8), cadj[:, 3, :])
    th = norm_T(x, tx, cadj[:, 3, :], mcol[:, 32:40], t_sc, hT, H3, hT_free[:])
    v_ = xn[:, :, :].rearrange("p t n -> p (t n)")[:, 0:1024].rearrange("p (t n) -> p t n", t=2)
    for t, (b, tp) in enumerate(rows_of(t_in["wo_v"], 512, [(H3, th, 0), (H3, th, 1)])):
        tv = ve.do(CP(v_[:, t, :], ps[:, b, :]), tp, xn_free[:])
        bank_free[b] = [tv]
        ve.do(TT(s1[:, 512 * t:512 * t + 512], v_[:, t, :], v_[:, t, :], ALU.mult), s1_free[:])
        tv = ve.do(RED(st[:, 8 + 4 * t:12 + 4 * t], s1[:, 512 * t:512 * t + 512].rearrange("p (g c) -> p g c", g=4),
                       ALU.add))
    rests = [adaln_ve(1, piece) for piece in (10, 11)]
    tv = rstd(st[:, 16:24], st[:, 8:16], 1.0 / 128, st[:, 24:32], tv)
    for t in range(2):
        zg = v_[:, t, :].rearrange("p (g c) -> p g c", g=4)
        ve.do(TT(zg, zg, st[:, 16 + 4 * t:20 + 4 * t].unsqueeze(2).broadcast_to([P, 4, 128]), ALU.mult))
        t_v = ve.do(TT(v_[:, t, :], v_[:, t, :], R("sgg"), ALU.mult), t_row)
    uT = zf[:, 0:1024].rearrange("p (g n) -> p g n", g=4)
    hxT = zf[:, 1024:2048].rearrange("p (g n) -> p g n", g=4)
    bgT = zf[:, 2048:3072].rearrange("p (g n) -> p g n", g=4)
    zTf = zf[:, 3072:3072 + 4 * 258]
    zT = zTf.rearrange("p (g n) -> p g n", g=4)
    t_pad = ve.do(lambda e: e.memset(zTf, 0.0), hT_free[:])
    for name, dst in (("wo_u", uT), ("wo_hx", hxT), ("wo_bg", bgT)):
        for j in range(2):
            b, tp = cols_of(t_in[name][j], H3, th)
            ta = ac.do(AC(dst[:, 2 * j:2 * j + 2, :], two(ps[:, b, :])), tp, hT_free[:])
            bank_free[b] = [ta]
        if name == "wo_u":
            for r_ in rests:
                r_()
            t_u = ta
    for j in range(2):
        b, tp = cols_of(t_in["wo_cg"][j], H3, th)
        tv = ve.do(TT(zT[:, 2 * j:2 * j + 2, 1:257], two(ps[:, b, :]), hxT[:, 2 * j:2 * j + 2, :], ALU.mult), tp, ta)
        bank_free[b] = [tv]
    hT_free[:] = [tp]
    yt = []
    for g in range(4):
        b = take("B")
        tp = pe.do([mm(ps[:, b, 128 * t:128 * t + 128], v_[:, t, 128 * g:128 * g + 128], K("sgw", 128 * g, 128),
                       True, True) for t in range(2)], t_v, t_col, bank_free[b])
        xn_free[:] = [tp]
        s_ = s2[:, 256 * g:256 * g + 256]
        tv = ve.do(TT(s_.rearrange("p (t n) -> p t n", t=2), ps[:, b, 0:256].rearrange("p (t n) -> p t n", t=2),
                      bc(R("sgb", 128 * g, 128), 2), ALU.add), tp)
        bank_free[b] = [tv]
        tv = ve.do(TT(uT[:, g, :], s_, uT[:, g, :], ALU.mult), t_u)
        if g % 2:
            yt += split_cols(uT[:, g - 1:g + 1, :], [q[:, g - 1:g + 1, :] for q in Y3], tv)
    for g in range(4):
        y = hxT[:, g, :]
        ve.do(TS(y, zT[:, g, 0:256], K("cw", g, 1), None, ALU.mult))
        ve.do(STT(y, zT[:, g, 1:257], K("cw", 4 + g, 1), y, ALU.mult, ALU.add))
        ve.do(STT(y, zT[:, g, 2:258], K("cw", 8 + g, 1), y, ALU.mult, ALU.add))
        tv = ve.do(TT(y, y, bgT[:, g, :], ALU.mult), ta)
        if g % 2:
            yt += split_cols(hxT[:, g - 1:g + 1, :], [q[:, 3 + g:5 + g, :] for q in Y3], tv)
    tx, tp = out_proj(t_in["wo_out"], Y3, yt, (1, 0))
    dump("x2", x, tx)
    t_sc = cond_scale(1, 1, K("n2a", 8, 8), cadj[:, 3, :])
    th = norm_T(x, tx, cadj[:, 3, :], mcol[:, 48:56], t_sc, hT, H3, hT_free[:])
    tx = experts(1, th, {})
    dump("x3", x, tx)

    T = [K("plw", 56 * i, 56) for i in range(6)]
    t3 = lambda a: a.rearrange("p (t n) -> p t n", t=2)
    posf = st[:, 90:92]
    ve.do(CP(posf, posi[:, :]), t_pos)
    ve.do(TT(t3(T[0]), posf.unsqueeze(2).broadcast_to([P, 2, 28]), bc(C("inv"), 2), ALU.mult), t_cst)
    ve.do(TS(T[1], T[0], 1.0 / TWO_PI, None, ALU.mult))
    ve.do(TS(T[1], T[1], 12582912.0, None, ALU.add))
    ve.do(TS(T[1], T[1], 12582912.0, None, ALU.subtract))
    for part in (6.28125, 1.9350051879882812e-03, 3.0199159819567e-07):
        ve.do(STT(T[0], T[1], -part, T[0], ALU.mult, ALU.add))
    PI = 3.1415925
    ve.do(TS(T[2], T[0], 1.5707963267948966, None, ALU.add))
    ve.do(TS(T[3], T[2], PI, -TWO_PI, ALU.is_gt, ALU.mult))
    ve.do(TT(T[2], T[2], T[3], ALU.add))
    ve.do(TS(T[0], T[0], PI, -PI, ALU.min, ALU.max))
    tv = ve.do(TS(T[2], T[2], PI, -PI, ALU.min, ALU.max))
    ac.do(AC(T[4], T[2], ACT.Sin), tv)
    t_tab = ac.do(AC(T[5], T[0], ACT.Sin))
    cos, sin = t3(T[4]), t3(T[5])

    sgT = big[:, 0:8192].rearrange("p (g n) -> p g n", g=32)
    off = [0]

    def area(n):
        a = off[0]
        off[0] += n
        return ar[:, a:a + n]

    nq = area(512).rearrange("p (i n) -> p i n", i=2)
    dq = area(512).rearrange("p (i n) -> p i n", i=2)
    kk = area(768).rearrange("p (i n) -> p i n", i=3)
    mq = area(1024).rearrange("p (h n) -> p h n", h=4)
    mk = area(1024).rearrange("p (h n) -> p h n", h=4)
    pbs = [area(1024), area(1024)]
    gr = grow[:, :, :].rearrange("p a n -> p (a n)")
    pTs = [area(1536), gr[:, 0:1536]]
    pTs = [(p[:, 0:1024].rearrange("p (h n) -> p h n", h=4), p[:, 1024:1536].rearrange("p (h n) -> p h n", h=4))
           for p in pTs]
    cmpb = area(400)
    cmb = acc[:, :, :].rearrange("p a n -> p (a n)")
    oTs = S["oTs"][:, :].rearrange("p (n i m) -> p n i m", n=4, i=2)
    mzb = xn[:, :, :].rearrange("p t n -> p (t n)")
    mixf = mzb.rearrange("p (k n) -> p k n", k=8)
    dmask = K("sgw").rearrange("p (t n) -> p t n", t=2)
    rp = rt
    z_free, big_free, oTs_free = [tx[-1]], [], []

    def rope(view, half, c0, *after):
        n = view.shape[2]
        m = n * half
        a, b = [[rp[:, m * (2 * i + t):m * (2 * i + t) + m].rearrange("p (h j) -> p h j", h=n) for t in range(2)]
                for i in range(2)]
        c = [bc(cos[:, t, c0:c0 + half], n) for t in range(2)]
        s = [bc(sin[:, t, c0:c0 + half], n) for t in range(2)]
        x1, x2 = view[:, :, :, 0:half], view[:, :, :, half:2 * half]
        ve.do([TT(a[t], x1[:, t], s[t], ALU.mult) for t in range(2)]
              + [TT(b[t], x2[:, t], s[t], ALU.mult) for t in range(2)], t_tab, *after)
        ve.do([TT(x1[:, t], x1[:, t], c[t], ALU.mult) for t in range(2)]
              + [TT(x2[:, t], x2[:, t], c[t], ALU.mult) for t in range(2)])
        return ve.do([TT(x1[:, t], x1[:, t], b[t], ALU.subtract) for t in range(2)]
                     + [TT(x2[:, t], x2[:, t], a[t], ALU.add) for t in range(2)])

    def layer2(l, tx):
        th = norm_T(x, tx, K("n1b", 8 * l, 8), None, t_col, hT, H3, hT_free[:])
        zo = [0]
        for wd in ZW:
            zo.append(zo[-1] + wd)
        tz = []
        for i, wd in enumerate(ZW):
            r = rows_of(t_in["wz"][l, :, 8 * zo[i]:8 * zo[i] + 8 * wd], wd, [(H3, th, 0), (H3, th, 1)],
                        lo="po" if i % 2 else "ve")
            for t, (b, tp) in enumerate(r):
                o, i_ = z[:, t, zo[i]:zo[i] + wd], ps[:, b, 0:wd]
                tt = ac.do(AC(o, i_), tp, z_free[:]) if t else ve.do(CP(o, i_), tp, z_free[:])
                bank_free[b] = [tt]
                tz.append(tt)
        tz = [tz[2 * i:2 * i + 2] for i in range(6)]
        barrier()
        t_hl = tp
        gates = []
        last_gate = []

        def gate_tiles():
            for d in range(8):
                for n in range(4):
                    if n % 2 == 0:
                        w = load(t_in["wgt"][l, d, n // 2], split=False)
                        wv = kn(w.raw, 8)
                        b = take("B")
                    o = ps[:, b, 256 * (n % 2):256 * (n % 2) + 256]
                    tp = pe.do([mm(o, wv[:, k, 128 * (n % 2):128 * (n % 2) + 128], hT[:, k, :],
                                   k == 0, k == 7) for k in range(8)], w.landed, bank_free[b] if n % 2 == 0 else None)
                    used(w, tp)
                    if n % 2:
                        ta = ac.do(AC(sgv[:, n - 1:n + 1, d, :], two(ps[:, b, :]), ACT.Tanh, scale=0.5), tp, t_hl,
                                   big_free[:])
                        bank_free[b] = [ta]
                        gates.append(ta)
                    last_gate[:] = [tp]
                    if n % 2:
                        yield

        sgv = big[:, 0:8192].rearrange("p (n d m) -> p n d m", n=4, d=8)
        gen = gate_tiles()

        def fill():
            next(gen, None)

        Z = lambda t, a, n: z[:, t, a:a + n]
        zr = z[:, :, 312:1080].rearrange("p t (h d) -> p t h d", d=64)
        zi = z[:, :, 0:288].rearrange("p t (h d) -> p t h d", d=32)
        SM = 288
        RQ, VV, ML, FQ, FV = 312, 1080, 1336, 1752, 2264
        tok = {}
        HB = lambda ap, h: ap[64 * (h % 2):64 * (h % 2) + 64]
        causal = lambda t, n: C("mask")[:, 256 - n:256]
        to = {}

        def indexer():
            t_i = rope(zi[:, :, :, 0:8], 4, 24, tz[0])
            b = take("B")
            tp = pe.do([tr(ps[:, b, 256 * i + 128 * t:256 * i + 128 * t + 128], Z(t, 128 * i, 128))
                        for i in range(2) for t in range(2)], t_i, bank_free[b])
            ta1 = ac.do(AC(mq[:, 0:2, :], ps[:, b, :].rearrange("p (i n) -> p i n", i=2)), tp, t_hl)
            bank_free[b] = [ta1]
            b = take("B")
            kd = s2[:, 0:256].rearrange("p (t n) -> p t n", t=2)
            td = ve.do([CP(kd[:, t, :].rearrange("p (r d) -> p r d", r=4), bc(Z(t, 256, 32), 4)) for t in range(2)],
                       s2_free[:])
            tp = pe.do([tr(ps[:, b, 128 * t:128 * t + 128], kd[:, t, :]) for t in range(2)], td, bank_free[b])
            kiT = mq[:, 2, :]
            ta2 = ac.do(AC(kiT, ps[:, b, 0:256]), tp)
            bank_free[b] = [ta2]
            wi = lf[:, 0:16].rearrange("p (t h) -> p t h", t=2)
            ve.do(TS(wi, z[:, :, SM + 16:SM + 24], 8 ** -0.5, None, ALU.mult))
            rfree = [[tp]] * 4
            yield
            for t in (1, 0):
                nk = 128 * (t + 1)
                sc = s1[:, 256 * t:256 * t + nk]
                for j2 in range(2):
                    b = take2()
                    toks = []
                    for j in range(2):
                        p0 = 32 * (2 * j2 + j)
                        toks.append(pe.do([mm(ps[:, b + j, 256 * i:256 * i + nk],
                                              mq[p0:p0 + 32, i, 128 * t:128 * t + 128], kiT[p0:p0 + 32, 0:nk],
                                              True, True) for i in range(2)], ta1, ta2, bank_free[b + j]))
                    for j in range(2):
                        for i in range(2):
                            h = 4 * i + 2 * j2 + j
                            r = s2[:, 256 * (h % 4):256 * (h % 4) + nk]
                            ta = ac.do(AC(r, ps[:, b + j, 256 * i:256 * i + nk], ACT.Relu, scale=32 ** -0.5),
                                       toks[j], rfree[h % 4])
                            wcol = wi[:, t, h:h + 1]
                            if j == i == j2 == 0:
                                tv = ve.do(TS(sc, r, wcol, None, ALU.mult), ta, s1_free[:])
                            else:
                                tv = ve.do(STT(sc, r, wcol, sc, ALU.mult, ALU.add), ta)
                            rfree[h % 4] = [tv]
                        bank_free[b + j] = [ta]
                    yield
                mk_ = C("mask")[:, 256 - nk:256]
                ve.do(TT(sc, sc, mk_, ALU.add))
                wk = s1[:, 512 + 256 * t:512 + 256 * t + nk]
                m8 = lf[:, 16:24]
                src = sc
                for r8 in range(8):
                    ve.do(lambda e, src=src: e.max(m8, src))
                    ve.do(lambda e, src=src, wk=wk: e.match_replace(wk, m8, src, -3e38))
                    src = wk
                    if r8 in (2, 5):
                        yield
                ve.do(TS(wk, wk, -2e38, NEG, ALU.is_gt, ALU.mult))
                tok["sel"] = ve.do(TT(dmask[:, t, 0:nk], wk, mk_, ALU.min), tok.get("dmfree"))
                yield
            s1_free[:] = []
            s2_free[:] = [tok["sel"]]

        def heads():
            tok["r"] = t_h = rope(zr[:, :, :, 0:16], 8, 16, tz[1], tz[2])
            for dst, c0 in ((nq[:, 0], 0), (nq[:, 1], 128), (dq[:, 0], 448), (dq[:, 1], 576)):
                b = take("B")
                tp = pe.do([tr(ps[:, b, 128 * t:128 * t + 128], Z(t, RQ + c0, 128)) for t in range(2)], t_h,
                           bank_free[b])
                ta = ac.do(AC(dst, ps[:, b, 0:256]), tp, t_hl)
                bank_free[b] = [ta]
            for i, c0 in enumerate((320, 384, 704)):
                b = take("B")
                k2 = mzb[:, 256 * i:256 * i + 256].rearrange("p (t n) -> p t n", t=2)
                td = po.do([CP(k2[:, t, :].rearrange("p (r d) -> p r d", r=2), bc(Z(t, RQ + c0, 64), 2))
                            for t in range(2)], t_h, xn_free[:])
                tp = pe.do([tr(ps[:, b, 128 * t:128 * t + 128], k2[:, t, :]) for t in range(2)], td, bank_free[b])
                tok["kk"] = ac.do(AC(kk[:, i], ps[:, b, 0:256]), tp, t_hl)
                bank_free[b] = [tok["kk"]]
            xn_free[:] = [tp]
            yield

        def compress():
            t_h = tok["r"]
            w2 = [load(t_in["wcmp"][l, :, 2048 * s:2048 * s + 2048], parts=64, split=False) for s in range(2)]
            b = take("B")
            tp = pe.do([tr(ps[0:64, b, 256 * s + 128 * t:256 * s + 128 * t + 128], Z(t, c0, 64))
                        for s, c0 in ((0, RQ + 256), (1, VV)) for t in range(2)], t_h, tz[2], bank_free[b])
            kcT = mzb[0:64, 1024:1536]
            t_ = ac.do(AC(kcT, ps[0:64, b, :]), tp, xn_free[:])
            bank_free[b] = [t_]
            G = pbs[1][0:64, 0:1024].rearrange("p (s m c) -> p s m c", s=2, m=32)
            fns = []
            for s in range(2):
                src = kcT[:, 256 * s:256 * s + 256]
                fns.append(CP(G[:, s, :, 15], K("pe", 64 * l + 32 * s, 32)[0:64, :]))
                for hh in range(2):
                    fns.append(CP(G[:, s, 16 * hh:16 * hh + 16, 0:15],
                                  src[:, 16 * hh:16 * hh + 240].rearrange("p (w m) -> p m w", m=16)))
            tv = po.do(fns, t_, pb_user[1], t_hl, t_col)
            yield
            kvc = cmpb[0:64, 0:32].rearrange("p (s c) -> p s c", s=2)
            b = take("B")
            for s in range(2):
                wcv = w2[s].raw.rearrange("p (m d) -> p m d", m=32)
                tp = pe.do([mm(ps[0:64, b, 16 * s:16 * s + 16], wcv[:, m, :], G[:, s, m, :], m == 0, m == 31)
                            for m in range(32)], tv, w2[s].landed, bank_free[b] if s == 0 else None)
                used(w2[s], tp)
            pb_user[1] = tp
            pc = ps[0:64, b, 0:32].rearrange("p (s c) -> p s c", s=2)
            kv_ = cmpb[0:64, 32:34]
            ve.do(CP(kv_, pc[:, :, 15]), tp, t_hl)
            tv = ve.do([TS(kvc[:, s, 0:15], pc[:, s, 0:15], kv_[:, s:s + 1], None, ALU.add) for s in range(2)])
            bank_free[b] = [tv]
            yield
            kct, vct, kr = cmpb[:, 40:56], cmpb[0:15, 64:128], cmpb[0:15, 128:256]
            b = take("B")
            tp = pe.do([tr(ps[0:15, b, 0:64], kvc[:, 0, 0:15], 64), tr(ps[0:15, b, 64:128], kvc[:, 1, 0:15], 64)],
                       tv, bank_free[b])
            t_vc = ve.do([CP(kr[:, 0:64], ps[0:15, b, 0:64]), CP(kr[:, 64:128], ps[0:15, b, 0:64]),
                          CP(vct, ps[0:15, b, 64:128])], tp)
            bank_free[b] = [t_vc]
            sg = lf[:, 24:48].rearrange("p (t n) -> p t n", t=2)
            ta = ac.do(AC(sg, z[:, :, SM:SM + 12], ACT.Exp, scale=-1.0), tz[0])
            ve.do(TS(sg, sg, 1.0, None, ALU.add), ta)
            tok["sg"] = ve.do(RCP(sg))
            yield
            b = take("B")
            tp = pe.do([tr(ps[:, b, 0:15], kr, 15)], t_vc, bank_free[b])
            t_kc = ve.do(CP(kct[:, 0:15], ps[:, b, 0:15]), tp)
            bank_free[b] = [t_kc]
            yield
            b = take2()
            pcp = cmpb[:, 256:376].rearrange("p (t h c) -> p t h c", t=2, h=4)
            tp = pe.do([mm(ps[:, b + h % 2, 32 * t + 16 * (h // 2):32 * t + 16 * (h // 2) + 15],
                           HB(nq, h)[:, h // 2, 128 * t:128 * t + 128], HB(kct, h)[:, 0:15], True, True)
                        for t in range(2) for h in range(4)], t_kc, tok["kk"], bank_free[b], bank_free[b + 1])
            ca, cm = C("cadd"), C("cmul")
            fns = []
            for t in range(2):
                for e2 in range(2):
                    i_ = ps[:, b + e2, 32 * t:32 * t + 32].rearrange("p (i c) -> p i c", i=2)[:, :, 0:15]
                    o = pcp[:, t].rearrange("p (i e) c -> p i e c", e=2)[:, :, e2, :]
                    fns.append(TT(o, i_, bc(ca[:, 15 * t:15 * t + 15], 2), ALU.add))
            tm = ve.do(fns, tp)
            bank_free[b] = bank_free[b + 1] = [tm]
            m, sm = st[:, 100:108], st[:, 108:116]
            p3 = pcp.rearrange("p t h c -> p (t h) c")
            mu = [bc(cm[:, 15 * t:15 * t + 15], 4) for t in range(2)]
            ve.do(RED(m, p3, ALU.max))
            tv = ve.do(TT(p3, p3, m.unsqueeze(2).broadcast_to([P, 8, 15]), ALU.subtract))
            ta = ac.do(AC(p3, p3, ACT.Exp, scale=0.125), tv)
            ve.do([TT(pcp[:, t], pcp[:, t], mu[t], ALU.mult) for t in range(2)], ta)
            ve.do(RED(sm, p3, ALU.add))
            ve.do(TS(sm, sm, 1e-30, None, ALU.max))
            ve.do(RCP(sm))
            ve.do(TT(sm.rearrange("p (t h) -> p t h", t=2), sm.rearrange("p (t h) -> p t h", t=2), sg[:, :, 0:4],
                     ALU.mult))
            tv = ve.do(TT(p3, p3, sm.unsqueeze(2).broadcast_to([P, 8, 15]), ALU.mult))
            yield
            pcT = cmb[0:15, :].rearrange("p (h n) -> p h n", h=4)
            for t in range(2):
                bb = take("B")
                tp = pe.do([tr(ps[0:15, bb, 128 * h:128 * h + 128], pcp[:, t, h, :]) for h in range(4)], tv,
                           bank_free[bb])
                tok["cmp"] = ac.do(AC(pcT[:, :, 128 * t:128 * t + 128],
                                      ps[0:15, bb, :].rearrange("p (h n) -> p h n", h=4)), tp, oTs_free[:])
                bank_free[bb] = [tok["cmp"]]
            tok["pcT"], tok["vct"] = pcT, vct

        def attend(name, q, k, scale, mask, gate, toks, slot, then=None):
            pT = pTs[slot]
            for t in range(2):
                n = 128 * (t + 1)
                v = slot
                pb = pbs[v]
                m, sm = st[:, 116 + 8 * v:120 + 8 * v], st[:, 120 + 8 * v:124 + 8 * v]
                b = take2()
                tp = pe.do([mm(ps[:, b + h % 2, n * (h // 2):n * (h // 2) + n], q(h, t), k(h, n), True, True)
                            for h in range(4)], toks(), bank_free[b], bank_free[b + 1])
                tm = ve.do([ADDMAX(pb[:, n * h:n * h + n], ps[:, b + h % 2, n * (h // 2):n * (h // 2) + n],
                                   mask(t, n), m[:, h:h + 1]) for h in range(4)], tp, pb_user[v], t_hl)
                bank_free[b] = bank_free[b + 1] = [tm]
                tv = ve.do(TS(m, m, -scale, None, ALU.mult))
                ta = ac.do([AC(pb[:, n * h:n * h + n], pb[:, n * h:n * h + n], ACT.Exp, bias=m[:, h:h + 1],
                               scale=scale, accum_out=sm[:, h:h + 1]) for h in range(4)], tv)
                yield
                tv = ve.do(RCP(sm), ta)
                if gate is not None:
                    tv = ve.do(TT(sm, sm, gate[:, t, :], ALU.mult), tok["sg"])
                pap = pb[:, 0:4 * n].rearrange("p (h n) -> p h n", h=4)
                tv = po.do(TT(pap, pap, sm.unsqueeze(2).broadcast_to([P, 4, n]), ALU.mult), tv)
                yield
                for kt in range(t + 1):
                    bb = take("B")
                    tp = pe.do([tr(ps[:, bb, 128 * h:128 * h + 128], pap[:, h, 128 * kt:128 * kt + 128])
                                for h in range(4)], tv, bank_free[bb])
                    dst = pT[0][:, :, 128 * t:128 * t + 128] if kt == 0 else pT[1]
                    ta = ac.do(AC(dst, ps[:, bb, :].rearrange("p (h n) -> p h n", h=4)), tp, pT_user[slot], t_hl)
                    bank_free[bb] = [ta]
                pb_user[v] = tp
                yield
            tok[name] = ta
            if then is not None:
                then()

        def values(n, paths, toks, slots):
            b = take("B")
            fns = []
            for h in range(4):
                lo = 64 * (h % 2)
                c0 = 256 * (h // 2)
                ops = paths(h)
                for i, (l_, r_, q0) in enumerate(ops):
                    fns.append(mm(ps[lo:lo + 64, b, c0 + q0:c0 + 256], l_, r_, i == 0, i == len(ops) - 1))
            tp = pe.do(fns, toks, bank_free[b])
            for s in slots:
                pT_user[s] = tp
            t_ = ve.do(CP(oTs[:, n], ps[:, b, :].rearrange("p (i m) -> p i m", i=2)), tp, oTs_free[:], t_hl)
            bank_free[b] = [t_]
            to[n] = t_

        def pv(a, h, slot):
            return [(Z(0, a(h), 64), pTs[slot][0][:, h, :], 0), (Z(1, a(h), 64), pTs[slot][1][:, h, :], 128)]

        def mla():
            wm = load(t_in["wmla"][l], split=False)
            for t in range(2):
                ve.do(TT(s2[:, 0:384], Z(t, ML, 384), Z(t, ML, 384), ALU.mult), tz[3], s2_free[:])
                tv = ve.do([RED(st[:, 8 + 2 * t:9 + 2 * t], s2[:, 0:256], ALU.add),
                            RED(st[:, 9 + 2 * t:10 + 2 * t], s2[:, 256:384], ALU.add)])
            tv = ve.do([TS(st[:, 9 + 2 * t:10 + 2 * t], st[:, 9 + 2 * t:10 + 2 * t], 2.0, None, ALU.mult)
                        for t in range(2)])
            tv = rstd(st[:, 12:16], st[:, 8:12], 1.0 / 256, st[:, 16:20], tv)
            tv = ve.do([f for t in range(2) for f in (
                TS(Z(t, ML, 256), Z(t, ML, 256), st[:, 12 + 2 * t:13 + 2 * t], None, ALU.mult),
                TS(Z(t, ML + 256, 128), Z(t, ML + 256, 128), st[:, 13 + 2 * t:14 + 2 * t], None, ALU.mult))])
            tkr = rope(z[:, :, ML + 384:ML + 416].unsqueeze(2), 16, 0)
            yield
            cT_ = s2[:, 0:768].rearrange("p (i n) -> p i n", i=3)
            for i in range(3):
                b = take("B")
                tp = pe.do([tr(ps[:, b, 128 * t:128 * t + 128], Z(t, ML + 128 * i, 128)) for t in range(2)], tv,
                           bank_free[b])
                g = K("gq", 2 * l + i, 1) if i < 2 else K("gkv", l, 1)
                t_ = ac.do(AC(cT_[:, i, :], ps[:, b, 0:256], scale=g), tp, tv)
                bank_free[b] = [t_]
            yield
            mz = mzb.rearrange("p (t n) -> p t n", t=2)
            for t in range(2):
                b = take("B")
                tp = pe.do([mm(ps[:, b, 0:384], cT_[:, k, 128 * t:128 * t + 128], wm.raw[:, 384 * k:384 * k + 384],
                               k == 0, k == 1) for k in range(2)], t_, wm.landed, bank_free[b])
                tq_ = ac.do(AC(mz[:, t, 0:384], ps[:, b, 0:384]), tp, tok["cmp"], tok["kk"], xn_free[:])
                bank_free[b] = [tq_]
                b = take("B")
                tp = pe.do([mm(ps[:, b, :], cT_[:, 2, 128 * t:128 * t + 128], wm.raw[:, 768:1280], True, True)],
                           bank_free[b])
                used(wm, tp)
                pv_ = ps[:, b, :].rearrange("p (h n) -> p h n", h=4)
                k4 = mz[:, t, 384:768].rearrange("p (h n) -> p h n", h=4)
                tv = ve.do([CP(k4[:, :, 0:64], pv_[:, :, 0:64]),
                            CP(mz[:, t, 768:1024].rearrange("p (h n) -> p h n", h=4), pv_[:, :, 64:128]),
                            CP(k4[:, :, 64:96], bc(Z(t, ML + 384, 32), 4))], tp, tok["cmp"], tok["kk"], xn_free[:])
                bank_free[b] = [tv]
            s2_free[:] = [tp]
            mqv = mz[:, :, 0:384].rearrange("p t (h n) -> p t h n", h=4)
            tv = rope(mqv[:, :, :, 64:96], 16, 0, tq_)
            yield
            for dst, c0 in ((mq, 0), (mk, 384)):
                for hp in range(2):
                    b = take("B")
                    tp = pe.do([tr(ps[0:96, b, 256 * i + 128 * t:256 * i + 128 * t + 128],
                                   mz[:, t, c0 + 96 * (2 * hp + i):c0 + 96 * (2 * hp + i) + 96])
                                for i in range(2) for t in range(2)], tv, bank_free[b])
                    tok["mk"] = ac.do(AC(dst[0:96, 2 * hp:2 * hp + 2, :],
                                         ps[0:96, b, :].rearrange("p (i n) -> p i n", i=2)), tp, tok["sel"], t_hl)
                    bank_free[b] = [tok["mk"]]
            yield
            done = lambda: values(0, lambda h: [(mz[:, 0, 768 + 64 * h:832 + 64 * h], pTs[0][0][:, h, :], 0),
                                                (mz[:, 1, 768 + 64 * h:832 + 64 * h], pTs[0][1][:, h, :], 128)],
                                  tok["mla"], [0])
            yield from attend("mla", lambda h, t: mq[0:96, h, 128 * t:128 * t + 128], lambda h, n: mk[0:96, h, 0:n],
                              96 ** -0.5, causal, None, lambda: tok["mk"], 0, done)

        def fox():
            f = lf[:, 48:56].rearrange("p (t n) -> p t n", t=2)
            g_ = lf[:, 56:64].rearrange("p (t n) -> p t n", t=2)
            ve.do(TT(f, z[:, :, SM + 12:SM + 16], bc(R("fb", 4 * l, 4), 2), ALU.add), t_row)
            tv = ve.do(STT(g_, f, -1.0, f, ALU.mult, ALU.min))
            ac.do(AC(g_, g_, ACT.Exp), tv)
            ta = ac.do(AC(g_, g_, ACT.Ln, bias=1.0))
            tv = ve.do(STT(f, f, 0.0, g_, ALU.min, ALU.subtract), ta)
            yield
            b = take("B")
            tp = pe.do([mm(ps[:, b, 0:4], C("tri"), f[:, 0, :], True, True),
                        mm(ps[:, b, 8:12], C("ones"), f[:, 0, :], True, False),
                        mm(ps[:, b, 8:12], C("tri"), f[:, 1, :], False, True)], tv, bank_free[b])
            fz = foxb.rearrange("p (s h n) -> p s h n", s=2, h=4)
            tc = ve.do(CP(lf[:, 0:8].rearrange("p (t h) -> p t h", t=2),
                          ps[:, b, 0:16].rearrange("p (t h) -> p t h", t=2)[:, :, 0:4]), tp, tok["sel"])
            bank_free[b] = [tc]
            fzf = None
            for t in range(2):
                zq = Z(t, FQ, 256).rearrange("p (h n) -> p h n", h=4)
                zk = Z(t, FQ + 256, 256).rearrange("p (h n) -> p h n", h=4)
                cc = lf[:, 4 * t:4 * t + 4]
                tv = ve.do([TS(fz[:, 0, :, 0:64], zq, 0.125, None, ALU.mult),
                            CP(fz[:, 1, :, 0:64], zk),
                            CP(fz[:, 0, :, 64], cc),
                            TS(fz[:, 1, :, 65], cc, -1.0, None, ALU.mult),
                            lambda e: e.memset(fz[:, 0, :, 65:66], 1.0),
                            lambda e: e.memset(fz[:, 1, :, 64:65], 1.0)], fzf, tok["sel"], tz[4])
                b2 = [take("B"), take("B")]
                for s in range(2):
                    tp = pe.do([tr(ps[0:66, b2[s], 128 * h:128 * h + 128], fz[:, s, h, :]) for h in range(4)], tv,
                               bank_free[b2[s]])
                    tok["fk"] = ac.do(AC((fq, fk)[s][0:66, :, 128 * t:128 * t + 128],
                                         ps[0:66, b2[s], :].rearrange("p (h n) -> p h n", h=4)), tp, tok["mla"])
                    bank_free[b2[s]] = [tok["fk"]]
                fzf = tp
                yield
            s1_free[:] = [tp]
            done = lambda: values(2, lambda h: pv(lambda h: FV + 64 * h, h, 1), [tok["fox"], tz[5]], [1])
            yield from attend("fox", lambda h, t: fq[0:66, h, 128 * t:128 * t + 128], lambda h, n: fk[0:66, h, 0:n],
                              1.0, causal, None, lambda: tok["fk"], 1, done)

        fq, fk = mq, mk
        foxb = s1[:, 0:528]
        sgl = lf[:, 24:48].rearrange("p (t n) -> p t n", t=2)
        nsa_q = lambda h, t: HB(nq, h)[:, h // 2, 128 * t:128 * t + 128]
        dsa_q = lambda h, t: HB(dq, h)[:, h // 2, 128 * t:128 * t + 128]
        kkh = lambda i: (lambda h, n: HB(kk, h)[:, i, 0:n])

        def dsa():
            done = lambda: values(3, lambda h: pv(lambda h: VV + 192, h, 0), tok["dsa"], [0])
            yield from attend("dsa", dsa_q, kkh(2), 0.125, lambda t, n: dmask[:, t, 0:n], None,
                              lambda: [tok["kk"], tok["sel"]], 0, done)

        def nsa_sel():
            yield from attend("nsel", nsa_q, kkh(0), 0.125, causal, sgl[:, :, 4:8], lambda: tok["kk"], 0)

        def nsa_win():
            done = lambda: values(1, lambda h: [(tok["vct"], tok["pcT"][:, h, :], 0)]
                                  + pv(lambda h: VV + 64, h, 0) + pv(lambda h: VV + 128, h, 1),
                                  [tok["cmp"], tok["nsel"], tok["nwin"]], [0, 1])
            yield from attend("nwin", nsa_q, kkh(1), 0.125, causal, sgl[:, :, 8:12], lambda: tok["kk"], 1, done)

        pb_user, pT_user = [None, None], [None, None]
        for _ in heads():
            fill()
        weave([indexer(), compress()], 2, fill)
        weave([nsa_sel(), nsa_win()], 2, fill)
        weave([mla()], 1, fill)
        weave([fox(), dsa()], 2, fill)
        for _ in gen:
            pass
        to_all = [to[n] for n in range(4)]
        dump(f"oT{l}", oTs, to_all)
        tm = [None] * 8
        for n in range(4):
            w = load(t_in["wbr"][l, n], split=False)
            wv = w.raw.rearrange("p (k d) -> p k d", k=2)
            for d in range(0, 8, 2):
                b = take("B")
                tp = pe.do([mm(ps[:, b, 256 * i:256 * i + 256], wv[:, k, 128 * (d + i):128 * (d + i) + 128],
                               oTs[:, n, k, :], k == 0, k == 1) for i in range(2) for k in range(2)],
                           w.landed, to[n], bank_free[b])
                used(w, tp)
                g2 = sgv[:, n, d:d + 2, :]
                mx = mixf[:, d:d + 2, :]
                if n == 0:
                    tv = ve.do(STT(mx, g2, 1.0, two(ps[:, b, :]), ALU.add, ALU.mult), tp, gates, to_all)
                    tm[d] = tv
                else:
                    tv = ve.do(STT(g2, g2, 1.0, two(ps[:, b, :]), ALU.add, ALU.mult), tp)
                    if n < 3:
                        tm[d] = po.do(TT(mx, mx, g2, ALU.add), tv, tm[d])
                    else:
                        tm[d] = ve.do(TT(mx, mx, g2, ALU.add), tm[d])
                        tm[d] = ve.do(TS(mx, mx, 0.5, None, ALU.mult))
                bank_free[b] = [tv]
        oTs_free[:] = [tp]
        pe_all = ("pe", pe.n)
        ts = []
        for d in range(0, 8, 2):
            ts += split_cols(mixf[:, d:d + 2, :], [q[:, d:d + 2, :] for q in H3], tm[d], pe_all)
        barrier()
        hl_free[:] = [pe_all, ("ve", ve.n), ("po", po.n)]
        xn_free[:] = ts
        z_free[:] = [pe_all]
        tx, tp = out_proj(t_in["wout"][l], H3, ts, None, lo="po")
        hT_free[:] = [tp, ("pe", pe.n)]
        dump(f"xa{l}", x, tx)
        fTh, fTl = S["fTh"], S["fTl"]
        th = norm_T(x, tx, K("n2b", 8 * l, 8), None, t_col, hT, H3, hT_free[:])
        f_free = [z_free[:], z_free[:]]
        tf = {}
        for c in range(9):
            if c < 8:
                tf[c] = []
                for j in range(2):
                    b, tp = cols_of(t_in["wup"][l, 2 * c + j], H3, th, lo="ve")
                    r = s2[:, 512 * j:512 * j + 512]
                    ta = ac.do(AC(r, ps[:, b, :], ACT.Relu), tp, s2_free[:], rf[j])
                    bank_free[b] = [ta]
                    r2 = s1[:, 512 * j:512 * j + 512]
                    tv = po.do(TT(r2, r, r, ALU.mult), ta, s1_free[:], rf1[j])
                    rf[j] = tv
                    ss = split_cols(two(r2), [q[:, c % 2, 2 * j:2 * j + 2, :] for q in (fTh, fTl)], tv, f_free[c % 2])
                    rf1[j] = ss
                    tf[c] += ss
            if c >= 1:
                q = c - 1
                for j in range(2):
                    w = load(t_in["wdown"][l, q, :, 2048 * j:2048 * j + 2048], lo="po")
                    wh, wl = kn(w.hi, 2), kn(w.lo, 2)
                    fns = []
                    for t in range(2):
                        for h in range(2):
                            for k in range(2):
                                fns += mm3(ps[:, 2 * t + h, :],
                                           [a[:, q % 2, 2 * j + k, 128 * t:128 * t + 128] for a in (fTh, fTl)],
                                           [a[:, k, 512 * h:512 * h + 512] for a in (wh, wl)],
                                           q == 0 and j == 0 and k == 0, q == 7 and j == 1 and k == 1)
                    tp = pe.do(fns, w.ready, tf[q], [bank_free[b] for b in range(4)] if q == 0 and j == 0 else None)
                    used(w, tp)
                f_free[q % 2] = tp
        hT_free[:] = [tp]
        z_free[:] = [tp]
        s1_free[:] = list(rf1[0]) + list(rf1[1])
        s2_free[:] = [rf[0], rf[1]]
        res = []
        for t in range(2):
            for h in range(2):
                xs = x[:, t, 512 * h:512 * h + 512]
                tt = ve.do(TT(xs, xs, ps[:, 2 * t + h, :], ALU.add), tp)
                bank_free[2 * t + h] = [tt]
                res.append(tt)
        dump(f"xb{l}", x, res)
        return res, pT_user

    rf, rf1 = [None, None], [[], []]
    tx, _ = layer2(0, tx)
    tx, pt = layer2(1, tx)
    t_fg = small(grow[:, 0, :], t_in["rowp"][0:1, 1712:2736].broadcast_to([P, 1024]), *pt)
    tn = norm_rows(x, tx)
    for t in range(2):
        tv = (ve if t else po).do(TT(xn[:, t, :], xn[:, t, :], grow[:, 0, :], ALU.mult), tn, t_fg)
        sp.dma(lambda e, t=t: e.dma_start(out[:, t, :], xn[:, t, :]), "out", 16 * (t + 1), tv)
    return noted, dict(pe=pe, ac=ac, ve=ve, po=po, sp=sp), ndma


def constants(np):
    f = np.float32
    c = np.zeros((P, NCST), f)

    def put(name, v):
        a, n = CST[name]
        c[:, a:a + n] = v

    i = np.arange(P)
    put("ident", np.eye(P))
    put("ones", 1.0)
    put("tri", i[:, None] <= i[None, :])
    put("mask", np.concatenate([np.zeros((P, P)), np.where(i[None, :] <= i[:, None], 0.0, NEG)], 1))
    tok = np.arange(256).reshape(2, P).T
    ok = (16 * np.arange(15) + 31)[None, None, :] <= tok[:, :, None]
    put("cadd", np.where(ok, 0.0, NEG).reshape(P, 30))
    put("cmul", ok.reshape(P, 30))
    inv = (f(10000.0) ** (-np.arange(0, 32, 2, dtype=f) / f(32))).astype(f)
    ra = (tok // 64).astype(f)[:, :, None] * inv
    ca = (tok % 64).astype(f)[:, :, None] * inv
    put("ropc", np.cos(np.concatenate([ra, ra, ca, ca], 2)).reshape(P, 128))
    put("rops", np.concatenate([-np.sin(ra), np.sin(ra), -np.sin(ca), np.sin(ca)], 2).reshape(P, 128))
    put("inv", np.concatenate([(f(500000.0) ** (-np.arange(0, r, 2, dtype=f) / f(r))).astype(f)
                               for r in (32, 16, 8)]))
    pm = np.zeros((256, 4, 256), f)
    for g, w in enumerate((2, 4, 8, 16)):
        for t in range(256):
            lo, hi = max(t - w // 2, 0), min(t + w - w // 2, 256)
            pm[lo:hi, g, t] = f(1.0) / f(hi - lo)
            pm[t, g, t] -= f(1.0)
    return c, pm.reshape(2, P, 4, 256).transpose(1, 0, 2, 3).reshape(P, 2048)


def layout(np, i):
    def rows(w, n):
        k, m = w.shape[-2] // P, w.shape[-1] // n
        lead = w.shape[:-2]
        w = w.reshape(*lead, k, P, m, n)
        r = len(lead)
        return np.ascontiguousarray(np.transpose(w, (*range(r), r + 2, r + 1, r, r + 3)).reshape(*lead, m, P, k * n))

    def cols(v):
        return v.reshape(-1, P).T

    a = {k: np.asarray(v) for k, v in i.items()}
    d = {}
    c, pm = constants(np)
    d["cst"], d["pm"] = c, pm
    colp = np.zeros((P, NCOL), np.float32)

    def put(name, v):
        b, n = COL[name]
        colp[:v.shape[0], b:b + n] = v

    put("n1a", cols(a["norm1_g"]))
    put("n2a", cols(a["norm2_g"]))
    put("n1b", cols(a["norm1_g_2"]))
    put("n2b", cols(a["norm2_g_2"]))
    put("modb", cols(a["mod_b"]))
    put("c", cols(a["c"]))
    put("cc", cols(a["c_ctx"]))
    put("ps", cols(a["pool_scale"]))
    put("cw", cols(a["conv_w"]))
    put("sgw", a["sg_w"][0].transpose(2, 0, 1).reshape(P, 512))
    put("plw", a["pool_w"][0].transpose(1, 0, 2).reshape(P, 512))
    r = np.concatenate([a["router_g_w"], a["router_e_w"]], 2)
    put("rw", r.reshape(2, 8, P, 20).transpose(2, 0, 1, 3).reshape(P, 320))
    put("gq", cols(a["mla_q_norm_g_2"]))
    put("gkv", cols(a["mla_kv_norm_g_2"]))
    put("pe", a["nsa_cmp_pe_2"].transpose(3, 0, 1, 2).reshape(64, 128))
    d["colp"] = colp
    kg = a["k_gain"].reshape(-1)
    qg = a["q_gain"].reshape(-1)
    gb = a["mod_b"].reshape(2, 6, 1024)[:, [2, 5], :].reshape(-1)
    rb = np.concatenate([a["router_g_b"], a["router_e_b"]], 1).reshape(-1)
    d["rowp"] = np.concatenate([np.tile(qg, 8), np.tile(kg, 2), a["sg_gain"].reshape(-1), a["sg_b"].reshape(-1),
                                rb, a["fox_f_bias_2"].reshape(-1), a["final_g_2"], gb]).reshape(1, NROW)
    d["x"] = np.ascontiguousarray(a["x"].reshape(2, P, 1024).transpose(1, 0, 2))
    d["ctx"] = np.ascontiguousarray(a["ctx"].reshape(2, P, 1024).transpose(1, 0, 2))
    d["pos"] = np.ascontiguousarray(a["positions_2"].reshape(2, P).T)
    d["wmod"] = rows(a["mod_w"], 512)
    w = a["even_w_in"][0]
    q = w[:, 0:512].reshape(1024, 2, 4, 64).transpose(0, 2, 1, 3).reshape(1024, 512)
    d["we_q"] = rows(q, 512)[0]
    d["we_kv"] = rows(w[:, 512:768], 256)[0]
    d["we_p"] = rows(w[:, 768:1280], 512)[0]
    w = a["even_w_out"][0]
    w = np.concatenate([w[0:512].reshape(2, 4, 64, 1024).transpose(1, 0, 2, 3).reshape(512, 1024), w[512:]], 0)
    d["we_out"] = rows(w, 512)
    w = a["odd_w_in"][0]
    d["wo_v"] = rows(w[:, 512:1024], 512)[0]
    for name, c0 in (("u", 0), ("hx", 1024), ("bg", 1536), ("cg", 2048)):
        d["wo_" + name] = rows(w[:, c0:c0 + 512], 256)
    d["wo_out"] = rows(a["odd_w_out"][0], 512)
    gu = np.stack([a["w_gate"], a["w_up"]], 2)
    d["wgu"] = np.ascontiguousarray(gu.reshape(2, 16, 2, 8, P, 256).transpose(0, 1, 4, 2, 3, 5)).reshape(2, 16, P, 4096)
    d["wdn"] = np.ascontiguousarray(a["w_down"].reshape(2, 8, 2, 2, P, 1024).transpose(0, 1, 4, 2, 3, 5)
                                    ).reshape(2, 8, P, 4096)
    w = a["w_in_2"]
    m, n, f, s = 0, 416, 1068, 1840
    order = [(s + 384, 288), (n + 640, 12), (f + 768, 4), (s + 672, 8),
             (n, 256), (n + 256, 64), (n + 384, 64), (n + 512, 64), (s, 256), (s + 256, 64),
             (n + 320, 64), (n + 448, 64), (n + 576, 64), (s + 320, 64),
             (m, 416), (f, 512), (f + 512, 256)]
    zw = np.concatenate([w[:, :, b:b + k] for b, k in order], 2)
    parts, b = [], 0
    for k in ZW:
        parts.append(zw[:, :, b:b + k].reshape(2, 8, P, k).transpose(0, 2, 1, 3).reshape(2, P, 8 * k))
        b += k
    d["wz"] = np.concatenate(parts, 2)
    g = w[:, :, 2520:].reshape(2, 8, P, 2, 2, 8, P)
    d["wgt"] = np.ascontiguousarray(g.transpose(0, 5, 3, 2, 1, 4, 6)).reshape(2, 8, 2, P, 2048)
    d["wmla"] = np.concatenate([a["mla_w_uq_2"].reshape(2, 2, P, 384).transpose(0, 2, 1, 3).reshape(2, P, 768),
                                a["mla_w_ukv_2"]], 2)
    d["wcmp"] = np.ascontiguousarray(a["nsa_cmp_w_2"].reshape(2, 2, 32, 64, 64).transpose(0, 3, 1, 2, 4)
                                     ).reshape(2, 64, 4096)
    d["wbr"] = np.ascontiguousarray(a["w_branch_2"].reshape(2, 4, 2, P, 1024).transpose(0, 1, 3, 2, 4)
                                    ).reshape(2, 4, P, 2048)
    d["wout"] = rows(a["w_out_2"], 512)
    d["wup"] = rows(a["w_up_2"], 256)
    d["wdown"] = np.ascontiguousarray(a["w_down_2"].reshape(2, 8, 4, P, 1024).transpose(0, 1, 3, 2, 4)
                                      ).reshape(2, 8, P, 4096)
    return d


def kernel(**inputs):
    import numpy as np
    from concourse import bacc
    from concourse.bass_utils import run_bass_kernel_spmd

    arrays = layout(np, inputs)
    nc = bacc.Bacc("TRN2", target_bir_lowering=False, num_devices=1)
    t_in = {k: nc.dram_tensor(f"in_{k}", v.shape, mybir.dt.from_np(v.dtype), kind="ExternalInput").ap()
            for k, v in arrays.items()}
    out = nc.dram_tensor("out_x", (P, 2, 1024), F32, kind="ExternalOutput").ap()
    build(nc, t_in, out)
    r = run_bass_kernel_spmd(nc, [{f"in_{k}": v for k, v in arrays.items()}], core_ids=[0])
    y = r.results[0]["out_x"]
    return y.transpose(1, 0, 2).reshape(1, 256, 1024)
```

```python
from contextlib import ExitStack
from itertools import chain

from concourse import mybir
from concourse.alu_op_type import AluOpType as ALU

F32 = mybir.dt.float32
I32 = mybir.dt.int32
ACT = mybir.ActivationFunctionType
AX = mybir.AxisListType.X
P = 128
EPS = 1e-6
NEG = -1e30
TWO_PI = 6.283185307179586
PIECE = 2048
NRAW = 4
NHL = 3
F32R = mybir.dt.float32r
ZW = (312, 512, 512, 416, 512, 256)

CST = dict(ident=(0, 128), ones=(128, 128), tri=(256, 128), mask=(384, 256), cadd=(640, 30),
           cmul=(670, 30), ropc=(700, 128), rops=(828, 128), inv=(956, 28))
NCST = 984
COL = dict(n1a=(0, 16), n2a=(16, 16), n1b=(32, 16), n2b=(48, 16), modb=(64, 96), c=(160, 8),
           cc=(168, 8), ps=(176, 4), cw=(180, 12), sgw=(192, 512), plw=(704, 512),
           rw=(1216, 320), gq=(1536, 4), gkv=(1540, 2), pe=(1542, 128))
NCOL = 1670
ROW = dict(qkg=(0, 640), sgg=(640, 512), sgb=(1152, 512), rb=(1664, 40), fb=(1704, 8),
           fg=(1712, 1024), gb=(2736, 4096))
NROW = 6832
RKEEP = 1712


class Engine:

    def __init__(self, key, chained):
        self.key, self.chained, self.n, self.queue = key, chained, 0, []

    def do(self, fns, *after):
        fns = fns if isinstance(fns, list) else [fns]
        if self.chained and self.n:
            after = (*after, (self.key, self.n))
        self.n += 1
        self.queue.append((after, fns, self.key, 1))
        return (self.key, self.n)

    def dma(self, fn, key, count, *after):
        self.queue.append((after, [fn], key, 16))
        return (key, count)


def tokens(after):
    for t in after:
        if t is None:
            continue
        if callable(t):
            yield from tokens([t()])
        elif isinstance(t, (list, dict)):
            yield from tokens(list(t.values()) if isinstance(t, dict) else t)
        else:
            yield t


def replay(engine, unit, sems):
    seen = {}
    for after, fns, key, inc in engine.queue:
        need = {}
        for k, v in tokens(after):
            need[k] = max(need.get(k, 0), v)
        for k, v in need.items():
            if seen.get(k, 0) < v:
                unit.wait_ge(sems[k], v)
                seen[k] = v
        for fn in fns:
            ins = fn(unit)
        ins.then_inc(sems[key], inc)


class Chunk:
    pass


def build(nc, t_in, out):
    with ExitStack() as ctx:
        base = nc.sbuf_base + (-nc.sbuf_base) % 64
        arena = ctx.enter_context(nc.sbuf_tensor("arena", [P, 52500], F32))
        del arena
        where = [base]

        def at(name, off, *shape, dt=F32, parts=P):
            return nc.alloc_sbuf_tensor_at(name, [parts, *shape], dt, offset=off)

        def sb(name, *shape, dt=F32, parts=P):
            n = 1
            for d in shape:
                n *= d
            off = where[0]
            where[0] += 4 * n + (-4 * n) % 32
            return at(name, off, *shape, dt=dt, parts=parts)

        S = {}
        S["cst"] = sb("cst", NCST)
        S["col"] = sb("col", NCOL)
        S["row"] = sb("row", RKEEP)
        S["mcol"] = sb("mcol", 64)
        S["sil"] = sb("sil", 16)
        S["st"] = sb("st", 160)
        S["cadj"] = sb("cadj", 4, 8)
        S["rt"] = sb("rt", 400)
        S["lf"] = sb("lf", 64)
        S["posi"] = sb("posi", 2, dt=I32)
        S["tab16"] = sb("tab16", 256, parts=16)
        S["x"] = sb("x", 2, 1024)
        S["xn"] = sb("xn", 2, 1024)
        S["s1"] = sb("s1", 1024)
        S["s2"] = sb("s2", 1024)
        S["grow"] = sb("grow", 2, 1024)
        S["acc"] = sb("acc", 2, 512)
        S["hT"] = sb("hT", 8, 256)
        S["raw"] = [sb(f"raw{i}", PIECE) for i in range(NRAW)]
        hl = where[0]
        S["hi"], S["lo"] = [], []
        for i in range(NHL):
            S["hi"].append(sb(f"hi{i}", PIECE, dt=F32R))
            S["lo"].append(sb(f"lo{i}", PIECE, dt=F32R))
        S["hTh"] = sb("hTh", 8, 256, dt=F32R)
        S["hTl"] = sb("hTl", 8, 256, dt=F32R)
        ye = where[0]
        S["yTh"] = sb("yTh", 8, 256, dt=F32R)
        S["yTl"] = sb("yTl", 8, 256, dt=F32R)
        ze = where[0]
        S["z"] = sb("z", 2, 2520)
        S["big"] = at("big", hl, 8192)
        S["ar"] = at("ar", hl + 4 * 8192, 8192)
        S["oTs"] = at("oTs", ye, 2048)
        S["ff"] = at("ff", ye + 8192, 2048)
        S["yf"] = at("yf", ze, 2048)
        S["hidh"] = at("hidh", ze, 2, 2, 256, dt=F32R)
        S["hidl"] = at("hidl", ze + 4096, 2, 2, 256, dt=F32R)
        S["ex"] = at("ex", ze + 8192, 2048)
        S["fTh"] = at("fTh", ze, 2, 4, 256, dt=F32R)
        S["fTl"] = at("fTl", ze + 8192, 2, 4, 256, dt=F32R)
        assert where[0] <= base + 4 * 52500
        S["ps"] = ctx.enter_context(nc.psum_tensor("ps", [P, 8, 512], F32))

        plan = emit(S, t_in, out, None)[0]
        _, engines, ndma = emit(S, t_in, out, plan)
        sems = {k: ctx.enter_context(nc.semaphore(f"s_{k}")) for k in
                ["pe", "ac", "ve", "po", "out", *[f"w{i}" for i in range(NRAW)],
                 *[f"d{i + 1}" for i in range(ndma)]]}
        block = ctx.enter_context(nc.Block())

        @block.sync
        def _(e):
            replay(engines["sp"], e, sems)
            e.wait_ge(sems["out"], 32)

        @block.tensor
        def _(e):
            replay(engines["pe"], e, sems)

        @block.scalar
        def _(e):
            replay(engines["ac"], e, sems)

        @block.vector
        def _(e):
            replay(engines["ve"], e, sems)

        @block.gpsimd
        def _(e):
            replay(engines["po"], e, sems)


def emit(S, t_in, out, plan):
    pe, ac, ve, po, sp = (Engine("pe", False), Engine("ac", True), Engine("ve", True),
                          Engine("po", True), Engine("sp", False))
    cst, col, row, mcol, sil, st, cadj, rt, lf, posi, tab16, x, xn, s1, s2, grow, acc, hT, z, big, ar, ps = (
        S[k] for k in ("cst", "col", "row", "mcol", "sil", "st", "cadj", "rt", "lf", "posi", "tab16", "x", "xn",
                       "s1", "s2", "grow", "acc", "hT", "z", "big", "ar", "ps"))
    H3, Y3 = (S["hTh"], S["hTl"]), (S["yTh"], S["yTl"])

    def C(name):
        a, n = CST[name]
        return cst[:, a:a + n]

    def K(name, a=0, n=None):
        b, m = COL[name]
        return col[:, b + a:b + (m if n is None else a + n)]

    def R(name, a=0, n=None):
        b, m = ROW[name]
        return row[:, b + a:b + (m if n is None else a + n)]

    bank_free = [[] for _ in range(8)]
    turn = dict(A=0, B=0)

    def take(pool):
        b = (0 if pool == "A" else 4) + turn[pool]
        turn[pool] = (turn[pool] + 1) % 4
        return b

    def take2():
        b = 0 if turn["A"] in (0, 3) else 2
        turn["A"] = (b + 2) % 4
        return b

    def mm(o, l, r, first, last):
        return lambda e: e.matmul(o, l, r, start=first, stop=last)

    def mm3(o, l, r, first, last):
        return [mm(o, l[0], r[0], first, False), mm(o, l[0], r[1], False, False), mm(o, l[1], r[0], False, last)]

    def tr(o, i, n=P):
        return lambda e: e.transpose(o, i, C("ident")[0:n, 0:n])

    def bc(ap, n, at=1):
        a = ap.unsqueeze(at)
        return a.broadcast_to([*a.shape[:at], n, *a.shape[at + 1:]])

    def TT(o, a, b, op):
        return lambda e: e.tensor_tensor(o, a, b, op)

    def TS(o, a, x1, x2, op0, op1=None):
        if op1 is None:
            return lambda e: e.tensor_scalar(o, a, x1, None, op0)
        return lambda e: e.tensor_scalar(o, a, x1, x2, op0, op1)

    def STT(o, a, s, b, op0, op1):
        return lambda e: e.scalar_tensor_tensor(out=o, in0=a, scalar=s, in1=b, op0=op0, op1=op1)

    def CP(o, a):
        return lambda e: e.tensor_copy(o, a)

    def AC(o, a, f=ACT.Copy, **kw):
        return lambda e: e.activation(o, a, f, **kw)

    def RED(o, i, op):
        return lambda e: e.tensor_reduce(o, i, AX, op)

    def ADDMAX(o, a, b, m):
        return lambda e: e.tensor_tensor_reduce(o, a, b, 1.0, -3e38, ALU.add, ALU.max, m)

    def RCP(o):
        return lambda e: e.reciprocal(o, o)

    two = lambda a: a.rearrange("p (g n) -> p g n", g=2)
    kn = lambda a, k: a.rearrange("p (k n) -> p k n", k=k)

    noted = []
    chunks = {}
    at_chunk = [0]
    state = dict(dma=0, split=0)
    split_at = []
    hl_free = [[] for _ in range(NHL)]
    next_slot = [0]
    slot_user = {}

    def chunk(n):
        if n not in chunks:
            c = chunks[n] = Chunk()
            c.free = c.pe = None
            c.ready = None
        return chunks[n]

    raw_no = {}

    def send_loads(upto):
        while state["dma"] < min(upto, len(noted) if plan is None else len(plan)):
            m = state["dma"]
            state["dma"] += 1
            item = (noted if plan is None else plan)[m]
            if item is None:
                continue
            src, parts, _, _ = item
            c = chunk(m)
            r = len(raw_no)
            raw_no[m] = r
            order.append(m)
            buf = S["raw"][r % NRAW]
            w = src.shape[1]
            c.raw = buf[0:parts, 0:w]
            c.landed = (f"w{r % NRAW}", 16 * (r // NRAW + 1))
            before = chunk(order[r - NRAW]) if r >= NRAW else None
            sp.dma(lambda e, c=c, src=src: e.dma_start(c.raw, src), *c.landed,
                   (lambda before=before: before.free) if before is not None else None)

    order = []

    def send_splits(n, most=NHL):
        items = noted if plan is None else plan
        accs = 0
        past = sum(1 for i in split_at if i < n)
        while state["split"] < len(items):
            m = state["split"]
            item = items[m]
            if item is None or (m > n and len(split_at) - past >= most):
                break
            src, parts, split, how = item
            if split and len(split_at) - past >= most:
                break
            send_loads(m + 1)
            r = raw_no[m]
            if m > n and r >= NRAW and chunk(order[r - NRAW]).free is None:
                break
            if not split and how is not None:
                if how[2] == 0 and acc_user(how[1] % 2) is None or accs == acc_limit[0] and m > n:
                    assert m > n
                    break
                accs += 1
            state["split"] = m + 1
            c = chunk(m)
            if not split:
                if how is not None:
                    c.free = [adaln_acc(c, *how)]
                continue
            k = next_slot[0]
            next_slot[0] = (k + 1) % NHL
            split_at.append(m)
            w = src.shape[1]
            c.hi, c.lo = S["hi"][k][:, 0:w], S["lo"][k][:, 0:w]
            before = slot_user.get(k)
            slot_user[k] = c
            wait = (lambda before=before: before.pe) if before is not None else None
            th = ac.do(AC(c.hi, c.raw), c.landed, wait, hl_free[k])
            eng = po if how == "po" else ve
            tl = eng.do(TT(c.lo, c.raw, c.hi.bitcast(F32), ALU.subtract), th)
            c.ready = [th, tl]
            c.free = [th, tl]

    def load(src, parts=P, split=True, lo="ve"):
        noted.append((src, parts, split, lo if split else None))
        return loaded(split)

    def load_acc(src, how):
        noted.append((src, P, False, how))
        return loaded(False)

    def loaded(split):
        n = at_chunk[0]
        at_chunk[0] += 1
        send_loads(n + 1)
        send_splits(n)
        send_loads(n + 1 + NRAW)
        c = chunk(n)
        if not split:
            c.ready = [c.landed]
        return c

    def barrier():
        noted.append(None)
        assert state["split"] == at_chunk[0]
        at_chunk[0] += 1
        state["split"] = at_chunk[0]
        next_slot[0] = NHL - 1
        send_loads(at_chunk[0])

    def ahead(most):
        send_loads(at_chunk[0] + NRAW)
        send_splits(at_chunk[0], most)

    def used(c, t):
        c.pe = t
        if c.free is None or c.free_is_pe:
            c.free, c.free_is_pe = [t], True

    Chunk.free_is_pe = False

    ndma = 0

    def small(dst, src, *after):
        nonlocal ndma
        ndma += 1
        return sp.dma(lambda e: e.dma_start(dst, src), f"d{ndma}", 16, *after)

    zf = z[:, :, :].rearrange("p t n -> p (t n)")
    cx = zf[:, 0:2048].rearrange("p (t n) -> p t n", t=2)
    t_c = small(sil[:, :], t_in["colp"][:, 160:176])
    send_loads(2)
    t_cst = small(cst[:, :], t_in["cst"])
    send_loads(4)
    t_col = small(col[:, :], t_in["colp"])
    t_x = small(x[:, :, :], t_in["x"])
    t_cx = small(cx, t_in["ctx"])

    t = ac.do(AC(st[:, 0:16], sil[:, :], ACT.Exp, scale=-1.0), t_c)
    ve.do(TS(st[:, 0:16], st[:, 0:16], 1.0, None, ALU.add), t)
    ve.do(RCP(st[:, 0:16]))
    t_sil = ve.do(TT(sil[:, :], sil[:, :], st[:, 0:16], ALU.mult))

    r2_free = [None, None]
    acc_used, acc_last, acc_limit = {}, [None, None], [1]
    t_mcol, t_grow, t_gb = {}, {}, {}

    def acc_user(a):
        return [] if acc_last[a] is None else acc_used.get(acc_last[a])

    def adaln_acc(c, l, piece, i, eng):
        a = piece % 2
        wv = kn(c.raw, 4)
        if i == 0:
            before, acc_last[a] = acc_user(a), (l, piece)
        if eng == "po":
            s = sil[:, 4 * i:4 * i + 4].unsqueeze(2).broadcast_to([P, 4, 512])
            po.do(TT(wv, wv, s, ALU.mult), c.landed, t_sil)
            po.do(TT(c.raw[:, 0:1024], c.raw[:, 0:1024], c.raw[:, 1024:2048], ALU.add))
            if i == 0:
                return po.do(TT(acc[:, a, :], wv[:, 0, :], wv[:, 1, :], ALU.add), before)
            po.do(TT(wv[:, 0, :], wv[:, 0, :], wv[:, 1, :], ALU.add))
            return po.do(TT(acc[:, a, :], acc[:, a, :], wv[:, 0, :], ALU.add))
        for k in range(4):
            s = sil[:, 4 * i + k:4 * i + k + 1]
            if i == k == 0:
                t = ve.do(TS(acc[:, a, :], wv[:, k, :], s, None, ALU.mult), c.landed, t_sil, before)
            else:
                t = ve.do(STT(acc[:, a, :], wv[:, k, :], s, acc[:, a, :], ALU.mult, ALU.add), c.landed)
        return t

    def part_of(piece):
        part, half = piece // 2, piece % 2
        return part, half, {0: 0, 1: 1, 3: 2, 4: 3}.get(part)

    def adaln_gate(l, piece, b, tp):
        part, half, _ = part_of(piece)
        g = 0 if part == 2 else 1
        dst = grow[:, g, 512 * half:512 * half + 512]
        tv = ve.do(TT(dst, dst, ps[:, b, :], ALU.add), tp, t_gb[(l, g)])
        bank_free[b] = [tv]
        t_grow[(l, g, half)] = tv

    def adaln_sum(l, piece, eng="ve"):
        part, half, j = part_of(piece)
        for i in range(2):
            c = load_acc(t_in["wmod"][l, piece, :, 2048 * i:2048 * i + 2048], (l, piece, i, eng))
        a, t = piece % 2, c.free

        def rest():
            b = take("B")
            if j is None:
                tp = pe.do([mm(ps[:, b, :], C("ones"), acc[:, a, :], True, True)], t, t_cst, bank_free[b])
                acc_used[(l, piece)] = tp
                adaln_gate(l, piece, b, tp)
            else:
                tp = pe.do([mm(ps[:, b, q:q + 1], acc[:, a, 128 * q:128 * q + 128], C("ones")[:, 0:1], True, True)
                            for q in range(4)], t, t_cst, bank_free[b])
                acc_used[(l, piece)] = tp
                m0 = 32 * l + 8 * j + 4 * half
                tv = ve.do(TT(mcol[:, m0:m0 + 4], ps[:, b, 0:4], K("modb", 48 * l + 8 * part + 4 * half, 4), ALU.add),
                           tp, t_col)
                bank_free[b] = [tv]
                t_mcol[(l, j)] = tv
        return rest

    def adaln_pe(l, piece, cdst=None):
        part, half, j = part_of(piece)
        sv = sil[:, :].rearrange("p (w k) -> p w k", w=2)
        b = take("B")
        for i in range(2):
            w = load(t_in["wmod"][l, piece, :, 2048 * i:2048 * i + 2048], split=False)
            wv = kn(w.raw, 4)
            fns = []
            for k in range(4):
                o = 4 * i + k
                if j is None:
                    fns.append(mm(ps[:, b, :], sil[:, o:o + 1].broadcast_to([P, P]), wv[:, k, :], o == 0, o == 7))
                else:
                    fns.append(mm(ps[0:2, b, :], sv[:, :, o], wv[:, k, :], o == 0, o == 7))
            tp = pe.do(fns, w.landed, t_sil, bank_free[b] if i == 0 else None)
            used(w, tp)
        a = piece % 2
        if j is not None:
            r2 = xn[0:2, a, 0:512]
            ta = ac.do(AC(r2, ps[0:2, b, :]), tp, r2_free[a])
            bank_free[b] = [ta]

        def rest():
            if j is None:
                adaln_gate(l, piece, b, tp)
                return None
            b2 = take("B")
            r2_free[a] = tr_ = pe.do([tr(ps[:, b2, 2 * q:2 * q + 2], r2[:, 128 * q:128 * q + 128], 2) for q in range(4)], ta,
                                t_cst, bank_free[b2])
            m0 = 32 * l + 8 * j + 4 * half
            bias = K("modb", 48 * l + 8 * part + 4 * half, 4)
            pv2 = ps[:, b2, 0:8].rearrange("p (q w) -> p q w", w=2)
            fns = [TT(mcol[:, m0:m0 + 4], pv2[:, :, 0], bias, ALU.add)]
            if cdst is not None:
                fns.append(TT(cdst, pv2[:, :, 1], bias, ALU.add))
            t_mcol[(l, j)] = t = ve.do(fns, tr_, t_col)
            bank_free[b2] = [t]
            return t
        return rest

    def gate_bias(l, g, *free):
        n0 = 2736 + (2 * l + g) * 1024
        t_gb[(l, g)] = small(grow[:, g, :], t_in["rowp"][0:1, n0:n0 + 1024].broadcast_to([P, 1024]), *free)

    def rstd(dst, ss, inv_n, tmp, *after):
        ve.do(TS(ss, ss, inv_n, EPS, ALU.mult, ALU.add), *after)
        ve.do(TS(tmp.bitcast(I32), ss.bitcast(I32), 1, None, ALU.arith_shift_right))
        ve.do(TS(dst.bitcast(I32), tmp.bitcast(I32), -1.0, 1597463007.0, ALU.mult, ALU.add))
        for _ in range(3):
            ve.do(STT(tmp, dst, -0.5, dst, ALU.mult, ALU.mult))
            ve.do(TT(tmp, tmp, ss, ALU.mult))
            t = ve.do(STT(dst, tmp, 1.5, dst, ALU.add, ALU.mult))
        return t

    hT_free, xn_free, s1_free, s2_free = [], [], [], []

    def norm_stats(src, after, buf=s1, c0=0, *free):
        q = buf[:, 0:512]
        for h in range(2):
            for t in range(2):
                ta = ac.do(AC(q, src[:, t, 512 * h:512 * h + 512], ACT.Square,
                              accum_out=st[:, c0 + 2 * h + t:c0 + 2 * h + t + 1]),
                           after[2 * h + t] if isinstance(after, list) else after, *free)
        ss = st[:, c0:c0 + 2]
        ve.do(TT(ss, ss, st[:, c0 + 2:c0 + 4], ALU.add), ta)
        return st[:, c0 + 4:c0 + 6], rstd(st[:, c0 + 4:c0 + 6], ss, 1.0 / 1024, st[:, c0 + 6:c0 + 8])

    def norm_diag(src, after, buf=s1, c0=0, *free):
        r, t_r = norm_stats(src, after, buf, c0, *free)
        dg = buf[:, 512:768].rearrange("p (t n) -> p t n", t=2)
        return dg, ve.do([TS(dg[:, t, :], C("ident"), r[:, t:t + 1], None, ALU.mult) for t in range(2)], t_r, t_cst,
                         *free)

    def norm_T(src, diag, scale, shift, t_sc, f32, parts, *free):
        dg, t_d = diag
        res = {}
        for k in range(0, 8, 2):
            b = take("B")
            tp = pe.do([mm(ps[:, b, 256 * j + 128 * t:256 * j + 128 * t + 128],
                           src[:, t, 128 * (k + j):128 * (k + j) + 128], dg[:, t, :], True, True)
                        for j in range(2) for t in range(2)], t_d, bank_free[b])
            fns = []
            for j in range(2):
                i, o = ps[:, b, 256 * j:256 * j + 256], f32[:, k + j, :]
                sc = scale[:, k + j:k + j + 1]
                sh = 0.0 if shift is None else shift[:, k + j:k + j + 1]
                if k % 4:
                    fns.append(AC(o, i, scale=sc) if shift is None else AC(o, i, ACT.Identity, scale=sc, bias=sh))
                else:
                    fns.append(TS(o, i, sc, None, ALU.mult) if shift is None else TS(o, i, sc, sh, ALU.mult, ALU.add))
            tv = (ac if k % 4 else ve).do(fns, tp, t_sc, *free)
            bank_free[b] = [tv]
            f, hi, lo = (q[:, k:k + 2, :] for q in (f32, *parts))
            ta = ac.do(AC(hi, f), tv, *free)
            tl = (po if k % 4 else ve).do(TT(lo, f, hi.bitcast(F32), ALU.subtract), ta, *free)
            res[k // 2] = [ta, tv, tl]
        s1_free[:] = [tp]
        return res

    def split_cols(f, parts, *after):
        th = ac.do(AC(parts[0], f), *after)
        tl = ve.do(TT(parts[1], f, parts[0].bitcast(F32), ALU.subtract), th, *after)
        return [th, tl]

    def pair(t, k):
        return t[k // 2] if isinstance(t, dict) else t

    def cond_scale(l, which, norm, dst):
        sc = mcol[:, 32 * l + 16 * which + 8:32 * l + 16 * which + 16]
        return ve.do(STT(dst, sc, 1.0, norm, ALU.add, ALU.mult), t_mcol[(l, 2 * which + 1)], t_col)

    def rows_of(src, wd, jobs, lo="ve", pool="B"):
        banks = [take(pool) for _ in jobs]
        for i in range(2):
            w = load(src[:, 4 * wd * i:4 * wd * i + 4 * wd], lo=lo)
            wh, wl = kn(w.hi, 4), kn(w.lo, 4)
            toks = []
            for b, (hs, t_h, tile) in zip(banks, jobs):
                for k in range(4):
                    lh = [q[:, 4 * i + k, 128 * tile:128 * tile + 128] for q in hs]
                    tp = pe.do(mm3(ps[:, b, 0:wd], lh, (wh[:, k, :], wl[:, k, :]), i == k == 0, i == 1 and k == 3),
                               w.ready, pair(t_h, 4 * i + k), bank_free[b] if i == 0 else None)
                toks.append(tp)
            used(w, toks[-1])
        return list(zip(banks, toks))

    def cols_of(src, hs, t_h, lo="ve"):
        w = load(src, lo=lo)
        wh, wl = kn(w.hi, 8), kn(w.lo, 8)
        b = take("B")
        for i in range(2):
            for k in range(8):
                tp = pe.do(mm3(ps[:, b, 256 * i:256 * i + 256], [q[:, k, 128 * i:128 * i + 128] for q in (wh, wl)],
                               [q[:, k, :] for q in hs], k == 0, k == 7), w.ready, pair(t_h, k), bank_free[b])
        used(w, tp)
        return b, tp

    def out_proj(srcs, ys, t_y, gate, lo="ve"):
        res = []
        for h in range(2):
            for t, (b, tp) in enumerate(rows_of(srcs[h], 512, [(ys, t_y, 0), (ys, t_y, 1)], lo=lo)):
                xs = x[:, t, 512 * h:512 * h + 512]
                if gate is None:
                    tt = ve.do(TT(xs, xs, ps[:, b, :], ALU.add), tp)
                else:
                    gl, g = gate
                    ve.do(TT(s2[:, 0:512], ps[:, b, :], grow[:, g, 512 * h:512 * h + 512], ALU.mult), tp,
                          t_grow[(gl, g, h)], s2_free[:])
                    tt = ve.do(TT(xs, xs, s2[:, 0:512], ALU.add))
                bank_free[b] = [tt]
                res.append(tt)
        return res, tp

    def weave(tasks, width, filler):
        live, tasks = [], list(tasks)
        while live or tasks:
            while tasks and len(live) < width:
                live.append(tasks.pop(0))
            for g in list(live):
                if next(g, "end") == "end":
                    live.remove(g)
                else:
                    filler()

    dgx = norm_diag(x, t_x, s1, 0, t_sil)
    dgc = norm_diag(cx, t_cx, s2, 32)
    ctx_pieces, before = [], None
    for piece in range(4):
        part, half = piece // 2, piece % 2
        rest = adaln_pe(0, piece, cadj[:, part, 4 * half:4 * half + 4])
        if before is not None:
            ctx_pieces.append(before())
        before = rest
    ctx_pieces.append(before())
    t_row = small(row[:, :], t_in["rowp"][0:1, 0:RKEEP].broadcast_to([P, RKEEP]))
    t_pos = small(posi[:, :], t_in["pos"])
    gate_bias(0, 0)
    gate_bias(0, 1)
    t_cc = ve.do(STT(cadj[:, 2, :], cadj[:, 1, :], 1.0, K("n1a", 0, 8), ALU.add, ALU.mult), *ctx_pieces)
    t_sc = cond_scale(0, 0, K("n1a", 0, 8), cadj[:, 3, :])
    th = norm_T(x, dgx, cadj[:, 3, :], mcol[:, 0:8], t_sc, hT, H3)
    thc = norm_T(cx, dgc, cadj[:, 2, :], cadj[:, 0, :], t_cc,
                 zf[:, 2048:4096].rearrange("p (k n) -> p k n", k=8), Y3)
    tz = []
    r = rows_of(t_in["we_kv"], 256, [(H3, th, 0), (H3, th, 1), (Y3, thc, 0), (Y3, thc, 1)], lo="po")
    for i, (b, tp) in enumerate(r):
        c0 = 512 if i < 2 else 1280
        tt = ve.do(CP(z[:, i % 2, c0:c0 + 256], ps[:, b, 0:256]), tp, thc, ("pe", pe.n))
        bank_free[b] = [tt]
    for t, (b, tp) in enumerate(rows_of(t_in["we_q"], 512, [(H3, th, 0), (H3, th, 1)])):
        tt = ve.do(CP(z[:, t, 0:512], ps[:, b, :]), tp)
        bank_free[b] = [tt]
    t_qk = tt
    for t, (b, tp) in enumerate(rows_of(t_in["we_p"], 512, [(H3, th, 0), (H3, th, 1)], lo="po")):
        tt = ac.do(AC(z[:, t, 768:1280], ps[:, b, :]), tp)
        bank_free[b] = [tt]
        tz.append(tt)
    hT_free[:] = [tp]
    yT_free = [tp]
    barrier()
    t_hl = tp
    first = [adaln_pe(0, piece) for piece in (4, 5)]
    s1_free[:] = []
    for t in range(2):
        ve.do(TT(s1[:, 0:640], z[:, t, 0:640], z[:, t, 0:640], ALU.mult), s1_free[:], t_qk)
        ve.do(RED(st[:, 8 + 12 * t:18 + 12 * t], s1[:, 0:640].rearrange("p (h d) -> p h d", d=64), ALU.add))
        ve.do(TT(s1[:, 640:768], z[:, t, 1280:1408], z[:, t, 1280:1408], ALU.mult))
        t_r = ve.do(RED(st[:, 18 + 12 * t:20 + 12 * t], s1[:, 640:768].rearrange("p (h d) -> p h d", d=64), ALU.add))
    t_r = rstd(st[:, 32:56], st[:, 8:32], 1.0 / 64, st[:, 56:80], t_r)
    qT = big[:, 0:1024].rearrange("p (i n) -> p i n", i=4)
    kT = big[:, 1024:1536]
    for t in range(2):
        zq = z[:, t, 0:640].rearrange("p (h d) -> p h d", d=64)
        zc = z[:, t, 1280:1408].rearrange("p (h d) -> p h d", d=64)
        r = st[:, 32 + 12 * t:42 + 12 * t].unsqueeze(2).broadcast_to([P, 10, 64])
        rc = st[:, 42 + 12 * t:44 + 12 * t].unsqueeze(2).broadcast_to([P, 2, 64])
        ve.do(TT(zq, zq, r, ALU.mult), t_row)
        ve.do(TT(z[:, t, 0:640], z[:, t, 0:640], R("qkg"), ALU.mult))
        ve.do(TT(zc, zc, rc, ALU.mult))
        ve.do(TT(z[:, t, 1280:1408], z[:, t, 1280:1408], R("qkg", 512, 128), ALU.mult))
        cosv, sinv = C("ropc")[:, 64 * t:64 * t + 64], C("rops")[:, 64 * t:64 * t + 64]
        z5 = z[:, t, 0:640].rearrange("p (h a b j) -> p h a b j", a=2, b=2, j=16)
        s5 = s2[:, 0:640].rearrange("p (h a b j) -> p h a b j", a=2, b=2, j=16)
        v4 = sinv.rearrange("p (a b j) -> p a b j", a=2, b=2)
        ve.do([TT(s1[:, 0:640].rearrange("p (h d) -> p h d", d=64), zq, bc(cosv, 10), ALU.mult)]
              + [TT(s5[:, :, a, q, :], z5[:, :, a, 1 - q, :], bc(v4[:, a, q, :], 10), ALU.mult)
                 for a in range(2) for q in range(2)])
        t_q = ve.do(TT(z[:, t, 0:640], s1[:, 0:640], s2[:, 0:640], ALU.add))
    s1_free[:], s2_free[:] = [], []
    for rest in first:
        rest()
    tq = []
    for i in (5, 4, 0, 1, 2, 3):
        b = take("B")
        c0 = 128 * i if i < 5 else 1280
        tp = pe.do([tr(ps[:, b, 128 * t:128 * t + 128], z[:, t, c0:c0 + 128]) for t in range(2)],
                   t_q, bank_free[b])
        dst = qT[:, i, :] if i < 4 else (kT[:, 256:512] if i == 4 else kT[:, 0:256])
        t_ = ac.do(AC(dst, ps[:, b, 0:256]), tp, t_hl)
        bank_free[b] = [t_]
        tq.append(t_)
    pT = big[:, 1536:5632].rearrange("p (u k n) -> p u k n", u=4, k=4)
    pbuf = big[:, 5632:7680].rearrange("p (u n) -> p u n", u=4)
    pT_free, pb_free = [None] * 4, [None] * 4
    yf = ar[:, 4096:6144].rearrange("p (k n) -> p k n", k=8)
    ty = {}

    def y_parts(k, t):
        ty[k // 2] = split_cols(yf[:, k:k + 2, :], [q[:, k:k + 2, :] for q in Y3], t, t_hl)

    vno = [0]

    def head(i, s):
        lo = 64 * s
        u = (2 * i + s) % 4
        for t in range(2):
            v = vno[0] % 4
            vno[0] += 1
            b = take("A")
            tp = pe.do([mm(ps[:, b, :], qT[lo:lo + 64, i, 128 * t:128 * t + 128], kT[lo:lo + 64, :], True, True)],
                       tq, bank_free[b])
            m, sm = st[:, 80 + v:81 + v], st[:, 84 + v:85 + v]
            ve.do(RED(m, ps[:, b, :], ALU.max), tp, pb_free[v])
            tv = ve.do(TS(m, m, -0.125, None, ALU.mult))
            ta = ac.do(AC(pbuf[:, v, :], ps[:, b, :], ACT.Exp, bias=m, scale=0.125, accum_out=sm), tv, pb_free[v])
            bank_free[b] = [ta]
            yield
            ve.do(RCP(sm), ta)
            tv = ve.do(TS(pbuf[:, v, :], pbuf[:, v, :], sm, None, ALU.mult))
            b = take("B")
            tp = pe.do([tr(ps[:, b, 128 * k:128 * k + 128], pbuf[:, v, 128 * k:128 * k + 128]) for k in range(4)],
                       tv, bank_free[b])
            pb_free[v] = tp
            t_p = ac.do(AC(pT[:, u, :, 128 * t:128 * t + 128], ps[:, b, :].rearrange("p (k n) -> p k n", k=4)), tp,
                        pT_free[u])
            bank_free[b] = [t_p]
            yield
        b = take("B")
        fns = []
        for k in range(4):
            vv = z[:, k % 2, 1408 + lo:1472 + lo] if k < 2 else z[:, k % 2, 640 + lo:704 + lo]
            fns.append(mm(ps[lo:lo + 64, b, 0:256], vv, pT[:, u, k, :], k == 0, k == 3))
        tp = pe.do(fns, t_p, bank_free[b])
        pT_free[u] = tp
        t_ = ve.do(CP(yf[lo:lo + 64, i, :], ps[lo:lo + 64, b, 0:256]), tp, t_hl)
        bank_free[b] = [t_]
        if i % 2 and s:
            y_parts(i - 1, t_)

    def pooling():
        w = load(t_in["pm"], split=False)
        pm = w.raw.rearrange("p (k g n) -> p k g n", k=2, g=4)
        ta = []
        for g in range(0, 4, 2):
            b = take("B")
            tp = pe.do([mm(ps[:, b, 256 * i:256 * i + 256], z[:, k, 768 + 128 * (g + i):896 + 128 * (g + i)],
                           pm[:, k, g + i, :], k == 0, k == 1) for i in range(2) for k in range(2)],
                       w.landed, tz, bank_free[b])
            used(w, tp)
            ta.append(ac.do(AC(s1[:, 256 * g:256 * g + 512], ps[:, b, :]), tp, t_q))
            bank_free[b] = [ta[-1]]
        yield
        for g in range(4):
            b = take("B")
            tp = pe.do([mm(ps[:, b, 0:256], K("plw", 128 * g, 128), s1[:, 256 * g:256 * g + 256], True, True)],
                       ta[g // 2], t_col, bank_free[b])
            tv = ve.do(TS(yf[:, 4 + g, :], ps[:, b, 0:256], K("ps", g, 1), None, ALU.mult), tp, t_hl)
            bank_free[b] = [tv]
            if g % 2:
                y_parts(3 + g, tv)
            yield
        s1_free[:] = [tp]

    def conditions():
        rests = []
        xn_free[:] = list(r2_free)
        for piece in (8, 9):
            rests.append(adaln_sum(0, piece, "po"))
            yield
        for _ in range(16):
            yield
        for rest in rests:
            rest()
            yield

    for piece in (6, 7):
        adaln_pe(0, piece)()

    def later():
        if next(cond, "end") == "end" and not ended:
            ended.append(1)
            barrier()
            ahead(1)

    cond, ended = conditions(), []
    weave([pooling(), *[head(i, s) for i in range(4) for s in range(2)]], 4, later)
    assert ended
    hl_free[0] = hl_free[1] = [("pe", pe.n)]
    hl_free[2] = [t_hl]
    tx, tp = out_proj(t_in["we_out"], Y3, ty, (0, 0), lo="po")
    t_gf = tx[-1:]

    cT_free = []

    def router(l, t_h):
        L = rt[:, 0:40].rearrange("p (t n) -> p t n", t=2)
        b = take("B")
        rw = K("rw", 160 * l, 160).rearrange("p (k n) -> p k n", k=8)
        fns = []
        for t in range(2):
            fns += [mm(ps[:, b, 20 * t:20 * t + 20], hT[:, k, 128 * t:128 * t + 128], rw[:, k, :],
                       k == 0, k == 7) for k in range(8)]
        tp = pe.do(fns, t_h, t_col, bank_free[b])
        tv = ve.do(TT(L, ps[:, b, 0:40].rearrange("p (t n) -> p t n", t=2), bc(R("rb", 20 * l, 20), 2),
                      ALU.add), tp, t_row)
        bank_free[b] = [tv]
        G, E_ = L[:, :, 0:4], L[:, :, 4:20]
        gm, gs = rt[:, 40:42], rt[:, 42:44]
        m1, m2, d = rt[:, 44:46], rt[:, 46:48], rt[:, 48:50]
        w1, w2 = rt[:, 50:52], rt[:, 52:54]
        v3 = lambda a, n: rt[:, a:a + n].rearrange("p (t n) -> p t n", t=2)
        ge, gk, gc, em, k1, k2, cu, comb, pen = (v3(56, 8), v3(64, 8), v3(72, 8), v3(80, 32), v3(112, 32),
                                                 v3(144, 32), v3(176, 32), v3(208, 32), v3(240, 8))
        b3 = lambda a, n: a.unsqueeze(2).broadcast_to([P, 2, n])

        def first_only(k, c):
            ve.do([lambda e, t=t: e.tensor_tensor_scan(c[:, t, :], k[:, t, :], k[:, t, :], 0.0,
                                                       ALU.add, ALU.bypass) for t in range(2)])
            ve.do(STT(k, c, 1.0, k, ALU.is_equal, ALU.mult))

        ve.do(RED(gm, G, ALU.max))
        tv = ve.do(TT(ge, G, b3(gm, 4), ALU.subtract))
        ac.do(AC(ge, ge, ACT.Exp), tv)
        ve.do(TT(gk, G, b3(gm, 4), ALU.is_equal))
        first_only(gk, gc)
        ve.do(TS(pen, gk, 1.0, 1e30, ALU.subtract, ALU.mult))
        ve.do([TT(em[:, t, :].rearrange("p (g n) -> p g n", n=4), E_[:, t, :].rearrange("p (g n) -> p g n", n=4),
                  pen[:, t, :].unsqueeze(2).broadcast_to([P, 4, 4]), ALU.add) for t in range(2)])
        ve.do(RED(m1, em, ALU.max))
        ve.do(TT(k1, em, b3(m1, 16), ALU.is_equal))
        first_only(k1, cu)
        ve.do(STT(em, k1, -3e30, em, ALU.mult, ALU.add))
        ve.do(RED(m2, em, ALU.max))
        ve.do(TT(k2, em, b3(m2, 16), ALU.is_equal))
        first_only(k2, cu)
        tv = ve.do(TT(d, m2, m1, ALU.subtract))
        ta = ac.do(AC(d, d, ACT.Exp), tv)
        ve.do(RED(gs, ge, ALU.add), ta)
        ve.do(STT(w1, d, 1.0, gs, ALU.add, ALU.mult))
        ve.do(RCP(w1))
        ve.do(TT(w2, w1, d, ALU.mult))
        ve.do([TT(comb, k1, b3(w1, 16), ALU.mult), TT(k2, k2, b3(w2, 16), ALU.mult)])
        tv = ve.do(TT(comb, comb, k2, ALU.add))

        def to_rows():
            b = take("B")
            tp = pe.do([tr(ps[0:16, b, 128 * t:128 * t + 128], comb[:, t, :]) for t in range(2)], tv, bank_free[b])
            t_ = ve.do(CP(tab16[:, :], ps[0:16, b, 0:256]), tp, cT_free[:])
            bank_free[b] = [t_]
            return t_
        return to_rows

    hidh, hidl, ex = S["hidh"], S["hidl"], S["ex"][:, :].rearrange("p (u n) -> p u n", u=4)

    def experts(l, t_h, extra):
        ex_free, hid_free, tps = [None, None], [None, None], [None, None]
        done = {}
        rests = []
        for e_ in range(18):
            if e_ < 16:
                u = e_ % 2
                banks = [take("B"), take("B")]
                for s in range(2):
                    w = load(t_in["wgu"][l, e_, :, 2048 * s:2048 * s + 2048], lo="po" if e_ == 0 else "ve")
                    wh, wl = kn(w.hi, 8), kn(w.lo, 8)
                    for f in range(2):
                        for k in range(8):
                            tp = pe.do(mm3(ps[:, banks[f], 256 * s:256 * s + 256],
                                           [q[:, k, 128 * f:128 * f + 128] for q in (wh, wl)],
                                           [q[:, k, :] for q in H3], k == 0, k == 7),
                                       w.ready, pair(t_h, k), bank_free[banks[f]] if s == 0 else None)
                        if s == 1:
                            b = banks[f]
                            v = ex[:, 2 * u + f, 0:256]
                            ta = ac.do(AC(v, ps[:, b, 0:256], ACT.Silu), tp, ex_free[u], hT_free[:])
                            tv = ve.do(TT(v, v, ps[:, b, 256:512], ALU.mult), ta)
                            bank_free[b] = [tv]
                    used(w, tp)
                    if e_ == s == 0:
                        to_rows = router(l, t_h)
            if 1 <= e_ < 17:
                q = e_ - 1
                u = q % 2
                if q == 0:
                    t_c = to_rows()
                b = take("B")
                tcw = pe.do([mm(ps[:, b, 0:256], C("ident")[0:16, q:q + 1].broadcast_to([16, P]),
                                tab16[:, :], True, True)], t_c, bank_free[b])
                hf = []
                for f in range(2):
                    v2 = ex[:, 2 * u + f, 256:512]
                    tv = ve.do(TT(v2, ex[:, 2 * u + f, 0:256], ps[:, b, 0:256], ALU.mult), tcw)
                    hf += split_cols(v2, (hidh[:, u, f, :], hidl[:, u, f, :]), tv, hid_free[u])
                bank_free[b] = [tv]
                ex_free[u] = tv
                done[q] = hf
            if e_ >= 2:
                q = e_ - 2
                w = load(t_in["wdn"][l, q // 2, :, 2048 * (q % 2):2048 * (q % 2) + 2048], lo="po")
                wh, wl = kn(w.hi, 2), kn(w.lo, 2)
                fns = []
                for h in range(2):
                    for t in range(2):
                        for f in range(2):
                            fns += mm3(ps[:, 2 * t + h, :],
                                       [a[:, q % 2, f, 128 * t:128 * t + 128] for a in (hidh, hidl)],
                                       [a[:, f, 512 * h:512 * h + 512] for a in (wh, wl)],
                                       q == 0 and f == 0, q == 15 and f == 1)
                    tp = pe.do(fns, w.ready, done[q], [bank_free[b] for b in range(4)] if q == 0 else None)
                    fns = []
                    tps[h] = tp
                used(w, tp)
                hid_free[q % 2] = tp
            if e_ in extra:
                if rests:
                    rests.pop(0)()
                rest = extra[e_]()
                if rest is not None:
                    rests.append(rest)
        for rest in rests:
            rest()
        hT_free[:] = [tp]
        cT_free[:] = [tp]
        res = []
        for h in range(2):
            for t in range(2):
                b = 2 * t + h
                ve.do(TT(s2[:, 0:512], ps[:, b, :], grow[:, 1, 512 * h:512 * h + 512], ALU.mult), tps[h],
                      t_grow[(l, 1, h)], s2_free[:])
                xs = x[:, t, 512 * h:512 * h + 512]
                tt = ve.do(TT(xs, xs, s2[:, 0:512], ALU.add))
                bank_free[b] = [tt]
                res.append(tt)
        s2_free[:] = [tt]
        return res

    t_sc = cond_scale(0, 1, K("n2a", 0, 8), cadj[:, 3, :])
    th = norm_T(x, norm_diag(x, tx, s1, 0, s1_free[:]), cadj[:, 3, :], mcol[:, 16:24], t_sc, hT, H3, hT_free[:])
    gate_bias(1, 0, t_gf)
    acc_limit[0] = 4
    extra = {e_: (lambda e_=e_: adaln_sum(1, e_ - 2)) for e_ in range(2, 12)}
    for piece in (10, 11):
        extra[piece + 2] = lambda piece=piece: adaln_sum(0, piece)
    kept = []
    for piece in (10, 11):
        extra[piece + 4] = lambda piece=piece: kept.append(adaln_sum(1, piece))
    tx = experts(0, th, extra)
    gate_bias(1, 1, tx[-1:])

    t_sc = cond_scale(1, 0, K("n1a", 8, 8), cadj[:, 3, :])
    th = norm_T(x, norm_diag(x, tx, s1, 0, s1_free[:]), cadj[:, 3, :], mcol[:, 32:40], t_sc, hT, H3, hT_free[:])
    v_ = xn[:, :, :].rearrange("p t n -> p (t n)")[:, 0:1024].rearrange("p (t n) -> p t n", t=2)
    for t, (b, tp) in enumerate(rows_of(t_in["wo_v"], 512, [(H3, th, 0), (H3, th, 1)], lo="po")):
        tv = ve.do(CP(v_[:, t, :], ps[:, b, :]), tp, xn_free[:])
        bank_free[b] = [tv]
        ve.do(TT(s1[:, 512 * t:512 * t + 512], v_[:, t, :], v_[:, t, :], ALU.mult), s1_free[:])
        tv = ve.do(RED(st[:, 8 + 4 * t:12 + 4 * t], s1[:, 512 * t:512 * t + 512].rearrange("p (g c) -> p g c", g=4),
                       ALU.add))
    tv = rstd(st[:, 16:24], st[:, 8:16], 1.0 / 128, st[:, 24:32], tv)
    for t in range(2):
        zg = v_[:, t, :].rearrange("p (g c) -> p g c", g=4)
        ve.do(TT(zg, zg, st[:, 16 + 4 * t:20 + 4 * t].unsqueeze(2).broadcast_to([P, 4, 128]), ALU.mult))
        t_v = ve.do(TT(v_[:, t, :], v_[:, t, :], R("sgg"), ALU.mult), t_row)
    uT = zf[:, 0:1024].rearrange("p (g n) -> p g n", g=4)
    hxT = zf[:, 1024:2048].rearrange("p (g n) -> p g n", g=4)
    bgT = zf[:, 2048:3072].rearrange("p (g n) -> p g n", g=4)
    zTf = zf[:, 3072:3072 + 4 * 258]
    zT = zTf.rearrange("p (g n) -> p g n", g=4)
    t_pad = ve.do(lambda e: e.memset(zTf, 0.0), hT_free[:])
    yt = {}
    for name, dst in (("wo_u", uT), ("wo_hx", hxT), ("wo_bg", bgT)):
        for j in range(2):
            b, tp = cols_of(t_in[name][j], H3, th, lo="po" if name == "wo_u" else "ve")
            ta = ac.do(AC(dst[:, 2 * j:2 * j + 2, :], two(ps[:, b, :])), tp, hT_free[:])
            bank_free[b] = [ta]
        if name == "wo_u":
            for rest in kept:
                rest()
            t_u = ta
        if name == "wo_hx":
            for g in range(4):
                b = take("B")
                tp = pe.do([mm(ps[:, b, 128 * t:128 * t + 128], v_[:, t, 128 * g:128 * g + 128],
                               K("sgw", 128 * g, 128), True, True) for t in range(2)], t_v, t_col, bank_free[b])
                s_ = s2[:, 256 * g:256 * g + 256]
                tv = ve.do(TT(s_.rearrange("p (t n) -> p t n", t=2), ps[:, b, 0:256].rearrange("p (t n) -> p t n", t=2),
                              bc(R("sgb", 128 * g, 128), 2), ALU.add), tp)
                bank_free[b] = [tv]
                tv = ve.do(TT(uT[:, g, :], s_, uT[:, g, :], ALU.mult), t_u)
                if g % 2:
                    yt[g // 2] = split_cols(uT[:, g - 1:g + 1, :], [q[:, g - 1:g + 1, :] for q in Y3], tv)
            xn_free[:] = [tp]
    for j in range(2):
        b, tp = cols_of(t_in["wo_cg"][j], H3, th)
        tv = ve.do(TT(zT[:, 2 * j:2 * j + 2, 1:257], two(ps[:, b, :]), hxT[:, 2 * j:2 * j + 2, :], ALU.mult), tp, ta)
        bank_free[b] = [tv]
        gs = (2 * j, 2 * j + 1)
        ve.do([TS(hxT[:, g, :], zT[:, g, 0:256], K("cw", g, 1), None, ALU.mult) for g in gs])
        for c in (1, 2):
            ve.do([STT(hxT[:, g, :], zT[:, g, c:c + 256], K("cw", 4 * c + g, 1), hxT[:, g, :], ALU.mult, ALU.add)
                   for g in gs])
        y = hxT[:, 2 * j:2 * j + 2, :]
        tv = ve.do(TT(y, y, bgT[:, 2 * j:2 * j + 2, :], ALU.mult))
        yt[2 + j] = split_cols(y, [q[:, 4 + 2 * j:6 + 2 * j, :] for q in Y3], tv)
    hT_free[:] = [tp]
    tx, tp = out_proj(t_in["wo_out"], Y3, yt, (1, 0), lo="po")
    t_sc = cond_scale(1, 1, K("n2a", 8, 8), cadj[:, 3, :])
    th = norm_T(x, norm_diag(x, tx, s1, 0, s1_free[:]), cadj[:, 3, :], mcol[:, 48:56], t_sc, hT, H3, hT_free[:])
    T = [K("plw", 56 * i, 56) for i in range(6)]
    t3 = lambda a: a.rearrange("p (t n) -> p t n", t=2)
    posf = st[:, 90:92]
    ve.do(CP(posf, posi[:, :]), t_pos)
    ve.do(TT(t3(T[0]), posf.unsqueeze(2).broadcast_to([P, 2, 28]), bc(C("inv"), 2), ALU.mult), t_cst)
    ve.do(TS(T[1], T[0], 1.0 / TWO_PI, None, ALU.mult))
    ve.do(TS(T[1], T[1], 12582912.0, None, ALU.add))
    ve.do(TS(T[1], T[1], 12582912.0, None, ALU.subtract))
    for part in (6.28125, 1.9350051879882812e-03, 3.0199159819567e-07):
        ve.do(STT(T[0], T[1], -part, T[0], ALU.mult, ALU.add))
    PI = 3.1415925
    ve.do(TS(T[2], T[0], 1.5707963267948966, None, ALU.add))
    ve.do(TS(T[3], T[2], PI, -TWO_PI, ALU.is_gt, ALU.mult))
    ve.do(TT(T[2], T[2], T[3], ALU.add))
    ve.do(TS(T[0], T[0], PI, -PI, ALU.min, ALU.max))
    tv = ve.do(TS(T[2], T[2], PI, -PI, ALU.min, ALU.max))
    ac.do(AC(T[4], T[2], ACT.Sin), tv)
    t_tab = ac.do(AC(T[5], T[0], ACT.Sin))
    cos, sin = t3(T[4]), t3(T[5])

    tx = experts(1, th, {})

    sgT = big[:, 0:8192].rearrange("p (g n) -> p g n", g=32)
    off = [0]

    def area(n):
        a = off[0]
        off[0] += n
        return ar[:, a:a + n]

    nq = area(512).rearrange("p (i n) -> p i n", i=2)
    dq = area(512).rearrange("p (i n) -> p i n", i=2)
    kk = area(768).rearrange("p (i n) -> p i n", i=3)
    mq = area(1024).rearrange("p (h n) -> p h n", h=4)
    mk = area(1024).rearrange("p (h n) -> p h n", h=4)
    off[0] = 4096
    pbs = [area(1024), area(1024)]
    gr = grow[:, :, :].rearrange("p a n -> p (a n)")
    pTs = [area(1536), gr[:, 0:1536]]
    pTs = [(p[:, 0:1024].rearrange("p (h n) -> p h n", h=4), p[:, 1024:1536].rearrange("p (h n) -> p h n", h=4))
           for p in pTs]
    cmpb = area(400)
    cmb = acc[:, :, :].rearrange("p a n -> p (a n)")
    oTs = S["oTs"][:, :].rearrange("p (n i m) -> p n i m", n=4, i=2)
    mzb = xn[:, :, :].rearrange("p t n -> p (t n)")
    mixf = mzb.rearrange("p (k n) -> p k n", k=8)
    dmask = K("sgw").rearrange("p (t n) -> p t n", t=2)
    rp = rt
    z_free, big_free, oTs_free = [tx[-1]], [], []

    def rope(view, half, c0, *after):
        n = view.shape[2]
        m = n * half
        a, b = [[rp[:, m * (2 * i + t):m * (2 * i + t) + m].rearrange("p (h j) -> p h j", h=n) for t in range(2)]
                for i in range(2)]
        c = [bc(cos[:, t, c0:c0 + half], n) for t in range(2)]
        s = [bc(sin[:, t, c0:c0 + half], n) for t in range(2)]
        x1, x2 = view[:, :, :, 0:half], view[:, :, :, half:2 * half]
        ve.do([TT(a[t], x1[:, t], s[t], ALU.mult) for t in range(2)]
              + [TT(b[t], x2[:, t], s[t], ALU.mult) for t in range(2)], t_tab, *after)
        ve.do([TT(x1[:, t], x1[:, t], c[t], ALU.mult) for t in range(2)]
              + [TT(x2[:, t], x2[:, t], c[t], ALU.mult) for t in range(2)])
        return ve.do([TT(x1[:, t], x1[:, t], b[t], ALU.subtract) for t in range(2)]
                     + [TT(x2[:, t], x2[:, t], a[t], ALU.add) for t in range(2)])

    def layer2(l, tx):
        th = norm_T(x, norm_diag(x, tx, s1, 0, s1_free[:]), K("n1b", 8 * l, 8), None, t_col, hT, H3, hT_free[:])
        zo = [0]
        for wd in ZW:
            zo.append(zo[-1] + wd)
        tz = []
        for i, wd in enumerate(ZW):
            r = rows_of(t_in["wz"][l, :, 8 * zo[i]:8 * zo[i] + 8 * wd], wd, [(H3, th, 0), (H3, th, 1)],
                        lo="po" if i % 2 else "ve")
            for t, (b, tp) in enumerate(r):
                o, i_ = z[:, t, zo[i]:zo[i] + wd], ps[:, b, 0:wd]
                tt = ac.do(AC(o, i_), tp, z_free[:]) if t else ve.do(CP(o, i_), tp, z_free[:])
                bank_free[b] = [tt]
                tz.append(tt)
        tz = [tz[2 * i:2 * i + 2] for i in range(6)]
        barrier()
        t_hl = tp
        gates = []

        def gate_tiles():
            for d in range(8):
                for n in range(4):
                    if n % 2 == 0:
                        w = load(t_in["wgt"][l, d, n // 2], split=False)
                        wv = kn(w.raw, 8)
                    b = take("B")
                    tp = pe.do([mm(ps[:, b, 0:256], wv[:, k, 128 * (n % 2):128 * (n % 2) + 128], hT[:, k, :],
                                   k == 0, k == 7) for k in range(8)], w.landed, bank_free[b])
                    used(w, tp)
                    ta = ac.do(AC(sgv[:, n, d, :], ps[:, b, 0:256], ACT.Tanh, scale=0.5), tp, t_hl, big_free[:])
                    bank_free[b] = [ta]
                    gates.append(ta)
                    yield

        sgv = big[:, 0:8192].rearrange("p (n d m) -> p n d m", n=4, d=8)

        lifts, tsum = [], {}

        def lift():
            for i in range(4):
                while not lifts:
                    yield
                n = lifts.pop(0)
                w = load(t_in["wbr"][l, n], split=False)
                wv = w.raw.rearrange("p (k d) -> p k d", k=2)
                if i == 3:
                    assert n in (2, 3) and len(to) == 4
                    hl_free[2] = [("pe", pe.n)]
                    hl_free[0] = [("po", po.n), ("ve", ve.n)]
                    barrier()
                    ahead(2)
                for d in range(0, 8, 2):
                    b = take("B")
                    tp = pe.do([mm(ps[:, b, 256 * j:256 * j + 256], wv[:, k, 128 * (d + j):128 * (d + j) + 128],
                                   oTs[:, n, k, :], k == 0, k == 1) for j in range(2) for k in range(2)],
                               w.landed, to[n], bank_free[b])
                    used(w, tp)
                    g2 = sgv[:, n, d:d + 2, :]
                    t = ve.do(STT(g2, g2, 1.0, two(ps[:, b, :]), ALU.add, ALU.mult), tp, gates)
                    bank_free[b] = [t]
                    if i == 0:
                        tsum[d] = (g2, t)
                    elif i < 3:
                        tsum[d] = (g2, po.do(TT(g2, g2, tsum[d][0], ALU.add), t, tsum[d][1]))
                    else:
                        mx = mixf[:, d:d + 2, :]
                        t = ve.do(TT(mx, g2, tsum[d][0], ALU.add), tsum[d][1], to[0], xn_free[:])
                        ts[d // 2] = split_cols(mx, [q[:, d:d + 2, :] for q in H3], t, ("pe", pe.n))
                    yield

        ts = {}

        def fillers():
            yield from gate_tiles()
            yield from lift()

        gen = fillers()

        def fill():
            next(gen, None)

        Z = lambda t, a, n: z[:, t, a:a + n]
        zr = z[:, :, 312:1080].rearrange("p t (h d) -> p t h d", d=64)
        zi = z[:, :, 0:288].rearrange("p t (h d) -> p t h d", d=32)
        SM = 288
        RQ, VV, ML, FQ, FV = 312, 1080, 1336, 1752, 2264
        tok = {}
        HB = lambda ap, h: ap[64 * (h % 2):64 * (h % 2) + 64]
        causal = lambda t, n: C("mask")[:, 256 - n:256]
        to = {}

        def indexer():
            t_i = rope(zi[:, :, :, 0:8], 4, 24, tz[0])
            b = take("B")
            tp = pe.do([tr(ps[:, b, 256 * i + 128 * t:256 * i + 128 * t + 128], Z(t, 128 * i, 128))
                        for i in range(2) for t in range(2)], t_i, bank_free[b])
            ta1 = ac.do(AC(mq[:, 0:2, :], ps[:, b, :].rearrange("p (i n) -> p i n", i=2)), tp, t_hl)
            bank_free[b] = [ta1]
            b = take("B")
            kd = s2[:, 0:256].rearrange("p (t n) -> p t n", t=2)
            td = ve.do([CP(kd[:, t, :].rearrange("p (r d) -> p r d", r=4), bc(Z(t, 256, 32), 4)) for t in range(2)],
                       s2_free[:])
            tp = pe.do([tr(ps[:, b, 128 * t:128 * t + 128], kd[:, t, :]) for t in range(2)], td, bank_free[b])
            kiT = mq[:, 2, :]
            ta2 = ac.do(AC(kiT, ps[:, b, 0:256]), tp)
            bank_free[b] = [ta2]
            wi = lf[:, 0:16].rearrange("p (t h) -> p t h", t=2)
            ve.do(TS(wi, z[:, :, SM + 16:SM + 24], 8 ** -0.5, None, ALU.mult))
            rfree = [[tp]] * 4
            yield
            for t in (1, 0):
                nk = 128 * (t + 1)
                sc = s1[:, 256 * t:256 * t + nk]
                for j2 in range(2):
                    b = take2()
                    toks = []
                    for j in range(2):
                        p0 = 32 * (2 * j2 + j)
                        toks.append(pe.do([mm(ps[:, b + j, 256 * i:256 * i + nk],
                                              mq[p0:p0 + 32, i, 128 * t:128 * t + 128], kiT[p0:p0 + 32, 0:nk],
                                              True, True) for i in range(2)], ta1, ta2, bank_free[b + j]))
                    for j in range(2):
                        for i in range(2):
                            h = 4 * i + 2 * j2 + j
                            r = s2[:, 256 * (h % 4):256 * (h % 4) + nk]
                            ta = ac.do(AC(r, ps[:, b + j, 256 * i:256 * i + nk], ACT.Relu, scale=32 ** -0.5),
                                       toks[j], rfree[h % 4])
                            wcol = wi[:, t, h:h + 1]
                            if j == i == j2 == 0:
                                tv = ve.do(TS(sc, r, wcol, None, ALU.mult), ta, s1_free[:])
                            else:
                                tv = ve.do(STT(sc, r, wcol, sc, ALU.mult, ALU.add), ta)
                            rfree[h % 4] = [tv]
                        bank_free[b + j] = [ta]
                    yield
                mk_ = C("mask")[:, 256 - nk:256]
                ve.do(TT(sc, sc, mk_, ALU.add))
                wk = s1[:, 512 + 256 * t:512 + 256 * t + nk]
                m8 = lf[:, 16:24]
                src = sc
                for r8 in range(8):
                    ve.do(lambda e, src=src: e.max(m8, src))
                    ve.do(lambda e, src=src, wk=wk: e.match_replace(wk, m8, src, -3e38))
                    src = wk
                    if r8 in (2, 5):
                        yield
                ve.do(TS(wk, wk, -2e38, NEG, ALU.is_gt, ALU.mult))
                tok["sel"] = ve.do(TT(dmask[:, t, 0:nk], wk, mk_, ALU.min), tok.get("dmfree"))
                yield
            s1_free[:] = []
            s2_free[:] = [tok["sel"]]

        def heads():
            tok["r"] = t_h = rope(zr[:, :, :, 0:16], 8, 16, tz[1], tz[2])
            for dst, c0 in ((nq[:, 0], 0), (nq[:, 1], 128), (dq[:, 0], 448), (dq[:, 1], 576)):
                b = take("B")
                tp = pe.do([tr(ps[:, b, 128 * t:128 * t + 128], Z(t, RQ + c0, 128)) for t in range(2)], t_h,
                           bank_free[b])
                ta = ac.do(AC(dst, ps[:, b, 0:256]), tp, t_hl)
                bank_free[b] = [ta]
            for i, c0 in enumerate((320, 384, 704)):
                b = take("B")
                k2 = mzb[:, 256 * i:256 * i + 256].rearrange("p (t n) -> p t n", t=2)
                td = po.do([CP(k2[:, t, :].rearrange("p (r d) -> p r d", r=2), bc(Z(t, RQ + c0, 64), 2))
                            for t in range(2)], t_h, xn_free[:])
                tp = pe.do([tr(ps[:, b, 128 * t:128 * t + 128], k2[:, t, :]) for t in range(2)], td, bank_free[b])
                tok["kk"] = ac.do(AC(kk[:, i], ps[:, b, 0:256]), tp, t_hl)
                bank_free[b] = [tok["kk"]]
            xn_free[:] = [tp]
            yield

        def compress():
            t_h = tok["r"]
            w2 = [load(t_in["wcmp"][l, :, 2048 * s:2048 * s + 2048], parts=64, split=False) for s in range(2)]
            b = take("B")
            tp = pe.do([tr(ps[0:64, b, 256 * s + 128 * t:256 * s + 128 * t + 128], Z(t, c0, 64))
                        for s, c0 in ((0, RQ + 256), (1, VV)) for t in range(2)], t_h, tz[2], bank_free[b])
            kcT = mzb[0:64, 1024:1536]
            t_ = ac.do(AC(kcT, ps[0:64, b, :]), tp, xn_free[:])
            bank_free[b] = [t_]
            G = pbs[1][0:64, 0:1024].rearrange("p (s m c) -> p s m c", s=2, m=32)
            fns = []
            for s in range(2):
                src = kcT[:, 256 * s:256 * s + 256]
                fns.append(CP(G[:, s, :, 15], K("pe", 64 * l + 32 * s, 32)[0:64, :]))
                for hh in range(2):
                    fns.append(CP(G[:, s, 16 * hh:16 * hh + 16, 0:15],
                                  src[:, 16 * hh:16 * hh + 240].rearrange("p (w m) -> p m w", m=16)))
            tv = po.do(fns, t_, pb_user[1], t_hl, t_col)
            yield
            kvc = cmpb[0:64, 0:32].rearrange("p (s c) -> p s c", s=2)
            b = take("B")
            for s in range(2):
                wcv = w2[s].raw.rearrange("p (m d) -> p m d", m=32)
                tp = pe.do([mm(ps[0:64, b, 16 * s:16 * s + 16], wcv[:, m, :], G[:, s, m, :], m == 0, m == 31)
                            for m in range(32)], tv, w2[s].landed, bank_free[b] if s == 0 else None)
                used(w2[s], tp)
            pb_user[1] = tp
            pc = ps[0:64, b, 0:32].rearrange("p (s c) -> p s c", s=2)
            kv_ = cmpb[0:64, 32:34]
            ve.do(CP(kv_, pc[:, :, 15]), tp, t_hl)
            tv = ve.do([TS(kvc[:, s, 0:15], pc[:, s, 0:15], kv_[:, s:s + 1], None, ALU.add) for s in range(2)])
            bank_free[b] = [tv]
            yield
            kct, vct, kr = cmpb[:, 40:56], cmpb[0:15, 64:128], cmpb[0:15, 128:256]
            b = take("B")
            tp = pe.do([tr(ps[0:15, b, 0:64], kvc[:, 0, 0:15], 64), tr(ps[0:15, b, 64:128], kvc[:, 1, 0:15], 64)],
                       tv, bank_free[b])
            t_vc = ve.do([CP(kr[:, 0:64], ps[0:15, b, 0:64]), CP(kr[:, 64:128], ps[0:15, b, 0:64]),
                          CP(vct, ps[0:15, b, 64:128])], tp)
            bank_free[b] = [t_vc]
            sg = lf[:, 24:48].rearrange("p (t n) -> p t n", t=2)
            ta = ac.do(AC(sg, z[:, :, SM:SM + 12], ACT.Exp, scale=-1.0), tz[0])
            ve.do(TS(sg, sg, 1.0, None, ALU.add), ta)
            tok["sg"] = ve.do(RCP(sg))
            yield
            b = take("B")
            tp = pe.do([tr(ps[:, b, 0:15], kr, 15)], t_vc, bank_free[b])
            t_kc = ve.do(CP(kct[:, 0:15], ps[:, b, 0:15]), tp)
            bank_free[b] = [t_kc]
            yield
            b = take2()
            pcp = cmpb[:, 256:376].rearrange("p (t h c) -> p t h c", t=2, h=4)
            tp = pe.do([mm(ps[:, b + h % 2, 32 * t + 16 * (h // 2):32 * t + 16 * (h // 2) + 15],
                           HB(nq, h)[:, h // 2, 128 * t:128 * t + 128], HB(kct, h)[:, 0:15], True, True)
                        for t in range(2) for h in range(4)], t_kc, tok["kk"], bank_free[b], bank_free[b + 1])
            ca, cm = C("cadd"), C("cmul")
            fns = []
            for t in range(2):
                for e2 in range(2):
                    i_ = ps[:, b + e2, 32 * t:32 * t + 32].rearrange("p (i c) -> p i c", i=2)[:, :, 0:15]
                    o = pcp[:, t].rearrange("p (i e) c -> p i e c", e=2)[:, :, e2, :]
                    fns.append(TT(o, i_, bc(ca[:, 15 * t:15 * t + 15], 2), ALU.add))
            tm = ve.do(fns, tp)
            bank_free[b] = bank_free[b + 1] = [tm]
            m, sm = st[:, 100:108], st[:, 108:116]
            p3 = pcp.rearrange("p t h c -> p (t h) c")
            mu = [bc(cm[:, 15 * t:15 * t + 15], 4) for t in range(2)]
            ve.do(RED(m, p3, ALU.max))
            tv = ve.do(TT(p3, p3, m.unsqueeze(2).broadcast_to([P, 8, 15]), ALU.subtract))
            ta = ac.do(AC(p3, p3, ACT.Exp, scale=0.125), tv)
            ve.do([TT(pcp[:, t], pcp[:, t], mu[t], ALU.mult) for t in range(2)], ta)
            ve.do(RED(sm, p3, ALU.add))
            ve.do(TS(sm, sm, 1e-30, None, ALU.max))
            ve.do(RCP(sm))
            ve.do(TT(sm.rearrange("p (t h) -> p t h", t=2), sm.rearrange("p (t h) -> p t h", t=2), sg[:, :, 0:4],
                     ALU.mult))
            tv = ve.do(TT(p3, p3, sm.unsqueeze(2).broadcast_to([P, 8, 15]), ALU.mult))
            yield
            pcT = cmb[0:15, :].rearrange("p (h n) -> p h n", h=4)
            for t in range(2):
                bb = take("B")
                tp = pe.do([tr(ps[0:15, bb, 128 * h:128 * h + 128], pcp[:, t, h, :]) for h in range(4)], tv,
                           bank_free[bb])
                tok["cmp"] = ac.do(AC(pcT[:, :, 128 * t:128 * t + 128],
                                      ps[0:15, bb, :].rearrange("p (h n) -> p h n", h=4)), tp, oTs_free[:])
                bank_free[bb] = [tok["cmp"]]
            tok["pcT"], tok["vct"] = pcT, vct

        def attend(name, q, k, scale, mask, gate, toks, slot, then=None):
            pT = pTs[slot]
            for t in range(2):
                n = 128 * (t + 1)
                v = slot
                pb = pbs[v]
                m, sm = st[:, 116 + 8 * v:120 + 8 * v], st[:, 120 + 8 * v:124 + 8 * v]
                b = take2()
                tp = pe.do([mm(ps[:, b + h % 2, n * (h // 2):n * (h // 2) + n], q(h, t), k(h, n), True, True)
                            for h in range(4)], toks(), bank_free[b], bank_free[b + 1])
                tm = ve.do([ADDMAX(pb[:, n * h:n * h + n], ps[:, b + h % 2, n * (h // 2):n * (h // 2) + n],
                                   mask(t, n), m[:, h:h + 1]) for h in range(4)], tp, pb_user[v], t_hl)
                bank_free[b] = bank_free[b + 1] = [tm]
                tv = ve.do(TS(m, m, -scale, None, ALU.mult))
                ta = ac.do([AC(pb[:, n * h:n * h + n], pb[:, n * h:n * h + n], ACT.Exp, bias=m[:, h:h + 1],
                               scale=scale, accum_out=sm[:, h:h + 1]) for h in range(4)], tv)
                yield
                tv = ve.do(RCP(sm), ta)
                if gate is not None:
                    tv = ve.do(TT(sm, sm, gate[:, t, :], ALU.mult), tok["sg"])
                pap = pb[:, 0:4 * n].rearrange("p (h n) -> p h n", h=4)
                tv = ve.do(TT(pap, pap, sm.unsqueeze(2).broadcast_to([P, 4, n]), ALU.mult), tv)
                yield
                for kt in range(t + 1):
                    bb = take("B")
                    tp = pe.do([tr(ps[:, bb, 128 * h:128 * h + 128], pap[:, h, 128 * kt:128 * kt + 128])
                                for h in range(4)], tv, bank_free[bb])
                    dst = pT[0][:, :, 128 * t:128 * t + 128] if kt == 0 else pT[1]
                    ta = ac.do(AC(dst, ps[:, bb, :].rearrange("p (h n) -> p h n", h=4)), tp, pT_user[slot], t_hl)
                    bank_free[bb] = [ta]
                pb_user[v] = tp
                yield
            tok[name] = ta
            if then is not None:
                then()

        def values(n, paths, toks, slots):
            b = take("B")
            fns = []
            for h in range(4):
                lo = 64 * (h % 2)
                c0 = 256 * (h // 2)
                ops = paths(h)
                for i, (l_, r_, q0) in enumerate(ops):
                    fns.append(mm(ps[lo:lo + 64, b, c0 + q0:c0 + 256], l_, r_, i == 0, i == len(ops) - 1))
            tp = pe.do(fns, toks, bank_free[b])
            for s in slots:
                pT_user[s] = tp
            t_ = ve.do(TS(oTs[:, n], ps[:, b, :].rearrange("p (i m) -> p i m", i=2), 0.5, None, ALU.mult), tp,
                       oTs_free[:], t_hl)
            bank_free[b] = [t_]
            to[n] = t_
            lifts.append(n)

        def pv(a, h, slot):
            return [(Z(0, a(h), 64), pTs[slot][0][:, h, :], 0), (Z(1, a(h), 64), pTs[slot][1][:, h, :], 128)]

        def mla_in():
            wm = load(t_in["wmla"][l], split=False)
            for t in range(2):
                ve.do(TT(s2[:, 0:384], Z(t, ML, 384), Z(t, ML, 384), ALU.mult), tz[3], s2_free[:])
                tv = ve.do([RED(st[:, 8 + 2 * t:9 + 2 * t], s2[:, 0:256], ALU.add),
                            RED(st[:, 9 + 2 * t:10 + 2 * t], s2[:, 256:384], ALU.add)])
            tv = ve.do([TS(st[:, 9 + 2 * t:10 + 2 * t], st[:, 9 + 2 * t:10 + 2 * t], 2.0, None, ALU.mult)
                        for t in range(2)])
            tv = rstd(st[:, 12:16], st[:, 8:12], 1.0 / 256, st[:, 16:20], tv)
            tv = ve.do([f for t in range(2) for f in (
                TS(Z(t, ML, 256), Z(t, ML, 256), st[:, 12 + 2 * t:13 + 2 * t], None, ALU.mult),
                TS(Z(t, ML + 256, 128), Z(t, ML + 256, 128), st[:, 13 + 2 * t:14 + 2 * t], None, ALU.mult))])
            tkr = rope(z[:, :, ML + 384:ML + 416].unsqueeze(2), 16, 0)
            yield
            cT_ = s2[:, 0:768].rearrange("p (i n) -> p i n", i=3)
            for i in range(3):
                b = take("B")
                tp = pe.do([tr(ps[:, b, 128 * t:128 * t + 128], Z(t, ML + 128 * i, 128)) for t in range(2)], tv,
                           bank_free[b])
                g = K("gq", 2 * l + i, 1) if i < 2 else K("gkv", l, 1)
                t_ = ac.do(AC(cT_[:, i, :], ps[:, b, 0:256], scale=g), tp, tv)
                bank_free[b] = [t_]
            yield
            mz = mzb.rearrange("p (t n) -> p t n", t=2)
            for t in range(2):
                b = take("B")
                tp = pe.do([mm(ps[:, b, 0:384], cT_[:, k, 128 * t:128 * t + 128], wm.raw[:, 384 * k:384 * k + 384],
                               k == 0, k == 1) for k in range(2)], t_, wm.landed, bank_free[b])
                tq_ = ac.do(AC(mz[:, t, 0:384], ps[:, b, 0:384]), tp, tok["cmp"], tok["kk"], xn_free[:])
                bank_free[b] = [tq_]
                b = take("B")
                tp = pe.do([mm(ps[:, b, :], cT_[:, 2, 128 * t:128 * t + 128], wm.raw[:, 768:1280], True, True)],
                           bank_free[b])
                used(wm, tp)
                pv_ = ps[:, b, :].rearrange("p (h n) -> p h n", h=4)
                k4 = mz[:, t, 384:768].rearrange("p (h n) -> p h n", h=4)
                tv = ve.do([CP(k4[:, :, 0:64], pv_[:, :, 0:64]),
                            CP(mz[:, t, 768:1024].rearrange("p (h n) -> p h n", h=4), pv_[:, :, 64:128]),
                            CP(k4[:, :, 64:96], bc(Z(t, ML + 384, 32), 4))], tp, tok["cmp"], tok["kk"], xn_free[:])
                bank_free[b] = [tv]
            s2_free[:] = [tp]
            mqv = mz[:, :, 0:384].rearrange("p t (h n) -> p t h n", h=4)
            tv = rope(mqv[:, :, :, 64:96], 16, 0, tq_)
            yield
            for dst, c0 in ((mq, 0), (mk, 384)):
                for hp in range(2):
                    b = take("B")
                    tp = pe.do([tr(ps[0:96, b, 256 * i + 128 * t:256 * i + 128 * t + 128],
                                   mz[:, t, c0 + 96 * (2 * hp + i):c0 + 96 * (2 * hp + i) + 96])
                                for i in range(2) for t in range(2)], tv, bank_free[b])
                    tok["mk"] = ac.do(AC(dst[0:96, 2 * hp:2 * hp + 2, :],
                                         ps[0:96, b, :].rearrange("p (i n) -> p i n", i=2)), tp, tok["sel"], t_hl)
                    bank_free[b] = [tok["mk"]]

        def mla():
            mz = mzb.rearrange("p (t n) -> p t n", t=2)
            done = lambda: values(0, lambda h: [(mz[:, 0, 768 + 64 * h:832 + 64 * h], pTs[0][0][:, h, :], 0),
                                                (mz[:, 1, 768 + 64 * h:832 + 64 * h], pTs[0][1][:, h, :], 128)],
                                  tok["mla"], [0])
            yield from attend("mla", lambda h, t: mq[0:96, h, 128 * t:128 * t + 128], lambda h, n: mk[0:96, h, 0:n],
                              96 ** -0.5, causal, None, lambda: tok["mk"], 0, done)

        def fox():
            f = lf[:, 48:56].rearrange("p (t n) -> p t n", t=2)
            g_ = lf[:, 56:64].rearrange("p (t n) -> p t n", t=2)
            ve.do(TT(f, z[:, :, SM + 12:SM + 16], bc(R("fb", 4 * l, 4), 2), ALU.add), t_row)
            tv = ve.do(STT(g_, f, -1.0, f, ALU.mult, ALU.min))
            ac.do(AC(g_, g_, ACT.Exp), tv)
            ta = ac.do(AC(g_, g_, ACT.Ln, bias=1.0))
            tv = ve.do(STT(f, f, 0.0, g_, ALU.min, ALU.subtract), ta)
            yield
            b = take("B")
            tp = pe.do([mm(ps[:, b, 0:4], C("tri"), f[:, 0, :], True, True),
                        mm(ps[:, b, 8:12], C("ones"), f[:, 0, :], True, False),
                        mm(ps[:, b, 8:12], C("tri"), f[:, 1, :], False, True)], tv, bank_free[b])
            fz = foxb.rearrange("p (s h n) -> p s h n", s=2, h=4)
            tc = ve.do(CP(lf[:, 0:8].rearrange("p (t h) -> p t h", t=2),
                          ps[:, b, 0:16].rearrange("p (t h) -> p t h", t=2)[:, :, 0:4]), tp, tok["sel"])
            bank_free[b] = [tc]
            fzf = None
            for t in range(2):
                zq = Z(t, FQ, 256).rearrange("p (h n) -> p h n", h=4)
                zk = Z(t, FQ + 256, 256).rearrange("p (h n) -> p h n", h=4)
                cc = lf[:, 4 * t:4 * t + 4]
                tv = ve.do([TS(fz[:, 0, :, 0:64], zq, 0.125, None, ALU.mult),
                            CP(fz[:, 1, :, 0:64], zk),
                            CP(fz[:, 0, :, 64], cc),
                            TS(fz[:, 1, :, 65], cc, -1.0, None, ALU.mult),
                            lambda e: e.memset(fz[:, 0, :, 65:66], 1.0),
                            lambda e: e.memset(fz[:, 1, :, 64:65], 1.0)], fzf, tok["sel"], tz[4])
                b2 = [take("B"), take("B")]
                for s in range(2):
                    tp = pe.do([tr(ps[0:66, b2[s], 128 * h:128 * h + 128], fz[:, s, h, :]) for h in range(4)], tv,
                               bank_free[b2[s]])
                    tok["fk"] = ac.do(AC((fq, fk)[s][0:66, :, 128 * t:128 * t + 128],
                                         ps[0:66, b2[s], :].rearrange("p (h n) -> p h n", h=4)), tp, t_hl)
                    bank_free[b2[s]] = [tok["fk"]]
                fzf = tp
                yield
            s1_free[:] = [tp]
            done = lambda: values(2, lambda h: pv(lambda h: FV + 64 * h, h, 1), [tok["fox"], tz[5]], [1])
            yield from attend("fox", lambda h, t: fq[0:66, h, 128 * t:128 * t + 128], lambda h, n: fk[0:66, h, 0:n],
                              1.0, causal, None, lambda: tok["fk"], 1, done)

        fq, fk = [S["ff"][:, 1024 * i:1024 * i + 1024].rearrange("p (h n) -> p h n", h=4) for i in range(2)]
        foxb = s1[:, 0:528]
        sgl = lf[:, 24:48].rearrange("p (t n) -> p t n", t=2)
        nsa_q = lambda h, t: HB(nq, h)[:, h // 2, 128 * t:128 * t + 128]
        dsa_q = lambda h, t: HB(dq, h)[:, h // 2, 128 * t:128 * t + 128]
        kkh = lambda i: (lambda h, n: HB(kk, h)[:, i, 0:n])

        def dsa():
            done = lambda: values(3, lambda h: pv(lambda h: VV + 192, h, 0), tok["dsa"], [0])
            yield from attend("dsa", dsa_q, kkh(2), 0.125, lambda t, n: dmask[:, t, 0:n], None,
                              lambda: [tok["kk"], tok["sel"]], 0, done)

        def nsa_sel():
            yield from attend("nsel", nsa_q, kkh(0), 0.125, causal, sgl[:, :, 4:8], lambda: tok["kk"], 0)

        def nsa_win():
            done = lambda: values(1, lambda h: [(tok["vct"], tok["pcT"][:, h, :], 0)]
                                  + pv(lambda h: VV + 64, h, 0) + pv(lambda h: VV + 128, h, 1),
                                  [tok["cmp"], tok["nsel"], tok["nwin"]], [0, 1])
            yield from attend("nwin", nsa_q, kkh(1), 0.125, causal, sgl[:, :, 8:12], lambda: tok["kk"], 1, done)

        pb_user, pT_user = [None, None], [None, None]
        for _ in heads():
            fill()
        weave([indexer(), compress()], 2, fill)
        weave([nsa_sel(), nsa_win(), mla_in()], 3, fill)
        weave([chain(mla(), dsa()), fox()], 2, fill)
        for _ in gen:
            pass
        pe_all = ("pe", pe.n)
        oTs_free[:] = [pe_all]
        hl_free[1] = [pe_all, ("ve", ve.n), ("po", po.n)]
        xn_free[:] = [ts]
        z_free[:] = [pe_all]
        tx, tp = out_proj(t_in["wout"][l], H3, ts, None, lo="po")
        hT_free[:] = [tp, ("pe", pe.n)]
        fTh, fTl = S["fTh"], S["fTl"]
        th = norm_T(x, norm_diag(x, tx, s1, 0, s1_free[:]), K("n2b", 8 * l, 8), None, t_col, hT, H3, hT_free[:])
        f_free = [z_free[:], z_free[:]]
        tf, tps = {}, [None, None]
        for c in range(9):
            if c < 8:
                tf[c] = []
                for j in range(2):
                    b, tp = cols_of(t_in["wup"][l, 2 * c + j], H3, th, lo="po" if c == 0 else "ve")
                    r = s2[:, 512 * j:512 * j + 512]
                    ta = ac.do(AC(r, ps[:, b, :], ACT.Relu), tp, s2_free[:], rf[j])
                    bank_free[b] = [ta]
                    r2 = s1[:, 512 * j:512 * j + 512]
                    tv = po.do(TT(r2, r, r, ALU.mult), ta, s1_free[:], rf1[j])
                    rf[j] = tv
                    ss = split_cols(two(r2), [q[:, c % 2, 2 * j:2 * j + 2, :] for q in (fTh, fTl)], tv, f_free[c % 2])
                    rf1[j] = ss
                    tf[c] += ss
            if c >= 1:
                q = c - 1
                for j in range(2):
                    w = load(t_in["wdown"][l, q, :, 2048 * j:2048 * j + 2048], lo="po")
                    wh, wl = kn(w.hi, 2), kn(w.lo, 2)
                    for h in range(2):
                        fns = []
                        for t in range(2):
                            for k in range(2):
                                fns += mm3(ps[:, 2 * t + h, :],
                                           [a[:, q % 2, 2 * j + k, 128 * t:128 * t + 128] for a in (fTh, fTl)],
                                           [a[:, k, 512 * h:512 * h + 512] for a in (wh, wl)],
                                           q == 0 and j == 0 and k == 0, q == 7 and j == 1 and k == 1)
                        tp = tps[h] = pe.do(fns, w.ready, tf[q],
                                            [bank_free[b] for b in range(4)] if q == 0 and j == 0 else None)
                    used(w, tp)
                f_free[q % 2] = tp
        hT_free[:] = [tp]
        z_free[:] = [tp]
        s1_free[:] = list(rf1[0]) + list(rf1[1])
        s2_free[:] = [rf[0], rf[1]]
        res = []
        for h in range(2):
            for t in range(2):
                xs = x[:, t, 512 * h:512 * h + 512]
                tt = ve.do(TT(xs, xs, ps[:, 2 * t + h, :], ALU.add), tps[h])
                bank_free[2 * t + h] = [tt]
                res.append(tt)
        return res, pT_user

    rf, rf1 = [None, None], [[], []]
    tx, _ = layer2(0, tx)
    tx, pt = layer2(1, tx)
    t_fg = small(grow[:, 0, :], t_in["rowp"][0:1, 1712:2736].broadcast_to([P, 1024]), *pt)
    r, t_r = norm_stats(x, tx, s1, 0, s1_free[:])
    for t in range(2):
        tv = ve.do(STT(xn[:, t, :], x[:, t, :], r[:, t:t + 1], grow[:, 0, :], ALU.mult, ALU.mult), t_r, t_fg, xn_free[:])
        sp.dma(lambda e, t=t: e.dma_start(out[:, t, :], xn[:, t, :]), "out", 16 * (t + 1), tv)
    return noted, dict(pe=pe, ac=ac, ve=ve, po=po, sp=sp), ndma


def constants(np):
    f = np.float32
    c = np.zeros((P, NCST), f)

    def put(name, v):
        a, n = CST[name]
        c[:, a:a + n] = v

    i = np.arange(P)
    put("ident", np.eye(P))
    put("ones", 1.0)
    put("tri", i[:, None] <= i[None, :])
    put("mask", np.concatenate([np.zeros((P, P)), np.where(i[None, :] <= i[:, None], 0.0, NEG)], 1))
    tok = np.arange(256).reshape(2, P).T
    ok = (16 * np.arange(15) + 31)[None, None, :] <= tok[:, :, None]
    put("cadd", np.where(ok, 0.0, NEG).reshape(P, 30))
    put("cmul", ok.reshape(P, 30))
    inv = (f(10000.0) ** (-np.arange(0, 32, 2, dtype=f) / f(32))).astype(f)
    ra = (tok // 64).astype(f)[:, :, None] * inv
    ca = (tok % 64).astype(f)[:, :, None] * inv
    put("ropc", np.cos(np.concatenate([ra, ra, ca, ca], 2)).reshape(P, 128))
    put("rops", np.concatenate([-np.sin(ra), np.sin(ra), -np.sin(ca), np.sin(ca)], 2).reshape(P, 128))
    put("inv", np.concatenate([(f(500000.0) ** (-np.arange(0, r, 2, dtype=f) / f(r))).astype(f)
                               for r in (32, 16, 8)]))
    pm = np.zeros((256, 4, 256), f)
    for g, w in enumerate((2, 4, 8, 16)):
        for t in range(256):
            lo, hi = max(t - w // 2, 0), min(t + w - w // 2, 256)
            pm[lo:hi, g, t] = f(1.0) / f(hi - lo)
            pm[t, g, t] -= f(1.0)
    return c, pm.reshape(2, P, 4, 256).transpose(1, 0, 2, 3).reshape(P, 2048)


def layout(np, i):
    def rows(w, n):
        k, m = w.shape[-2] // P, w.shape[-1] // n
        lead = w.shape[:-2]
        w = w.reshape(*lead, k, P, m, n)
        r = len(lead)
        return np.ascontiguousarray(np.transpose(w, (*range(r), r + 2, r + 1, r, r + 3)).reshape(*lead, m, P, k * n))

    def cols(v):
        return v.reshape(-1, P).T

    a = {k: np.asarray(v) for k, v in i.items()}
    d = {}
    c, pm = constants(np)
    d["cst"], d["pm"] = c, pm
    colp = np.zeros((P, NCOL), np.float32)

    def put(name, v):
        b, n = COL[name]
        colp[:v.shape[0], b:b + n] = v

    put("n1a", cols(a["norm1_g"]))
    put("n2a", cols(a["norm2_g"]))
    put("n1b", cols(a["norm1_g_2"]))
    put("n2b", cols(a["norm2_g_2"]))
    put("modb", cols(a["mod_b"]))
    put("c", cols(a["c"]))
    put("cc", cols(a["c_ctx"]))
    put("ps", cols(a["pool_scale"]))
    put("cw", cols(a["conv_w"]))
    put("sgw", a["sg_w"][0].transpose(2, 0, 1).reshape(P, 512))
    put("plw", a["pool_w"][0].transpose(1, 0, 2).reshape(P, 512))
    r = np.concatenate([a["router_g_w"], a["router_e_w"]], 2)
    put("rw", r.reshape(2, 8, P, 20).transpose(2, 0, 1, 3).reshape(P, 320))
    put("gq", cols(a["mla_q_norm_g_2"]))
    put("gkv", cols(a["mla_kv_norm_g_2"]))
    put("pe", a["nsa_cmp_pe_2"].transpose(3, 0, 1, 2).reshape(64, 128))
    d["colp"] = colp
    kg = a["k_gain"].reshape(-1)
    qg = a["q_gain"].reshape(-1)
    gb = a["mod_b"].reshape(2, 6, 1024)[:, [2, 5], :].reshape(-1)
    rb = np.concatenate([a["router_g_b"], a["router_e_b"]], 1).reshape(-1)
    d["rowp"] = np.concatenate([np.tile(qg, 8), np.tile(kg, 2), a["sg_gain"].reshape(-1), a["sg_b"].reshape(-1),
                                rb, a["fox_f_bias_2"].reshape(-1), a["final_g_2"], gb]).reshape(1, NROW)
    d["x"] = np.ascontiguousarray(a["x"].reshape(2, P, 1024).transpose(1, 0, 2))
    d["ctx"] = np.ascontiguousarray(a["ctx"].reshape(2, P, 1024).transpose(1, 0, 2))
    d["pos"] = np.ascontiguousarray(a["positions_2"].reshape(2, P).T)
    d["wmod"] = rows(a["mod_w"], 512)
    w = a["even_w_in"][0]
    q = w[:, 0:512].reshape(1024, 2, 4, 64).transpose(0, 2, 1, 3).reshape(1024, 512)
    d["we_q"] = rows(q, 512)[0]
    d["we_kv"] = rows(w[:, 512:768], 256)[0]
    d["we_p"] = rows(w[:, 768:1280], 512)[0]
    w = a["even_w_out"][0]
    w = np.concatenate([w[0:512].reshape(2, 4, 64, 1024).transpose(1, 0, 2, 3).reshape(512, 1024), w[512:]], 0)
    d["we_out"] = rows(w, 512)
    w = a["odd_w_in"][0]
    d["wo_v"] = rows(w[:, 512:1024], 512)[0]
    for name, c0 in (("u", 0), ("hx", 1024), ("bg", 1536), ("cg", 2048)):
        d["wo_" + name] = rows(w[:, c0:c0 + 512], 256)
    d["wo_out"] = rows(a["odd_w_out"][0], 512)
    gu = np.stack([a["w_gate"], a["w_up"]], 2)
    d["wgu"] = np.ascontiguousarray(gu.reshape(2, 16, 2, 8, P, 256).transpose(0, 1, 4, 2, 3, 5)).reshape(2, 16, P, 4096)
    d["wdn"] = np.ascontiguousarray(a["w_down"].reshape(2, 8, 2, 2, P, 1024).transpose(0, 1, 4, 2, 3, 5)
                                    ).reshape(2, 8, P, 4096)
    w = a["w_in_2"]
    m, n, f, s = 0, 416, 1068, 1840
    order = [(s + 384, 288), (n + 640, 12), (f + 768, 4), (s + 672, 8),
             (n, 256), (n + 256, 64), (n + 384, 64), (n + 512, 64), (s, 256), (s + 256, 64),
             (n + 320, 64), (n + 448, 64), (n + 576, 64), (s + 320, 64),
             (m, 416), (f, 512), (f + 512, 256)]
    zw = np.concatenate([w[:, :, b:b + k] for b, k in order], 2)
    parts, b = [], 0
    for k in ZW:
        parts.append(zw[:, :, b:b + k].reshape(2, 8, P, k).transpose(0, 2, 1, 3).reshape(2, P, 8 * k))
        b += k
    d["wz"] = np.concatenate(parts, 2)
    g = w[:, :, 2520:].reshape(2, 8, P, 2, 2, 8, P)
    d["wgt"] = np.ascontiguousarray(g.transpose(0, 5, 3, 2, 1, 4, 6)).reshape(2, 8, 2, P, 2048)
    d["wmla"] = np.concatenate([a["mla_w_uq_2"].reshape(2, 2, P, 384).transpose(0, 2, 1, 3).reshape(2, P, 768),
                                a["mla_w_ukv_2"]], 2)
    d["wcmp"] = np.ascontiguousarray(a["nsa_cmp_w_2"].reshape(2, 2, 32, 64, 64).transpose(0, 3, 1, 2, 4)
                                     ).reshape(2, 64, 4096)
    d["wbr"] = np.ascontiguousarray(a["w_branch_2"].reshape(2, 4, 2, P, 1024).transpose(0, 1, 3, 2, 4)
                                    ).reshape(2, 4, P, 2048)
    d["wout"] = rows(a["w_out_2"], 512)
    d["wup"] = rows(a["w_up_2"], 256)
    d["wdown"] = np.ascontiguousarray(a["w_down_2"].reshape(2, 8, 4, P, 1024).transpose(0, 1, 3, 2, 4)
                                      ).reshape(2, 8, P, 4096)
    return d


def kernel(**inputs):
    import numpy as np
    from concourse import bacc
    from concourse.bass_utils import run_bass_kernel_spmd

    arrays = layout(np, inputs)
    nc = bacc.Bacc("TRN2", target_bir_lowering=False, num_devices=1)
    t_in = {k: nc.dram_tensor(f"in_{k}", v.shape, mybir.dt.from_np(v.dtype), kind="ExternalInput").ap()
            for k, v in arrays.items()}
    out = nc.dram_tensor("out_x", (P, 2, 1024), F32, kind="ExternalOutput").ap()
    build(nc, t_in, out)
    r = run_bass_kernel_spmd(nc, [{f"in_{k}": v for k, v in arrays.items()}], core_ids=[0])
    y = r.results[0]["out_x"]
    return y.transpose(1, 0, 2).reshape(1, 256, 1024)
```
